# Optimizing a Trainium2 kernel written in Bass

```python
import math
import jax
import jax.numpy as jnp
from jax import lax
import numpy as np

D_MODEL = 1024
BATCH = 1
SEQ = 128
DEPTH = 4
DEC_BATCH = 1
DEC_SEQ = 256
PAST_LEN = 128

GRID_W = 64
N_MIXERS = 3
N_GMLP_LAYERS = (DEPTH + 2) // 3
N_SSD_LAYERS = (DEPTH + 1) // 3
N_HGRN_LAYERS = DEPTH // 3

ALPHA = (2.0 * DEPTH) ** 0.25
BETA = (8.0 * DEPTH) ** -0.25
LN_EPS = 1e-5

GMLP_CHUNK = 128
GMLP_WIDTH = 2 * D_MODEL
GMLP_GROUPS = 8
GMLP_GROUP_DIM = GMLP_WIDTH // GMLP_GROUPS

SSD_INNER = 2 * D_MODEL
SSD_HEADDIM = 64
SSD_HEADS = SSD_INNER // SSD_HEADDIM
SSD_GROUPS = 4
SSD_STATE = 128
SSD_CONV = 3
SSD_CHUNK = 128
SSD_CONV_DIM = SSD_INNER + 2 * SSD_GROUPS * SSD_STATE
SSD_IN_DIM = SSD_INNER + SSD_CONV_DIM + 2 * SSD_HEADS

HGRN_HEADS = 8
HGRN_KDIM = 128
HGRN_VDIM = D_MODEL // HGRN_HEADS
HGRN_KW = HGRN_HEADS * HGRN_KDIM
HGRN_VW = HGRN_HEADS * HGRN_VDIM
HGRN_CHUNK = 64
HGRN_IN_DIM = 3 * HGRN_KW + 2 * HGRN_VW

N_EXPERTS = 16
N_EXPERT_GROUPS = 4
EXPERTS_PER_GROUP = N_EXPERTS // N_EXPERT_GROUPS
TOP_K = 2
D_EXPERT = 256

kernel_name = 'hybrid_gmlp_ssd_hgrn2_moe_diffusion_step'

def layer_norm(x, g, b):
    xf = x.astype(jnp.float32)
    mu = jnp.mean(xf, -1, keepdims=True)
    var = jnp.mean(jnp.square(xf - mu), -1, keepdims=True)
    return ((xf - mu) * lax.rsqrt(var + LN_EPS) * g + b).astype(x.dtype)

def rms_norm(x, g):
    xf = x.astype(jnp.float32)
    return (xf * lax.rsqrt(jnp.mean(xf * xf, -1, keepdims=True) + LN_EPS) * g).astype(x.dtype)

def grid_pos_embed(rows, dtype):
    quarter = D_MODEL // 4
    freq = jnp.exp(-math.log(10000.0) / quarter * jnp.arange(quarter, dtype=jnp.float32))
    r = jnp.repeat(jnp.arange(rows, dtype=jnp.float32), GRID_W)
    col = jnp.tile(jnp.arange(GRID_W, dtype=jnp.float32), rows)
    ar = r[:, None] * freq[None, :]
    ac = col[:, None] * freq[None, :]
    return jnp.concatenate([jnp.sin(ar), jnp.cos(ar), jnp.sin(ac), jnp.cos(ac)], axis=-1).astype(dtype)

def modulation(cond, w_mod, b_mod):
    m = jax.nn.silu(cond) @ w_mod + b_mod
    return jnp.split(m[:, None, :], 6, axis=-1)

def dwconv_centred(x, w, b):
    pad = w.shape[0] // 2
    y = lax.conv_general_dilated(x, w[:, None, :], window_strides=(1,), padding=[(pad, pad)],
                                 dimension_numbers=('NWC', 'WIO', 'NWC'),
                                 feature_group_count=x.shape[-1])
    return y + b

def chunk_gmlp(h, w_in, ln_g, ln_b, w_s, b_s, w_out):
    bsz, L, _ = h.shape
    z = jax.nn.gelu(h @ w_in, approximate=False)
    u, v = jnp.split(z, 2, axis=-1)
    v = layer_norm(v, ln_g, ln_b)
    v = v.reshape(bsz, L // GMLP_CHUNK, GMLP_CHUNK, GMLP_GROUPS, GMLP_GROUP_DIM)
    mixed = jnp.einsum('hqp,bnphd->bnqhd', w_s, v) + b_s.T[None, None, :, :, None]
    return (u * mixed.reshape(bsz, L, GMLP_WIDTH)) @ w_out

def ssd_scan(x, dt, A, Bm, Cm, h0):
    f32 = jnp.float32
    b, L, H, P = x.shape
    G, N = Bm.shape[2], Bm.shape[3]
    R = H // G
    Q = SSD_CHUNK
    nc = L // Q
    xc = x.astype(f32).reshape(b, nc, Q, G, R, P)
    Bc = Bm.astype(f32).reshape(b, nc, Q, G, N)
    Cc = Cm.astype(f32).reshape(b, nc, Q, G, N)
    dtc = dt.reshape(b, nc, Q, G, R)
    acs = jnp.cumsum(dtc * A.reshape(G, R), axis=2)
    mask = jnp.tril(jnp.ones((Q, Q), bool))
    seg = acs[:, :, :, None] - acs[:, :, None]
    decay = jnp.exp(jnp.where(mask[:, :, None, None], seg, -jnp.inf))
    cb = jnp.einsum('bclgk,bcsgk->bclsg', Cc, Bc)
    w = cb[..., None] * decay * dtc[:, :, None]
    y_diag = jnp.einsum('bclsgr,bcsgrp->bclgrp', w, xc)
    decay_end = jnp.exp(acs[:, :, -1:] - acs)
    states = jnp.einsum('bcsgk,bcsgr,bcsgrp->bcgrpk', Bc, decay_end * dtc, xc)
    chunk_decay = jnp.exp(acs[:, :, -1])

    def step(hc, inp):
        st, dec = inp
        return hc * dec[..., None, None] + st, hc

    h_last, h_in = lax.scan(step, h0.astype(f32).reshape(b, G, R, P, N),
                            (jnp.moveaxis(states, 1, 0), jnp.moveaxis(chunk_decay, 1, 0)))
    h_in = jnp.moveaxis(h_in, 0, 1)
    y_off = jnp.einsum('bclgk,bcgrpk,bclgr->bclgrp', Cc, h_in, jnp.exp(acs))
    return (y_diag + y_off).reshape(b, L, H, P), h_last.reshape(b, H, P, N)

def ssd_mixer(h, h0_f, h0_b, w_in, conv_w, conv_b, dt_bias, a_log, d_skip, norm_g, w_out):
    f32 = jnp.float32
    bsz, L, _ = h.shape
    proj = h @ w_in
    z, xbc, dt_raw = jnp.split(proj, [SSD_INNER, SSD_INNER + SSD_CONV_DIM], axis=-1)
    xbc = jax.nn.silu(dwconv_centred(xbc, conv_w, conv_b))
    xs, Bm, Cm = jnp.split(xbc, [SSD_INNER, SSD_INNER + SSD_GROUPS * SSD_STATE], axis=-1)
    xs = xs.reshape(bsz, L, SSD_HEADS, SSD_HEADDIM)
    Bm = Bm.reshape(bsz, L, SSD_GROUPS, SSD_STATE)
    Cm = Cm.reshape(bsz, L, SSD_GROUPS, SSD_STATE)
    dt = jax.nn.softplus(dt_raw.astype(f32).reshape(bsz, L, 2, SSD_HEADS) + dt_bias.astype(f32))
    A = -jnp.exp(a_log.astype(f32))
    flip = lambda t: jnp.flip(t, axis=1)
    y_f, s_f = ssd_scan(xs, dt[:, :, 0], A[0], Bm, Cm, h0_f)
    y_b, s_b = ssd_scan(flip(xs), flip(dt[:, :, 1]), A[1], flip(Bm), flip(Cm), h0_b)
    y = y_f + flip(y_b) + xs.astype(f32) * d_skip.astype(f32)[:, None]
    y = y.reshape(bsz, L, SSD_INNER) * jax.nn.silu(z.astype(f32))
    y = rms_norm(y, norm_g).astype(h.dtype)
    return y @ w_out, s_f, s_b

def hgrn_lower_bounds(lb_logits):
    p = jax.nn.softmax(lb_logits.astype(jnp.float32), axis=0)
    return jnp.cumsum(p, axis=0) - p[0]

def hgrn2_scan(q, k, v, logf, s0):
    b, L, H, K = q.shape
    Q = HGRN_CHUNK
    nc = L // Q
    to_chunks = lambda t: jnp.moveaxis(t.reshape(b, nc, Q, H, t.shape[-1]), 1, 0)
    mask = jnp.tril(jnp.ones((Q, Q), bool))

    def step(S, inp):
        qc, kc, vc, gc = inp
        bcs = jnp.cumsum(gc, axis=1)
        o_inter = jnp.einsum('bthk,bhkv->bthv', qc * jnp.exp(bcs), S)
        diff = bcs[:, :, None] - bcs[:, None]
        dec = jnp.exp(jnp.where(mask[None, :, :, None, None], diff, -jnp.inf))
        att = jnp.einsum('bthk,btshk,bshk->bhts', qc, dec, kc)
        o_intra = jnp.einsum('bhts,bshv->bthv', att, vc)
        last = bcs[:, -1]
        S_new = S * jnp.exp(last)[..., None] + jnp.einsum(
            'bshk,bshv->bhkv', kc * jnp.exp(last[:, None] - bcs), vc)
        return S_new, o_inter + o_intra

    s_last, o = lax.scan(step, s0, (to_chunks(q), to_chunks(k), to_chunks(v), to_chunks(logf)))
    return jnp.moveaxis(o, 0, 1).reshape(b, L, H, v.shape[-1]), s_last

def hgrn2_mixer(h, s0_f, s0_b, lb, w_in, norm_g, w_out):
    f32 = jnp.float32
    bsz, L, _ = h.shape
    proj = h @ w_in
    q, f_f, f_b, i, g = jnp.split(
        proj, [HGRN_KW, 2 * HGRN_KW, 3 * HGRN_KW, 3 * HGRN_KW + HGRN_VW], axis=-1)
    heads_k = lambda t: t.astype(f32).reshape(bsz, L, HGRN_HEADS, HGRN_KDIM)
    q = heads_k(q)
    v = i.astype(f32).reshape(bsz, L, HGRN_HEADS, HGRN_VDIM)
    lb = lb.reshape(2, HGRN_HEADS, HGRN_KDIM)
    f_fw = lb[0] + (1.0 - lb[0]) * jax.nn.sigmoid(heads_k(f_f))
    f_bw = lb[1] + (1.0 - lb[1]) * jax.nn.sigmoid(heads_k(f_b))
    flip = lambda t: jnp.flip(t, axis=1)
    o_f, s_f = hgrn2_scan(q, 1.0 - f_fw, v, jnp.log(f_fw), s0_f.astype(f32))
    o_b, s_b = hgrn2_scan(flip(q), flip(1.0 - f_bw), flip(v), flip(jnp.log(f_bw)), s0_b.astype(f32))
    o = rms_norm(o_f + flip(o_b), norm_g)
    o = o * jax.nn.silu(g.astype(f32).reshape(bsz, L, HGRN_HEADS, HGRN_VDIM))
    return o.reshape(bsz, L, HGRN_VW).astype(h.dtype) @ w_out, s_f, s_b

def moe(h, w_router, b_router, w_gu, w_down):
    scores = jax.nn.sigmoid((h @ w_router).astype(jnp.float32))
    sel = scores + b_router.astype(jnp.float32)
    sel_g = sel.reshape(sel.shape[:-1] + (N_EXPERT_GROUPS, EXPERTS_PER_GROUP))
    group_score = lax.top_k(sel_g, TOP_K)[0].sum(-1)
    best = jnp.argmax(group_score, axis=-1)
    in_group = best[..., None] == jnp.arange(N_EXPERT_GROUPS)
    masked = jnp.where(in_group[..., None], sel_g, -jnp.inf).reshape(sel.shape)
    _, idx = lax.top_k(masked, TOP_K)
    gsel = jnp.take_along_axis(scores, idx, axis=-1)
    gsel = gsel / jnp.sum(gsel, -1, keepdims=True)
    combine = jnp.sum(jax.nn.one_hot(idx, N_EXPERTS, dtype=jnp.float32) * gsel[..., None], axis=-2)

    def per_seq(args):
        xs, cw = args
        gate, up = jnp.split(jnp.einsum('ld,edf->lef', xs, w_gu), 2, axis=-1)
        hid = jax.nn.silu(gate) * up * cw[..., None].astype(xs.dtype)
        return jnp.einsum('lef,efd->ld', hid, w_down)

    return lax.map(per_seq, (h, combine))

def run_trunk(x, cond, ssd_init, hgrn_init, w_mod, b_mod, ln_g, ln_b,
              gmlp_w_in, gmlp_ln_g, gmlp_ln_b, gmlp_w_s, gmlp_b_s, gmlp_w_out,
              ssd_w_in, ssd_conv_w, ssd_conv_b, ssd_dt_bias, ssd_a_log, ssd_d_skip,
              ssd_norm_g, ssd_w_out, hgrn_w_in, hgrn_lb_logits, hgrn_norm_g, hgrn_w_out,
              moe_w_router, moe_b_router, moe_w_gu, moe_w_down):
    lower_bounds = hgrn_lower_bounds(hgrn_lb_logits)
    ssd_states, hgrn_states = [], []
    ia = ib = ic = 0
    for li in range(DEPTH):
        sh1, sc1, g1, sh2, sc2, g2 = modulation(cond, w_mod[li], b_mod[li])
        h = x * (1 + sc1) + sh1
        kind = li % N_MIXERS
        if kind == 0:
            out = chunk_gmlp(h, gmlp_w_in[ia], gmlp_ln_g[ia], gmlp_ln_b[ia], gmlp_w_s[ia],
                             gmlp_b_s[ia], gmlp_w_out[ia])
            ia += 1
        elif kind == 1:
            out, s_f, s_b = ssd_mixer(h, ssd_init[:, ib, 0], ssd_init[:, ib, 1], ssd_w_in[ib],
                                      ssd_conv_w[ib], ssd_conv_b[ib], ssd_dt_bias[ib],
                                      ssd_a_log[ib], ssd_d_skip[ib], ssd_norm_g[ib], ssd_w_out[ib])
            ssd_states.append(jnp.stack([s_f, s_b], axis=1))
            ib += 1
        else:
            out, s_f, s_b = hgrn2_mixer(h, hgrn_init[:, ic, 0], hgrn_init[:, ic, 1], lower_bounds[li],
                                        hgrn_w_in[ic], hgrn_norm_g[ic], hgrn_w_out[ic])
            hgrn_states.append(jnp.stack([s_f, s_b], axis=1))
            ic += 1
        x = layer_norm(ALPHA * x + g1 * out, ln_g[li, 0], ln_b[li, 0])
        h = x * (1 + sc2) + sh2
        x = layer_norm(ALPHA * x + g2 * moe(h, moe_w_router, moe_b_router, moe_w_gu[li], moe_w_down[li]),
                       ln_g[li, 1], ln_b[li, 1])
    return x, jnp.stack(ssd_states, axis=1).astype(x.dtype), jnp.stack(hgrn_states, axis=1).astype(x.dtype)

def setup_inputs(seed: int = 0) -> dict:
    key = jax.random.key(seed)
    ks = iter(jax.random.split(key, 40))
    d = D_MODEL

    def nrm(shape, scale):
        return jax.random.normal(next(ks), shape, jnp.float32) * scale

    x_prompt = nrm((BATCH, SEQ, d), 1.0)
    x_sample = nrm((DEC_BATCH, DEC_SEQ, d), 1.0)
    state_ssd = nrm((DEC_BATCH, N_SSD_LAYERS, 2, SSD_HEADS, SSD_HEADDIM, SSD_STATE), 1.0)
    state_hgrn = nrm((DEC_BATCH, N_HGRN_LAYERS, 2, HGRN_HEADS, HGRN_KDIM, HGRN_VDIM), 1.0)
    c = nrm((DEC_BATCH, d), 1.0)
    c_ctx = nrm((d,), 1.0)
    w_mod = nrm((DEPTH, d, 6 * d), 0.5 * d ** -0.5)
    b_mod = nrm((DEPTH, 6 * d), 0.02)
    ln_g = 1.0 + nrm((DEPTH, 2, d), 0.02)
    ln_b = nrm((DEPTH, 2, d), 0.02)
    gmlp_w_in = nrm((N_GMLP_LAYERS, d, 2 * GMLP_WIDTH), d ** -0.5)
    gmlp_ln_g = 1.0 + nrm((N_GMLP_LAYERS, GMLP_WIDTH), 0.02)
    gmlp_ln_b = nrm((N_GMLP_LAYERS, GMLP_WIDTH), 0.02)
    gmlp_w_s = nrm((N_GMLP_LAYERS, GMLP_GROUPS, GMLP_CHUNK, GMLP_CHUNK), GMLP_CHUNK ** -0.5)
    gmlp_b_s = 1.0 + nrm((N_GMLP_LAYERS, GMLP_GROUPS, GMLP_CHUNK), 0.02)
    gmlp_w_out = nrm((N_GMLP_LAYERS, GMLP_WIDTH, d), BETA * GMLP_WIDTH ** -0.5)
    ssd_w_in = nrm((N_SSD_LAYERS, d, SSD_IN_DIM), d ** -0.5)
    ssd_conv_w = nrm((N_SSD_LAYERS, SSD_CONV, SSD_CONV_DIM), SSD_CONV ** -0.5)
    ssd_conv_b = nrm((N_SSD_LAYERS, SSD_CONV_DIM), 0.02)
    dt0 = jnp.exp(jax.random.uniform(next(ks), (N_SSD_LAYERS, 2, SSD_HEADS), jnp.float32,
                                     math.log(1e-3), math.log(1e-1)))
    ssd_dt_bias = dt0 + jnp.log(-jnp.expm1(-dt0))
    ssd_a_log = jnp.log(jax.random.uniform(next(ks), (N_SSD_LAYERS, 2, SSD_HEADS), jnp.float32, 1.0, 16.0))
    ssd_d_skip = 1.0 + nrm((N_SSD_LAYERS, SSD_HEADS), 0.1)
    ssd_norm_g = 1.0 + nrm((N_SSD_LAYERS, SSD_INNER), 0.02)
    ssd_w_out = nrm((N_SSD_LAYERS, SSD_INNER, d), BETA * SSD_INNER ** -0.5)
    hgrn_w_in = nrm((N_HGRN_LAYERS, d, HGRN_IN_DIM), d ** -0.5)
    hgrn_lb_logits = nrm((DEPTH, 2, HGRN_KW), 0.5)
    hgrn_norm_g = 1.0 + nrm((N_HGRN_LAYERS, HGRN_VDIM), 0.02)
    hgrn_w_out = nrm((N_HGRN_LAYERS, HGRN_VW, d), BETA * HGRN_VW ** -0.5)
    moe_w_router = nrm((d, N_EXPERTS), d ** -0.5)
    moe_b_router = nrm((N_EXPERTS,), 0.01)
    moe_w_gu = nrm((DEPTH, N_EXPERTS, d, 2 * D_EXPERT), d ** -0.5)
    moe_w_down = nrm((DEPTH, N_EXPERTS, D_EXPERT, d), BETA * D_EXPERT ** -0.5)
    return {'x_prompt': x_prompt, 'x_sample': x_sample, 'state_ssd': state_ssd,
            'state_hgrn': state_hgrn, 'c': c, 'c_ctx': c_ctx, 'w_mod': w_mod, 'b_mod': b_mod,
            'ln_g': ln_g, 'ln_b': ln_b, 'gmlp_w_in': gmlp_w_in, 'gmlp_ln_g': gmlp_ln_g,
            'gmlp_ln_b': gmlp_ln_b, 'gmlp_w_s': gmlp_w_s, 'gmlp_b_s': gmlp_b_s,
            'gmlp_w_out': gmlp_w_out, 'ssd_w_in': ssd_w_in, 'ssd_conv_w': ssd_conv_w,
            'ssd_conv_b': ssd_conv_b, 'ssd_dt_bias': ssd_dt_bias, 'ssd_a_log': ssd_a_log,
            'ssd_d_skip': ssd_d_skip, 'ssd_norm_g': ssd_norm_g, 'ssd_w_out': ssd_w_out,
            'hgrn_w_in': hgrn_w_in, 'hgrn_lb_logits': hgrn_lb_logits, 'hgrn_norm_g': hgrn_norm_g,
            'hgrn_w_out': hgrn_w_out, 'moe_w_router': moe_w_router, 'moe_b_router': moe_b_router,
            'moe_w_gu': moe_w_gu, 'moe_w_down': moe_w_down}

def reference(x_prompt, x_sample, state_ssd, state_hgrn, c, c_ctx, w_mod, b_mod, ln_g, ln_b,
              gmlp_w_in, gmlp_ln_g, gmlp_ln_b, gmlp_w_s, gmlp_b_s, gmlp_w_out,
              ssd_w_in, ssd_conv_w, ssd_conv_b, ssd_dt_bias, ssd_a_log, ssd_d_skip,
              ssd_norm_g, ssd_w_out, hgrn_w_in, hgrn_lb_logits, hgrn_norm_g, hgrn_w_out,
              moe_w_router, moe_b_router, moe_w_gu, moe_w_down):
    weights = (w_mod, b_mod, ln_g, ln_b, gmlp_w_in, gmlp_ln_g, gmlp_ln_b, gmlp_w_s, gmlp_b_s,
               gmlp_w_out, ssd_w_in, ssd_conv_w, ssd_conv_b, ssd_dt_bias, ssd_a_log, ssd_d_skip,
               ssd_norm_g, ssd_w_out, hgrn_w_in, hgrn_lb_logits, hgrn_norm_g, hgrn_w_out,
               moe_w_router, moe_b_router, moe_w_gu, moe_w_down)
    n_ctx = x_prompt.shape[0]
    cond_ctx = jnp.broadcast_to(c_ctx[None, :], (n_ctx, D_MODEL))
    zero_ssd = jnp.zeros((n_ctx, N_SSD_LAYERS, 2, SSD_HEADS, SSD_HEADDIM, SSD_STATE), jnp.float32)
    zero_hgrn = jnp.zeros((n_ctx, N_HGRN_LAYERS, 2, HGRN_HEADS, HGRN_KDIM, HGRN_VDIM), jnp.float32)
    y_prompt, new_state_ssd, new_state_hgrn = run_trunk(x_prompt, cond_ctx, zero_ssd, zero_hgrn, *weights)
    rows = x_sample.shape[1] // GRID_W
    x_lat = x_sample + grid_pos_embed(rows, x_sample.dtype)[None]
    y_sample, _, _ = run_trunk(x_lat, c, state_ssd, state_hgrn, *weights)
    return (y_prompt, y_sample, new_state_ssd, new_state_hgrn)


_drawn_inputs = setup_inputs


def setup_inputs(seed=0):
    import zlib

    import numpy as np

    out = dict(_drawn_inputs(seed))
    spreads = {}
    factors = {'state_hgrn': 8.0,
     'gmlp_ln_g': 28.819,
     'gmlp_ln_b': 26.412,
     'gmlp_b_s': 28.976,
     'ssd_d_skip': 8.0,
     'ssd_norm_g': 27.853,
     'hgrn_norm_g': 40.369,
     'moe_b_router': 3.504}
    for name, (base, spread) in spreads.items():
        noise = np.random.default_rng([zlib.crc32(name.encode()), seed]).standard_normal(out[name].shape)
        drawn = base * np.exp(spread * noise) if base else spread * noise
        out[name] = jnp.asarray(drawn.astype(out[name].dtype))
    for name, factor in factors.items():
        out[name] = (out[name] * factor).astype(out[name].dtype)
    return out
```

```python
import math
from contextlib import ExitStack, contextmanager

import concourse.bass as bass
import numpy as np
from concourse import mybir

F32 = mybir.dt.float32
F32R = mybir.dt.float32r
U32 = mybir.dt.uint32
ALU = mybir.AluOpType
ACT = mybir.ActivationFunctionType
AX = mybir.AxisListType

P = 128
D = 1024
KD = D // P
LC, LS = 128, 256
T = LC + LS
NT = T // P
DEPTH = 4
ALPHA = (2.0 * DEPTH) ** 0.25
EPS = 1e-5
SEGS = ((0, 0, LC), (1, LC, T))

GW = 2 * D
NE, NG, EG = 16, 4, 4
DE = 256
SH, SP_, SG_, SN = 32, 64, 4, 128
SI = SH * SP_
SSD_IN = 2 * SI + 2 * SG_ * SN + 2 * SH
HH = 8
LEVELS = 7
BIG = 1e30

SUB = 1024
RAW = 4
SPL = 4
MODC = 6 * D // 256
LN1_MODS, ROUTER_MODS, MOE_MODS, LN2_MODS = 2, 2, 16, 4
MOE_ITERS = 4

COLS = [("bmod", DEPTH * 48), ("lng", DEPTH * 16), ("lnb", DEPTH * 16), ("glng", 32), ("glnb", 32),
        ("convw", 72), ("convb", 24), ("dskip", 16), ("sng", 16), ("lbl", 64), ("hng", 1), ("cond", 16),
        ("dtb", 64), ("alog", 64), ("brout", 16), ("gkey", NG), ("ekey", NE)]
COL, _at = {}, 0
for _n, _w in COLS:
    COL[_n] = _at
    _at += _w
NCOL = _at

def moe_order(mods):
    return ([("G", 0), ("U", 0), ("G", 1), ("U", 1), ("D", 0), ("G", 2), ("U", 2), ("D", 1), ("G", 3),
             ("U", 3), ("D", 2)] + [("M", j) for j in range(mods)] + [("D", 3)])


def stream_plan():
    base, at, rows = {}, 0, []
    def part(name, n, k=KD):
        nonlocal at
        base[name] = at
        at += n
        rows.extend([k] * n)
    part("mod0", MODC)
    for l in range(DEPTH):
        kind = ("gmlp", "ssd", "hgrn")[l % 3]
        if kind == "gmlp":
            part((l, "v"), 8); part((l, "u"), 8); part((l, "out"), 8, 16)
        elif kind == "ssd":
            part((l, "dt"), 1); part((l, "xs"), 8); part((l, "bc"), 4); part((l, "z"), 8); part((l, "out"), 8, 16)
        else:
            part((l, "q"), 4); part((l, "f"), 8); part((l, "i"), 4); part((l, "g"), 4); part((l, "out"), 4)
        more = l + 1 < DEPTH
        part((l, "ln1"), LN1_MODS if more else 0)
        part((l, "router"), ROUTER_MODS if more else 0)
        order = moe_order(MOE_MODS // MOE_ITERS if more else 0)
        part((l, "moe"), MOE_ITERS * len(order))
        rows[base[(l, "moe")]:] = [2 if what == "D" else KD for what, _ in order] * MOE_ITERS
        part((l, "ln2"), LN2_MODS if more else 0)
    base["end"] = at
    return base, rows


class Chain:
    def __init__(self, eng, sem):
        self.eng, self.sem, self.n, self.shift = eng, sem, 0, 0

    def link(self, ins):
        self.n += 1
        ins.then_inc(self.sem, 1)
        self.eng.wait_ge(self.sem, self.shift + self.n)

    @contextmanager
    def loop(self, start, end, per):
        with self.eng.Fori(start, end) as i:
            first = self.n
            self.shift = (i - start) * per if start else i * per
            yield i
            assert self.n - first == per, (self.n - first, per)
        self.shift = 0
        self.n = first + per * (end - start)


def mods_before(l):
    return MODC // 4 + (3 + MOE_ITERS) * l


def trunk(nc, A, O):
    base, chunk_rows = stream_plan()
    NCHUNK = base["end"]
    NSUB = 2 * NCHUNK
    ctx = ExitStack()
    with ctx:
        def sem(name):
            return ctx.enter_context(nc.semaphore(name))

        place = [0]
        limit = 53200 * 4
        ctx.enter_context(nc.sbuf_tensor("whole", [P, limit // 4], F32))
        org = nc.sbuf_base - limit

        def at(name, shape, dt, offset):
            size = 4 * int(np.prod(shape[1:]))
            assert offset + size <= limit, (name, offset + size, limit)
            return nc.alloc_sbuf_tensor_at(name, shape, dt, offset=org + offset)

        def fixed(name, shape, dt=F32):
            t = at(name, shape, dt, place[0])
            place[0] += -(-4 * int(np.prod(shape[1:])) // 32) * 32
            return t

        raw = fixed("raw", [P, RAW, 2 * SUB])
        whi = fixed("whi", [P, SPL, SUB], F32R)
        wlo = fixed("wlo", [P, SPL, SUB], F32R)
        x = fixed("x_t", [P, KD, T])
        hh = fixed("hh", [P, KD, T], F32R)
        hl = fixed("hl", [P, KD, T], F32R)
        yoff = place[0]
        y = fixed("y_t", [P, KD, T])
        cols = fixed("cols", [P, NCOL])
        ident = fixed("ident", [P, P])
        ones = fixed("ones", [P, P])
        mean_d = fixed("mean_d", [P, P])
        mods = fixed("mods", [P, 2, 48, 2])
        cond = fixed("cond_s", [P, KD, 4], F32R)
        condf = fixed("cond_f", [P, KD, 2])
        cmod = fixed("cmod", [P, 2, KD, 2])
        eps = fixed("eps", [P, 1])
        modt = fixed("modt", [P, 8, 2])
        KB = 1024

        def ar(name, shape, dt=F32, kb=0.0):
            return at(name, shape, dt, AR + int(kb * KB))

        def yr(name, shape, dt=F32, kb=0.0):
            assert kb * KB + 4 * int(np.prod(shape[1:])) <= 12 * KB, name
            return at(name, shape, dt, yoff + int(kb * KB))

        wrt = fixed("wrt", [P, KD, NE])
        wrh = fixed("wrh", [P, KD, NE], F32R)
        wrl = fixed("wrl", [P, KD, NE], F32R)
        AR = place[0]
        sq = ar("ln_sq", [P, KD, T], F32, 0)
        h32 = ar("h32", [P, KD, T], F32, 12)
        std = ar("ln_std", [P, T], F32, 84)
        rstd = ar("ln_rstd", [P, T], F32, 86)
        gv = ar("gv", [P, NT, GW], F32, 0)
        gsh = ar("gsh", [P, 16, T], F32R, 24)
        gsl = ar("gsl", [P, 16, T], F32R, 48)
        gws = ar("gws", [P, 8, P], F32, 72)
        gu = ar("gu", [P, 4, T], F32, 76)
        gat = ar("gat", [P, T], F32, 82)
        gct = ar("gct", [P, 2, P], F32, 83.5)
        gst = ar("gst", [P, NT, 4, 6], F32, 85)
        gmv = ar("gmv", [P, NT, 2], F32, 86)
        grs = ar("grs", [P, NT, 2], F32, 86.5)
        gbs = yr("gbs", [P, 8, P], F32, 0)
        grow = yr("grow", [P, 8, P], F32, 4)
        gs32 = yr("gs32", [P, 2, T], F32, 8)
        cwb = ar("cwb", [P, NE, T], F32, 0)
        acc = ar("acc", [P, KD, T], F32, 24)
        diag = ar("diag", [P, NE, P], F32, 36)
        sg = ar("sg", [P, 2, 2, T], F32, 44)
        e32 = ar("e32", [P, 2, 2, T], F32, 50)
        eh = ar("eh", [P, 2, 2, T], F32R, 56)
        el = ar("el", [P, 2, 2, T], F32R, 62)
        et = ar("et", [P, 2, T], F32, 68)
        rt = ar("rt", [P, 16, NT, NE], F32, 71)
        xs = ar("xs", [P, 16, T], F32, 0)
        syh = ar("syh", [P, 16, T], F32R, 24)
        syl = ar("syl", [P, 16, T], F32R, 48)
        bc = ar("bc", [P, 8, T], F32, 24)
        xt = ar("xt", [P, NT, SI], F32, 36)
        bt = ar("bt", [P, NT, 4 * SN], F32, 60)
        cb = ar("cb", [P, NT, P], F32, 66)
        tri = ar("tri", [P, 2, P], F32, 72)
        lim = ar("lim", [P, 2, P], F32, 73)
        dt = ar("dt", [P, NT, 64], F32, 74)
        dta = ar("dta", [P, NT, 64], F32, 74.75)
        acs = ar("acs", [P, NT, 64], F32, 75.5)
        dend = ar("dend", [P, NT, 64], F32, 76.25)
        edec = ar("edec", [P, NT, 64], F32, 77)
        ea = ar("ea", [P, 64], F32, 77.75)
        se = [ar("se0", [P, 2, 4, P], F32, 78), ar("se1", [P, 2, 4, P], F32, 67.5)]
        sce = ar("sce", [P, 2, 4, P], F32, 82)
        swt = ar("swt", [P, 4, P], F32, 86)
        stg = ar("stg", [P, 2, T + 4], F32, 78)
        ctm = ar("ctm", [P, 2, T + 4], F32, 82)
        szt = ar("szt", [P, 2, T], F32, 78)
        sgy = ar("sgy", [P, 2, T], F32, 81)
        ssq = ar("ssq", [P, 2, T], F32, 84)
        srr = ar("srr", [P, T], F32, 87)
        s0 = yr("s0", [P, 2, 512], F32, 0)
        s1 = yr("s1", [P, 2, 512], F32, 4)
        xdd = yr("xdd", [P, 2, 512], F32, 8)
        dtw = ar("dtw", [P, 6, NT * 64], F32, 82)
        hq = ar("hq", [P, HH, T], F32, 0)
        hk = ar("hk", [P, 2, HH, T], F32, 12)
        hoh = ar("hoh", [P, HH, T], F32R, 12)
        hol = ar("hol", [P, HH, T], F32R, 24)
        hf = ar("hf", [P, 2, HH, T], F32, 36)
        hv = ar("hv", [P, NT, D], F32, 60)
        lvl = ar("lvl", [P, LEVELS, P], U32, 72)
        hrs = ar("hrs", [P, T], F32, 72)
        uw = ar("uw", [P, 2, 2, T], F32, 76)
        att = yr("att", [P, T], F32, 10)
        hs0 = yr("hs0", [P, 2, HH, P], F32, 0)
        hqe = yr("hqe", [P, 2, LS], F32, 8)
        hkh = ar("hkh", [P, 2, P], F32, 82)
        hkt = ar("hkt", [P, 2, P], F32, 83)
        hs1 = ar("hs1", [P, 2, P], F32, 84)
        hsto = ar("hsto", [P, 2, P], F32, 85)
        hmask = ar("hmask", [P, T], F32, 86)
        lbt2 = ar("lbt", [P, 96], F32, 75.5)
        hed = ar("hed", [P, 2], F32, 87.5)
        hres = ar("hres", [P, T], F32, 74)
        hsg = ar("hsg", [P, 2, T], F32, 76)
        hon = ar("hon", [P, 2, T], F32, 80)
        hsq = ar("hsq", [P, 2, T], F32, 84)

        ps = ctx.enter_context(nc.psum_tensor("ps", [P, 8, 512], F32))
        def bank(b):
            return ps[:, b, 0:T]

        raw_in = [sem(f"raw_in{i}") for i in range(RAW)]
        hst_out = [sem(f"hst_out{d}") for d in range(2)]
        names = """cols_in x_in consts_set hi_ready lo_ready sub_done mod_read cond_ready
            h32_ready hh_ready hl_ready y_ready mean_done diff_ready sq_ready var_done std_ready norm_ready x_ready
            v_evac v_norm u_evac rows_done rows_read mix_done a_ready s32_ready sh_ready sl_ready gmlp_in
            router_in router_split router_done route_ready cw_ready cwb_done cwb_read
            gate_read up_read e32_ready eh_ready el_ready down_added down_done
            dve_step act_step pool_step out_done ssd_in gstat_done gstd_done dtm_done dt_act dt_vec acs_done
            stage_ready conv_ready xbc_ready xpose_done xpose_read cb_done cb_read s0_in
            xdd_ready st_done s1_ready stout_read seg_done seg_ready exp_ready ce_exp ce_ready w_ready ydone y_read
            z_act gz_ready gy_ready gsq_ready syh_ready syl_ready rms_done rms_std
            hgrn_in q_evac f_act k_ready f_ln scan_ready vi_evac hs0_in u_sub u_exp uw_ready lv_done lv_read diag_done
            kh_exp kh_ready khT_done khT_read hst_done hs1_ready qe_exp qe_ready o_done o_read
            ho_sq hms_done hstd on_ready hg_act hon_ready hoh_ready hol_ready hmask_set conv_pad st_out edec_ready lb_act lb_vec""".split()
        S = {n: sem(n) for n in names}

        block = ctx.enter_context(nc.Block())

        def c_(name, i, n=1):
            return cols[:, COL[name] + i:COL[name] + i + n]

        @block.sync
        def _(sp):
            def load(c, slot, src, sub_width=SUB):
                if not (isinstance(c, int) and c < RAW):
                    sp.wait_ge(S["lo_ready"], (c - RAW) * 2 + 2)
                dst = raw[:, slot, :].rearrange("p (k n) -> p k n", k=src.shape[1])
                sp.dma_start(dst, src).then_inc(raw_in[slot], 16)

            def run(name, n, view, lo=0):
                c0 = base[name]
                if n >= 2 * RAW and n % RAW == 0 and c0 >= RAW:
                    with sp.Fori(0, n // RAW) as i:
                        for j in range(RAW):
                            load(c0 + j + i * RAW, (c0 + j) % RAW, view[bass.ds(lo + j + i * RAW, 1)][0])
                else:
                    for j in range(n):
                        load(c0 + j, (c0 + j) % RAW, view[lo + j])

            v8 = lambda w: w.rearrange("(k p) (c n) -> c p k n", p=P, n=2 * P)
            v16 = lambda w: w.rearrange("(k p) (c n) -> c p k n", p=P, n=P)
            sp.dma_start(cols[:, :], A["cols"]).then_inc(S["cols_in"], 16)
            mview = [v8(A["w_mod"][l]) for l in range(DEPTH)]
            for j in range(MODC):
                load(base["mod0"] + j, (base["mod0"] + j) % RAW, mview[0][j])
                if j == 3:
                    sp.dma_start(x[:, :, :], A["x_t"]).then_inc(S["x_in"], 16)
                    sp.dma_start(h32[:, :, 0:LS], A["pos_t"]).then_inc(S["x_in"], 16)
                    sp.dma_start(ident[:, :], A["masks"][:, 0:P]).then_inc(S["x_in"], 16)
                    sp.dma_start(wrt[:, :, :], A["w_router"].rearrange("(k p) e -> p k e", p=P)).then_inc(S["router_in"], 16)
            for l in range(DEPTH):
                kind = ("gmlp", "ssd", "hgrn")[l % 3]
                if kind == "gmlp":
                    g = l // 3
                    if l:
                        sp.wait_ge(S["hl_ready"], 8 * (2 * l + 1))
                    sp.dma_start(gws[:, :, :], A["gmlp_ws"][g]).then_inc(S["gmlp_in"], 16)
                    sp.dma_start(gbs[:, :, :], A["gmlp_bs"][g:g + 1, :].partition_broadcast(P)).then_inc(S["gmlp_in"], 16)
                    win = v8(A["gmlp_w_in"][g])
                    run((l, "v"), 8, win, 8)
                    run((l, "u"), 8, win, 0)
                    run((l, "out"), 8, v16(A["gmlp_w_out"][g]))
                elif kind == "ssd":
                    sp.wait_ge(S["hl_ready"], 8 * (2 * l + 1))
                    sp.dma_start(tri[:, :, :], A["masks"][:, P:3 * P]).then_inc(S["ssd_in"], 16)
                    sp.dma_start(lim[:, :, :], A["masks"][:, 3 * P:5 * P]).then_inc(S["ssd_in"], 16)
                    w = A["ssd_w_in"][0]
                    run((l, "dt"), 1, v8(w[:, SSD_IN - 256:SSD_IN]))
                    run((l, "xs"), 8, v8(w[:, SI:2 * SI]))
                    run((l, "bc"), 4, v8(w[:, 2 * SI:2 * SI + 1024]))
                    z = v8(w[:, 0:SI])
                    for j in range(4):
                        load(base[(l, "z")] + j, (base[(l, "z")] + j) % RAW, z[j])
                    for g in range(SG_):
                        if g:
                            sp.wait_ge(S["y_read"], 6 * g)
                        else:
                            sp.wait_ge(S["acs_done"], 2)
                        sp.dma_start(s0[:, :, :], A["s_ssd"][:, :, g * 512:(g + 1) * 512].rearrange("d n c -> n d c")).then_inc(S["s0_in"], 16)
                    for j in range(4, 8):
                        load(base[(l, "z")] + j, (base[(l, "z")] + j) % RAW, z[j])
                    run((l, "out"), 8, v16(A["ssd_w_out"][0]))
                else:
                    sp.wait_ge(S["hl_ready"], 8 * (2 * l + 1))
                    sp.dma_start(lvl[:, :, :], A["levels"]).then_inc(S["hgrn_in"], 16)
                    sp.dma_start(hs0[:, :, :, :], A["s_hgrn"]).then_inc(S["hgrn_in"], 16)
                    w = v8(A["hgrn_w_in"][0])
                    run((l, "q"), 4, w, 0)
                    run((l, "f"), 8, w, 4)
                    run((l, "i"), 4, w, 12)
                    run((l, "g"), 4, w, 16)
                    run((l, "out"), 4, v8(A["hgrn_w_out"][0]))
                more = l + 1 < DEPTH
                q = 0
                for part, n in (("ln1", LN1_MODS), ("router", ROUTER_MODS)):
                    for j in range(n if more else 0):
                        load(base[(l, part)] + j, (base[(l, part)] + j) % RAW, mview[l + 1][q])
                        q += 1
                gu_ = A["moe_w_gu"][l].rearrange("e (k p) (c n) -> e c p k n", p=P, n=2 * P)
                dn = A["moe_w_down"][l].rearrange("e (k p) n -> e p k n", p=P)
                nm = MOE_MODS // MOE_ITERS if more else 0
                c0 = base[(l, "moe")]
                with sp.Fori(0, MOE_ITERS) as i:
                    for p, (what, j) in enumerate(moe_order(nm)):
                        c = c0 + p + i * (12 + nm)
                        slot = (c0 + p) % RAW
                        if what == "M":
                            load(c, slot, mview[l + 1][bass.ds(q + j + i * nm, 1)][0])
                        elif what == "D":
                            load(c, slot, dn[bass.ds(j + i * EG, 1)][0])
                        else:
                            load(c, slot, gu_[bass.ds(j + i * EG, 1)][0][int(what == "U")])
                q += MOE_MODS
                for j in range(LN2_MODS if more else 0):
                    load(base[(l, "ln2")] + j, (base[(l, "ln2")] + j) % RAW, mview[l + 1][q])
                    q += 1
            sp.wait_ge(S["x_ready"], 8 * (2 * DEPTH + 1))
            sp.dma_start(O["y_t"], x[:, :, :]).then_inc(S["out_done"], 16)
            sp.wait_ge(S["out_done"], 16)
            sp.wait_ge(S["st_out"], 16 * 2 * SG_)
            for d in range(2):
                sp.wait_ge(hst_out[d], 16 * HH)
        def sb(name, j=0):
            return 2 * base[name] + j

        STATES = ((0, 0), (0, 1), (1, 0), (2, 1))
        def toks(t):
            return slice(t * P, (t + 1) * P)

        def act_ssd(act, l, feed):
            for j in range(24):
                s = sb((l, "xs"), j)
                if j == 0:
                    feed(sb((l, "dt")) + 3)
                    act.wait_ge(S["dt_vec"], 1)
                    act.activation(dtw[:, 2, :], dtw[:, 1, :], ACT.Exp).then_inc(S["dt_act"], 1)
                    act.activation(ea[:, :], c_("alog", 0, 64), ACT.Exp).then_inc(S["dt_act"], 1)
                    act.wait_ge(S["dt_vec"], 2)
                    act.activation(dtw[:, 4, :], dtw[:, 3, :], ACT.Ln).then_inc(S["dt_act"], 1)
                    act.wait_ge(S["dt_vec"], 4)
                    act.activation(dend[:, :, :], dend[:, :, :], ACT.Exp).then_inc(S["dt_act"], 1)
                    act.activation(edec[:, :, :], ps[:, 5, 0:NT * 64].rearrange("p (t h) -> p t h", t=NT),
                                   ACT.Exp).then_inc(S["dt_act"], 1)
                    act.wait_ge(S["conv_pad"], 1)
                feed(s + 3)
                act.wait_ge(S["sub_done"], s + 1)
                if j >= 2:
                    act.wait_ge(S["conv_ready"], j - 1)
                act.activation(stg[:, j % 2, 1:LC + 1], ps[:, j % 4, 0:LC], ACT.Copy)
                act.activation(stg[:, j % 2, LC + 3:T + 3], ps[:, j % 4, LC:T], ACT.Copy).then_inc(S["stage_ready"], 1)
                for i in ([j - 1] if j else []) + ([23] if j == 23 else []):
                    act.wait_ge(S["conv_ready"], i + 1)
                    dst = xs[:, i, :] if i < 16 else bc[:, i - 16, :]
                    act.activation(dst[:, 0:LC], ctm[:, i % 2, 0:LC], ACT.Silu)
                    act.activation(dst[:, LC:T], ctm[:, i % 2, LC + 2:T + 2], ACT.Silu).then_inc(S["xbc_ready"], 1)
            feed(sb((l, "z")) + 3)
            for n in range(15):
                act.wait_ge(S["xpose_done"], n + 1)
                t, g = divmod(n, 5)
                dst = xt[:, t, g * 512:(g + 1) * 512] if g < 4 else bt[:, t, :]
                act.activation(dst, ps[:, 4 + n % 4, :], ACT.Copy).then_inc(S["xpose_read"], 1)
            for g in range(SG_):
                act.wait_ge(S["cb_done"], g + 1)
                act.activation(cb[:, :, :].rearrange("p t n -> p (t n)"), bank(6 + g % 2), ACT.Copy).then_inc(S["cb_read"], 1)
                for d in range(2):
                    act.wait_ge(S["st_done"], 4 * g + d + 1)
                    act.activation(sce[:, d, :, :].rearrange("p a b -> p (a b)"), ps[:, 4 + d, :], ACT.Copy).then_inc(S["stout_read"], 1)
                    act.wait_ge(S["stout_read"], 2 * g + d + 1)
                    act.dma_start(O["n_ssd"][d][:, g * 512:(g + 1) * 512],
                                  sce[:, d, :, :].rearrange("p a b -> p (a b)")).then_inc(S["st_out"], 16)
                for u in range(6 * g, 6 * g + 6):
                    t = (u % 6) // 2
                    act.wait_ge(S["seg_ready"], u + 1)
                    act.activation(se[u % 2][:, :, :, :], se[u % 2][:, :, :, :], ACT.Exp).then_inc(S["exp_ready"], 1)
                    if t:
                        if u % 6 == 2:
                            act.wait_ge(S["st_out"], 32 * (g + 1))
                        else:
                            act.wait_ge(S["ydone"], u)
                        act.activation(sce[:, :, :, :].rearrange("p d r n -> p d (r n)"),
                                       ps[:, 2 * (u % 2):2 * (u % 2) + 2, :], ACT.Exp).then_inc(S["ce_exp"], 1)
            for j in range(17):
                if j < 16:
                    s = sb((l, "z"), j)
                    feed(s + 3)
                    act.wait_ge(S["sub_done"], s + 1)
                    if j >= 2:
                        act.wait_ge(S["gz_ready"], j - 1)
                    act.activation(szt[:, j % 2, :], bank(j % 4), ACT.Silu).then_inc(S["z_act"], 1)
                if j == 16:
                    feed(sb((l, "out")) + 3)
                if j:
                    act.wait_ge(S["gz_ready"], j)
                    if j >= 3:
                        act.wait_ge(S["rms_done"], j - 2)
                    act.activation(ssq[:, (j - 1) % 2, :], xs[:, j - 1, :], ACT.Square).then_inc(S["gsq_ready"], 1)
                    act.wait_ge(S["gy_ready"], j)
                    act.activation(syh[:, j - 1, :], sgy[:, (j - 1) % 2, :], ACT.Copy).then_inc(S["syh_ready"], 1)
            act.wait_ge(S["rms_done"], 16)
            act.activation(srr[:, :], bank(6), ACT.Sqrt, bias=eps[:, 0:1], scale=0.5).then_inc(S["rms_std"], 1)
            for m in range(8):
                feed(sb((l, "out"), 2 * m + 2) + 3)

        def pool_ssd(pool, l, feed):
            pool.memset(stg[:, :, :], 0.0).then_inc(S["conv_pad"], 1)
            feed(sb((l, "z")) + 3)
            for u in range(24):
                if (u % 6) // 2:
                    t, g = (u % 6) // 2, u // 6
                    n = sum(1 for v in range(u) if (v % 6) // 2)
                    pool.wait_ge(S["ce_exp"], n + 1)
                    pool.tensor_tensor(sce[:, :, :, :].rearrange("p d r n -> p (d r) n"), sce[:, :, :, :].rearrange("p d r n -> p (d r) n"),
                                       bc[:, 4 + g, toks(t)].unsqueeze(1).to_broadcast([P, 8, P]), ALU.mult).then_inc(S["ce_ready"], 1)
            for j in range(16):
                feed(min(sb((l, "z"), j) + 4, sb((l, "out")) + 3))
                pool.wait_ge(S["syh_ready"], j + 1)
                pool.tensor_tensor(syl[:, j, :], sgy[:, j % 2, :], syh[:, j, :].bitcast(F32), ALU.subtract).then_inc(S["syl_ready"], 1)

        def pe_ssd(pe, l, claim, release, full, by_token, out_tiles):
            for k in range(KD):
                pe.wait_ge(S["hl_ready"], 8 * (2 * l) + k + 1)
            s = sb((l, "dt"))
            pe.wait_ge(S["lo_ready"], s + 2)
            claim(4, "dt_vec", 1)
            for t in range(NT):
                for k in range(KD):
                    w = slice(k * P + 64, (k + 1) * P)
                    o = ps[:, 4, t * 64:(t + 1) * 64]
                    pe.matmul(o, hh[:, k, toks(t)], whi[:, (s + 1) % SPL, w], start=(k == 0), stop=False)
                    pe.matmul(o, hl[:, k, toks(t)], whi[:, (s + 1) % SPL, w], start=False, stop=False)
                    ins = pe.matmul(o, hh[:, k, toks(t)], wlo[:, (s + 1) % SPL, w], start=False, stop=(k == KD - 1))
            ins.then_inc(S["sub_done"], 2)
            for j in range(24):
                s = sb((l, "xs"), j)
                pe.wait_ge(S["lo_ready"], s + 1)
                if j == 0:
                    for b in range(4):
                        claim(b, "stage_ready", b + 1)
                else:
                    claim(j % 4, "stage_ready", j + 1) if j >= 4 else None
                full(s, bank(j % 4), hh, hl)
                if j == 1:
                    pe.wait_ge(S["dt_vec"], 3)
                    pe.wait_ge(S["ssd_in"], 32)
                    claim(5, "dt_act", 5)
                    claim(4, "dt_vec", 4)
                    for t in range(NT):
                        for d in range(2):
                            c = t * 64 + d * 32
                            ins = pe.matmul(ps[:, 4, c:c + 32], tri[:, d, :], dta[:, t, d * 32:(d + 1) * 32], start=True, stop=True)
                    ins.then_inc(S["acs_done"], 1)
                    pe.matmul(ps[:, 5, 0:NT * 64], ones[:, :], dta[:, :, :].rearrange("p t h -> p (t h)"), start=True,
                              stop=True).then_inc(S["acs_done"], 1)
            pe.wait_ge(S["dt_act"], 5)
            for n in range(15):
                t, g = divmod(n, 5)
                pe.wait_ge(S["xbc_ready"], 4 * g + 4)
                claim(4 + n % 4, "xpose_read", n + 1)
                for i in range(4):
                    src = xs[:, 4 * g + i, toks(t)] if g < 4 else bc[:, i, toks(t)]
                    ins = pe.transpose(ps[:, 4 + n % 4, i * P:(i + 1) * P], src, ident[:, :])
                ins.then_inc(S["xpose_done"], 1)
            pe.wait_ge(S["xbc_ready"], 24)

            def seg(u):
                t, h0 = (u % 6) // 2, (u // 6) * 8 + (u % 2) * 4
                if u < 2:
                    claim(2 * u, "w_ready", 0); claim(2 * u + 1, "w_ready", 0)
                for d in range(2):
                    for r in range(4):
                        ins = pe.matmul(ps[:, 2 * (u % 2) + d, r * P:(r + 1) * P],
                                        dta[:, t, d * 32 + h0 + r:d * 32 + h0 + r + 1].to_broadcast([P, P]), tri[:, d, :],
                                        start=True, stop=True)
                ins.then_inc(S["seg_done"], 1)

            for g in range(SG_):
                claim(6 + g % 2, "cb_read", g + 1)
                if g:
                    pe.wait_ge(S["w_ready"], 6 * g)
                for t in range(NT):
                    ins = pe.matmul(ps[:, 6 + g % 2, toks(t)], bc[:, g, toks(t)], bc[:, 4 + g, toks(t)], start=True, stop=True)
                ins.then_inc(S["cb_done"], 1)
                for j, (t, d) in enumerate(STATES):
                    pe.wait_ge(S["xdd_ready"], 4 * g + j + 1)
                    if j < 2:
                        claim(4 + j, "stout_read", 2 * g + j + 1)
                    else:
                        claim(2 + j, "s1_ready", 2 * g + j - 1)
                    pe.matmul(ps[:, 4 + j % 2, :], bt[:, t, g * SN:(g + 1) * SN], xdd[:, j % 2, :], start=True,
                              stop=True).then_inc(S["st_done"], 1)
                if g == 0:
                    seg(0)
                for u in range(6 * g, 6 * g + 6):
                    if u + 1 < 24:
                        seg(u + 1)
                    t, q = (u % 6) // 2, u % 2
                    pe.wait_ge(S["cb_read"], g + 1)
                    pe.wait_ge(S["w_ready"], u + 1)
                    if t:
                        n = sum(1 for v in range(u) if (v % 6) // 2)
                        pe.wait_ge(S["ce_ready"], n + 1)
                        pe.wait_ge(S["s1_ready"], 2 * g + 2)
                    claim(6 + u % 2, "y_read", u + 1)
                    for r in range(4):
                        o = ps[64 * (r % 2):64 * (r % 2) + 64, 6 + u % 2, (r // 2) * P:(r // 2 + 1) * P]
                        hc = slice((4 * q + r) * SP_, (4 * q + r + 1) * SP_)
                        ins = pe.matmul(o, xt[:, t, g * 512 + hc.start:g * 512 + hc.stop], swt[:, r, :], start=True, stop=(t == 0))
                        if t:
                            pe.matmul(o, (s0 if t == 1 else s1)[:, 0, hc], sce[:, 0, r, :], start=False, stop=False)
                            ins = pe.matmul(o, (s1 if t == 1 else s0)[:, 1, hc], sce[:, 1, r, :], start=False, stop=True)
                    ins.then_inc(S["ydone"], 1)
            for b in range(4):
                release[b] = (S["w_ready"], 24)

            def squares(j):
                pe.wait_ge(S["gsq_ready"], j + 1)
                pe.matmul(bank(6), mean_d[:, :], ssq[:, j % 2, :], start=(j == 0),
                          stop=(j == 15)).then_inc(S["rms_done"], 1)

            claim(6, "rms_std", 1)
            for j in range(16):
                s = sb((l, "z"), j)
                pe.wait_ge(S["lo_ready"], s + 1)
                claim(j % 4, "z_act", j + 1)
                full(s, bank(j % 4), hh, hl)
                if j >= 2:
                    squares(j - 2)
            squares(14)
            squares(15)
            pe.wait_ge(S["syl_ready"], 16)
            out_tiles(l, syh, syl, 2)

        def dve_ssd(dve, l, link, start_residual, residual):
            w3 = lambda n: dtw[:, n, :].rearrange("p (t h) -> p t h", t=NT)
            dve.wait_ge(S["sub_done"], sb((l, "dt")) + 2)
            link(dve.tensor_tensor(w3(0), ps[:, 4, 0:NT * 64].rearrange("p (t h) -> p t h", t=NT),
                                   c_("dtb", 0, 64).unsqueeze(1).to_broadcast([P, NT, 64]), ALU.add))
            link(dve.tensor_scalar(dtw[:, 1, :], dtw[:, 0, :], -1.0, None, ALU.mult))
            dve.tensor_tensor(dtw[:, 1, :], dtw[:, 1, :], dtw[:, 0, :], ALU.min).then_inc(S["dt_vec"], 1)
            dve.wait_ge(S["dt_act"], 1)
            dve.tensor_scalar(dtw[:, 3, :], dtw[:, 2, :], 1.0, None, ALU.add).then_inc(S["dt_vec"], 1)
            dve.wait_ge(S["dt_vec"], 2)
            link(dve.tensor_scalar(dtw[:, 5, :], dtw[:, 3, :], -1.0, None, ALU.add))
            link(dve.tensor_tensor(dtw[:, 5, :], dtw[:, 2, :], dtw[:, 5, :], ALU.subtract))
            link(dve.reciprocal(dtw[:, 1, :], dtw[:, 3, :]))
            link(dve.tensor_tensor(dtw[:, 5, :], dtw[:, 5, :], dtw[:, 1, :], ALU.mult))
            dve.wait_ge(S["dt_act"], 3)
            link(dve.tensor_tensor(dtw[:, 5, :], dtw[:, 5, :], dtw[:, 4, :], ALU.add))
            link(dve.scalar_tensor_tensor(out=dt[:, :, :], in0=w3(0), scalar=0.0, in1=w3(5), op0=ALU.max, op1=ALU.add))
            dve.scalar_tensor_tensor(out=dta[:, :, :], in0=dt[:, :, :], scalar=-1.0,
                                     in1=ea[:, :].unsqueeze(1).to_broadcast([P, NT, 64]), op0=ALU.mult,
                                     op1=ALU.mult).then_inc(S["dt_vec"], 1)
            dve.wait_ge(S["acs_done"], 2)
            link(dve.tensor_copy(acs[:, :, :].rearrange("p t h -> p (t h)"), ps[:, 4, 0:NT * 64]))
            dve.tensor_tensor(dend[:, :, :].rearrange("p t h -> p (t h)"), ps[:, 5, 0:NT * 64],
                              acs[:, :, :].rearrange("p t h -> p (t h)"), ALU.subtract).then_inc(S["dt_vec"], 1)
            dve.wait_ge(S["dt_act"], 4)
            link(dve.tensor_tensor(dend[:, :, :], dend[:, :, :], dt[:, :, :], ALU.mult))
            for j in range(24):
                dve.wait_ge(S["stage_ready"], j + 1)
                if j >= 2:
                    dve.wait_ge(S["xbc_ready"], j - 1)
                a, n = ctm[:, j % 2, 0:T + 2], T + 2
                link(dve.tensor_scalar(a, stg[:, j % 2, 0:n], c_("convw", j), c_("convb", j), ALU.mult, ALU.add))
                link(dve.scalar_tensor_tensor(out=a, in0=stg[:, j % 2, 1:n + 1], scalar=c_("convw", 24 + j), in1=a, op0=ALU.mult, op1=ALU.add))
                dve.scalar_tensor_tensor(out=a, in0=stg[:, j % 2, 2:n + 2], scalar=c_("convw", 48 + j), in1=a, op0=ALU.mult,
                                         op1=ALU.add).then_inc(S["conv_ready"], 1)
            heads = lambda a, t, d, g: a[:, t, d * 32 + 8 * g:d * 32 + 8 * g + 8].unsqueeze(2).to_broadcast([P, 8, SP_])
            by_head = lambda a: a.rearrange("p (h w) -> p h w", w=SP_)

            def segment(u):
                t, h0 = (u % 6) // 2, (u // 6) * 8 + (u % 2) * 4
                dve.wait_ge(S["seg_done"], u + 1)
                if u >= 2:
                    dve.wait_ge(S["w_ready"], u - 1)
                for d in range(2):
                    for r in range(4):
                        ins = dve.scalar_tensor_tensor(out=se[u % 2][:, d, r, :], in0=ps[:, 2 * (u % 2) + d, r * P:(r + 1) * P],
                                                       scalar=acs[:, t, d * 32 + h0 + r:d * 32 + h0 + r + 1], in1=lim[:, d, :],
                                                       op0=ALU.subtract, op1=ALU.min)
                ins.then_inc(S["seg_ready"], 1)

            def y_out(u):
                t, g, q = (u % 6) // 2, u // 6, u % 2
                dve.wait_ge(S["ydone"], u + 1)
                for i in range(2):
                    f = 4 * g + 2 * q + i
                    ins = dve.scalar_tensor_tensor(out=xs[:, f, toks(t)], in0=xs[:, f, toks(t)], scalar=c_("dskip", f),
                                                   in1=ps[:, 6 + u % 2, i * P:(i + 1) * P], op0=ALU.mult, op1=ALU.add)
                ins.then_inc(S["y_read"], 1)

            dve.wait_ge(S["xpose_read"], 15)
            for g in range(SG_):
                if g:
                    y_out(6 * g - 1)
                for j, (t, d) in enumerate(STATES):
                    if 4 * g + j >= 2:
                        dve.wait_ge(S["st_done"], 4 * g + j - 1)
                    dve.tensor_tensor(by_head(xdd[:, j % 2, :]), by_head(xt[:, t, g * 512:(g + 1) * 512]), heads(dend, t, d, g),
                                      ALU.mult).then_inc(S["xdd_ready"], 1)
                dve.wait_ge(S["s0_in"], 16 * (g + 1))
                for j in (2, 3):
                    t, d = STATES[j]
                    link(dve.tensor_tensor(by_head(s1[:, d, :]), by_head(s0[:, d, :]), heads(edec, t, d, g), ALU.mult))
                    dve.wait_ge(S["st_done"], 4 * g + j + 1)
                    dve.tensor_tensor(s1[:, d, :], s1[:, d, :], ps[:, 4 + j % 2, :], ALU.add).then_inc(S["s1_ready"], 1)
                if g == 0:
                    segment(0)
                for u in range(6 * g, 6 * g + 6):
                    t, h0 = (u % 6) // 2, g * 8 + (u % 2) * 4
                    if u + 1 < 24:
                        segment(u + 1)
                    dve.wait_ge(S["exp_ready"], u + 1)
                    e = se[u % 2]
                    for r in range(4):
                        ins = dve.tensor_scalar(e[:, 1, r, :], e[:, 1, r, :], dt[:, t, 32 + h0 + r:33 + h0 + r], None, ALU.mult)
                    link(ins)
                    for r in range(4):
                        ins = dve.scalar_tensor_tensor(out=e[:, 0, r, :], in0=e[:, 0, r, :], scalar=dt[:, t, h0 + r:h0 + r + 1],
                                                       in1=e[:, 1, r, :], op0=ALU.mult, op1=ALU.add)
                    link(ins)
                    dve.wait_ge(S["cb_read"], g + 1)
                    if u:
                        dve.wait_ge(S["ydone"], u)
                    dve.tensor_tensor(swt[:, :, :], e[:, 0, :, :], cb[:, t, :].unsqueeze(1).to_broadcast([P, 4, P]),
                                      ALU.mult).then_inc(S["w_ready"], 1)
                    if u % 6:
                        y_out(u - 1)
            y_out(23)
            for j in range(16):
                dve.wait_ge(S["z_act"], j + 1)
                dve.tensor_tensor(xs[:, j, :], xs[:, j, :], szt[:, j % 2, :], ALU.mult).then_inc(S["gz_ready"], 1)
                dve.wait_ge(S["gz_ready"], j + 1)
                if j >= 2:
                    dve.wait_ge(S["syl_ready"], j - 1)
                dve.tensor_scalar(sgy[:, j % 2, :], xs[:, j, :], c_("sng", j), None, ALU.mult).then_inc(S["gy_ready"], 1)
            start_residual(2 * l)
            dve.wait_ge(S["rms_std"], 1)
            link(dve.reciprocal(srr[:, :], srr[:, :]))
            for m in range(KD):
                dve.wait_ge(S["sub_done"], sb((l, "out"), 2 * m + 2))
                link(dve.tensor_tensor(szt[:, m % 2, :], bank(m % 4), srr[:, :], ALU.mult))
                residual(l, m, szt[:, m % 2, :], 16)

        def act_hgrn(act, l, feed):
            feed(sb((l, "q")) + 3)
            act.wait_ge(S["lb_vec"], 1)
            act.activation(lbt2[:, 0:64], lbt2[:, 0:64], ACT.Exp).then_inc(S["lb_act"], 1)
            for j in range(8):
                s = sb((l, "q"), j)
                feed(s + 3)
                act.wait_ge(S["sub_done"], s + 1)
                act.activation(hq[:, j, :], bank(j % 4), ACT.Copy).then_inc(S["q_evac"], 1)
            for j in range(16):
                s = sb((l, "f"), j)
                feed(s + 3)
                act.wait_ge(S["sub_done"], s + 1)
                act.activation(hk[:, j // 8, j % 8, :], bank(j % 4), ACT.Sigmoid).then_inc(S["f_act"], 1)
            for c in range(4):
                s = sb((l, "i"), 2 * c)
                feed(s + 3)
                act.wait_ge(S["sub_done"], s + 2)
                for t in range(NT):
                    ins = act.activation(hv[:, t, c * 256:(c + 1) * 256], ps[:, 3 * (c % 2) + t, 0:256], ACT.Copy)
                ins.then_inc(S["vi_evac"], 1)
            feed(sb((l, "g")) + 3)
            act.wait_ge(S["k_ready"], 16)
            for d in range(2):
                act.activation(hf[:, d, :, :], hf[:, d, :, :], ACT.Ln).then_inc(S["f_ln"], 1)
            for h in range(HH):
                for j, (t, d) in enumerate(STATES):
                    n = 4 * h + j
                    act.wait_ge(S["scan_ready"], 8 + h + 1)
                    if n >= 2:
                        act.wait_ge(S["khT_done"], n - 1)
                    last = t * P + (P - 1 if d == 0 else 0)
                    act.activation(hkh[:, n % 2, :], hf[:, d, h, toks(t)], ACT.Exp, scale=-1.0,
                                   bias=hf[:, d, h, last:last + 1]).then_inc(S["kh_exp"], 1)
                if h:
                    act.wait_ge(S["o_done"], h)
                act.activation(hqe[:, :, :], hf[:, :, h, LC:T], ACT.Exp).then_inc(S["qe_exp"], 1)
                for j in (2, 3):
                    t, d = STATES[j]
                    last = t * P + (P - 1 if d == 0 else 0)
                    if h:
                        act.wait_ge(S["hs1_ready"], 2 * h)
                    act.activation(hed[:, d:d + 1], hf[:, d, h, last:last + 1], ACT.Exp).then_inc(S["edec_ready"], 1)
                for j in range(2):
                    act.wait_ge(S["hst_done"], 4 * h + j + 1)
                    if h:
                        act.wait_ge(hst_out[j], 16 * h)
                    act.activation(hsto[:, j, :], ps[:, 6 + j, 0:P], ACT.Copy).then_inc(S["stout_read"], 1)
                    act.wait_ge(S["stout_read"], 2 * SG_ + 2 * h + j + 1)
                    act.dma_start(O["n_hgrn"][:, j, h, :], hsto[:, j, :]).then_inc(hst_out[j], 16)
                for j in range(LEVELS):
                    n = LEVELS * h + j
                    act.wait_ge(S["u_sub"], n + 1)
                    act.activation(uw[:, (j + 1) % 2, :, :], uw[:, (j + 1) % 2, :, :], ACT.Exp).then_inc(S["u_exp"], 1)
                act.wait_ge(S["o_done"], h + 1)
                act.activation(hq[:, h, :], bank(2 + h % 2), ACT.Copy).then_inc(S["o_read"], 1)
            for d in range(2):
                act.wait_ge(hst_out[d], 16 * HH)
            for h in range(HH):
                if h >= 2:
                    act.wait_ge(S["hms_done"], h - 1)
                act.wait_ge(S["o_read"], h + 1)
                act.activation(hsq[:, h % 2, :], hq[:, h, :], ACT.Square).then_inc(S["ho_sq"], 1)
                if h >= 1:
                    act.wait_ge(S["hms_done"], h)
                    if h >= 2:
                        act.wait_ge(S["on_ready"], h - 1)
                    act.activation(hres[:, :], bank(4 + (h - 1) % 2), ACT.Sqrt, bias=eps[:, 0:1], scale=8.0).then_inc(S["hstd"], 1)
            act.wait_ge(S["hms_done"], HH)
            act.wait_ge(S["on_ready"], HH - 1)
            act.activation(hres[:, :], bank(4 + (HH - 1) % 2), ACT.Sqrt, bias=eps[:, 0:1], scale=8.0).then_inc(S["hstd"], 1)
            for j in range(9):
                if j < 8:
                    s = sb((l, "g"), j)
                    feed(s + 3)
                    act.wait_ge(S["sub_done"], s + 1)
                    if j >= 2:
                        act.wait_ge(S["hon_ready"], j - 1)
                    act.activation(hsg[:, j % 2, :], bank(j % 4), ACT.Silu).then_inc(S["hg_act"], 1)
                if j == 8:
                    feed(sb((l, "out")) + 3)
                if j:
                    act.wait_ge(S["hon_ready"], j)
                    act.activation(hoh[:, j - 1, :], hon[:, (j - 1) % 2, :], ACT.Copy).then_inc(S["hoh_ready"], 1)
            for m in range(8):
                feed(sb((l, "out"), m + 1) + 3)

        def pool_hgrn(pool, l, feed):
            pool.memset(hmask[:, :], 1.0).then_inc(S["hmask_set"], 1)
            pool.wait_ge(S["hmask_set"], 1)
            pool.memset(hmask[:, :].rearrange("p (t n) -> p t n", t=NT)[:, :, 0:1], 0.0).then_inc(S["hmask_set"], 1)
            feed(sb((l, "g")) + 3)
            for h in range(HH):
                pool.wait_ge(S["qe_exp"], h + 1)
                pool.tensor_tensor(hqe[:, :, :], hqe[:, :, :], hq[:, h, LC:T].unsqueeze(1).to_broadcast([P, 2, LS]),
                                   ALU.mult).then_inc(S["qe_ready"], 1)
            for j in range(8):
                feed(min(sb((l, "g"), j) + 4, sb((l, "out")) + 3))
                pool.wait_ge(S["hoh_ready"], j + 1)
                pool.tensor_tensor(hol[:, j, :], hon[:, j % 2, :], hoh[:, j, :].bitcast(F32), ALU.subtract).then_inc(S["hol_ready"], 1)

        def pe_hgrn(pe, l, claim, release, full, by_token, out_tiles):
            for k in range(KD):
                pe.wait_ge(S["hl_ready"], 8 * (2 * l) + k + 1)
            for part, n, name in (("q", 8, "q_evac"), ("f", 16, "f_act")):
                for j in range(n):
                    s = sb((l, part), j)
                    pe.wait_ge(S["lo_ready"], s + 1)
                    claim(j % 4, name, j + 1)
                    full(s, bank(j % 4), hh, hl)
            for c in range(4):
                s = sb((l, "i"), 2 * c)
                pe.wait_ge(S["lo_ready"], s + 2)
                for t in range(NT):
                    claim(3 * (c % 2) + t, "vi_evac", c + 1)
                by_token(s, [ps[:, 3 * (c % 2) + t, 0:256] for t in range(NT)])
            for b in range(6):
                pe.wait_ge(*release[b])
            for b in (6, 7):
                if b in release:
                    pe.wait_ge(*release[b])
            pe.wait_ge(S["mod_read"], mods_before(l))
            pe.wait_ge(S["hgrn_in"], 32)
            for h in range(HH):
                hc = slice(h * P, (h + 1) * P)

                def state(j):
                    n, (t, d) = 4 * h + j, STATES[j]
                    pe.wait_ge(S["khT_read"], n + 1)
                    if j >= 2:
                        pe.wait_ge(S["stout_read"], 2 * SG_ + 2 * h + j - 1)
                    elif h:
                        pe.wait_ge(S["hs1_ready"], 2 * h - 1 + j)
                    pe.matmul(ps[:, 6 + n % 2, 0:P], hkt[:, n % 2, :], hv[:, t, hc], start=True, stop=True).then_inc(S["hst_done"], 1)

                for j in range(4):
                    n = 4 * h + j
                    pe.wait_ge(S["kh_ready"], n + 1)
                    if n >= 2:
                        pe.wait_ge(S["khT_read"], n - 1)
                    pe.transpose(ps[:, 4 + n % 2, 0:P], hkh[:, n % 2, :], ident[:, :]).then_inc(S["khT_done"], 1)
                    if j:
                        state(j - 1)
                state(3)
                for j in range(LEVELS + 1):
                    n = (LEVELS + 1) * h + j
                    pe.wait_ge(S["uw_ready"], n + 1)
                    if n >= 2:
                        pe.wait_ge(S["lv_read"], n - 1)
                    for t in range(NT):
                        rhs = uw[:, j % 2, 1, toks(t)] if j else hq[:, h, toks(t)]
                        ins = pe.matmul(ps[:, n % 2, toks(t)], uw[:, j % 2, 0, toks(t)], rhs, start=True, stop=True)
                    ins.then_inc(S["lv_done"], 1)
                pe.wait_ge(S["lv_read"], (LEVELS + 1) * (h + 1))
                pe.wait_ge(S["qe_ready"], h + 1)
                pe.wait_ge(S["hs1_ready"], 2 * h + 2)
                if h >= 2:
                    pe.wait_ge(S["o_read"], h - 1)
                for t in range(NT):
                    o = ps[:, 2 + h % 2, toks(t)]
                    ins = pe.matmul(o, hv[:, t, hc], att[:, toks(t)], start=True, stop=(t == 0))
                    if t:
                        pe.matmul(o, hs0[:, 0, h, :] if t == 1 else hs1[:, 0, :], hqe[:, 0, toks(t - 1)], start=False, stop=False)
                        ins = pe.matmul(o, hs1[:, 1, :] if t == 1 else hs0[:, 1, h, :], hqe[:, 1, toks(t - 1)], start=False, stop=True)
                ins.then_inc(S["o_done"], 1)
            pe.wait_ge(S["khT_read"], 32)
            for h in range(HH):
                pe.wait_ge(S["ho_sq"], h + 1)
                if h >= 2:
                    pe.wait_ge(S["hstd"], h - 1)
                pe.matmul(bank(4 + h % 2), mean_d[:, :], hsq[:, h % 2, :], start=True, stop=True).then_inc(S["hms_done"], 1)
            release[4] = release[5] = (S["hstd"], 8)
            for b, v in ((0, ("lv_read", 64)), (1, ("lv_read", 64)), (2, ("o_read", 8)), (3, ("o_read", 8)),
                         (6, ("hs1_ready", 16)), (7, ("hs1_ready", 16))):
                release[b] = (S[v[0]], v[1])
            for j in range(8):
                s = sb((l, "g"), j)
                pe.wait_ge(S["lo_ready"], s + 1)
                claim(j % 4, "hg_act", j + 1)
                full(s, bank(j % 4), hh, hl)
            pe.wait_ge(*release[7])
            pe.wait_ge(S["hol_ready"], 8)
            out_tiles(l, hoh, hol, 1)

        def dve_hgrn(dve, l, link, start_residual, residual):
            lg = lambda i: c_("lbl", 16 * i, 16)
            e = lambda i: lbt2[:, 16 * i:16 * i + 16]
            link(dve.tensor_tensor(e(4), lg(0), lg(1), ALU.max))
            link(dve.tensor_tensor(e(4), e(4), lg(2), ALU.max))
            link(dve.tensor_tensor(e(4), e(4), lg(3), ALU.max))
            link(dve.tensor_tensor(lbt2[:, 0:64].rearrange("p (i c) -> p i c", i=DEPTH), c_("lbl", 0, 64).rearrange("p (i c) -> p i c", i=DEPTH),
                                   e(4).unsqueeze(1).to_broadcast([P, DEPTH, 16]), ALU.subtract))
            dve.tensor_copy(e(5), e(4)).then_inc(S["lb_vec"], 1)
            dve.wait_ge(S["lb_act"], 1)
            link(dve.tensor_tensor(e(4), e(0), e(1), ALU.add))
            link(dve.tensor_tensor(e(4), e(4), e(2), ALU.add))
            link(dve.tensor_tensor(e(5), e(4), e(3), ALU.add))
            link(dve.reciprocal(e(5), e(5)))
            link(dve.tensor_tensor(e(0), e(0), e(5), ALU.mult))
            link(dve.tensor_tensor(e(4), e(4), e(5), ALU.mult))
            link(dve.tensor_tensor(e(4), e(4), e(0), ALU.subtract))
            link(dve.tensor_scalar(e(5), e(4), -1.0, 1.0, ALU.mult, ALU.add))
            for j in range(16):
                dve.wait_ge(S["f_act"], j + 1)
                f, k = hf[:, j // 8, j % 8, :], hk[:, j // 8, j % 8, :]
                link(dve.tensor_scalar(f, k, e(5)[:, j:j + 1], e(4)[:, j:j + 1], ALU.mult, ALU.add))
                dve.tensor_scalar(k, f, -1.0, 1.0, ALU.mult, ALU.add).then_inc(S["k_ready"], 1)
            dve.wait_ge(S["hmask_set"], 2)
            for j in range(16):
                dve.wait_ge(S["f_ln"], j // 8 + 1)
                f = hf[:, j // 8, j % 8, :]
                f = f[:, ::-1] if j >= 8 else f
                dve.tensor_tensor_scan(f, hmask[:, :], f, 0.0, ALU.mult, ALU.add).then_inc(S["scan_ready"], 1)
            dve.wait_ge(S["scan_ready"], 16)
            dve.wait_ge(S["hgrn_in"], 32)
            dve.wait_ge(S["q_evac"], 8)
            for h in range(HH):
                for j in range(4):
                    n, (t, d) = 4 * h + j, STATES[j]
                    dve.wait_ge(S["kh_exp"], n + 1)
                    dve.tensor_tensor(hkh[:, n % 2, :], hkh[:, n % 2, :], hk[:, d, h, toks(t)], ALU.mult).then_inc(S["kh_ready"], 1)
                    dve.wait_ge(S["khT_done"], n + 1)
                    if n >= 2:
                        dve.wait_ge(S["hst_done"], n - 1)
                    dve.tensor_copy(hkt[:, n % 2, :], ps[:, 4 + n % 2, 0:P]).then_inc(S["khT_read"], 1)
                if h:
                    dve.wait_ge(S["o_done"], h)
                for j in (2, 3):
                    t, d = STATES[j]
                    last = t * P + (P - 1 if d == 0 else 0)
                    dve.wait_ge(S["edec_ready"], 2 * h + j - 1)
                    dve.wait_ge(S["hst_done"], 4 * h + j + 1)
                    dve.scalar_tensor_tensor(out=hs1[:, d, :], in0=hs0[:, d, h, :], scalar=hed[:, d:d + 1], in1=ps[:, 6 + j % 2, 0:P],
                                             op0=ALU.mult, op1=ALU.add).then_inc(S["hs1_ready"], 1)
                kf, kb, q = hk[:, 0, h, :], hk[:, 1, h, :], hq[:, h, :]

                def halves(a, j):
                    return a.rearrange("p (b two n) -> p b two n", two=2, n=1 << j)

                def differences(j):
                    n, hw = LEVELS * h + j, 1 << j
                    F, G = halves(hf[:, 0, h, :], j), halves(hf[:, 1, h, :], j)
                    U, W = halves(uw[:, (j + 1) % 2, 0, :], j), halves(uw[:, (j + 1) % 2, 1, :], j)
                    nb = T // (2 * hw)
                    rf = F[:, :, 0, hw - 1:hw].to_broadcast([P, nb, hw])
                    rg = G[:, :, 1, 0:1].to_broadcast([P, nb, hw])
                    if (LEVELS + 1) * h + j + 1 >= 2:
                        dve.wait_ge(S["lv_done"], (LEVELS + 1) * h + j)
                    dve.tensor_tensor(U[:, :, 0, :], rf, F[:, :, 0, :], ALU.subtract)
                    dve.tensor_tensor(U[:, :, 1, :], rg, G[:, :, 1, :], ALU.subtract)
                    dve.tensor_tensor(W[:, :, 1, :], F[:, :, 1, :], rf, ALU.subtract)
                    dve.tensor_tensor(W[:, :, 0, :], G[:, :, 0, :], rg, ALU.subtract).then_inc(S["u_sub"], 1)

                def keys_queries(j):
                    n = LEVELS * h + j
                    U, W = uw[:, (j + 1) % 2, 0, :], uw[:, (j + 1) % 2, 1, :]
                    dve.wait_ge(S["u_exp"], n + 1)
                    dve.tensor_tensor(halves(U, j)[:, :, 0, :], halves(U, j)[:, :, 0, :], halves(kf, j)[:, :, 0, :], ALU.mult)
                    dve.tensor_tensor(halves(U, j)[:, :, 1, :], halves(U, j)[:, :, 1, :], halves(kb, j)[:, :, 1, :], ALU.mult)
                    dve.tensor_tensor(W, W, q, ALU.mult).then_inc(S["uw_ready"], 1)

                a3 = att[:, :].rearrange("p (t n) -> p t n", t=NT)

                def pick(j):
                    n = (LEVELS + 1) * h + j
                    dve.wait_ge(S["lv_done"], n + 1)
                    dve.wait_ge(S["lv_read"], n)
                    src = bank(n % 2).rearrange("p (t n) -> p t n", t=NT)
                    if j == 0:
                        ins = dve.tensor_tensor(a3, src, ident[:, :].unsqueeze(1).to_broadcast([P, NT, P]), ALU.mult)
                    else:
                        ins = dve.copy_predicated(a3, lvl[:, j - 1, :].unsqueeze(1).to_broadcast([P, NT, P]), src)
                    ins.then_inc(S["lv_read"], 1)

                if h:
                    dve.wait_ge(S["lv_done"], (LEVELS + 1) * h)
                dve.tensor_tensor(uw[:, 0, 0, :], kf, kb, ALU.add).then_inc(S["uw_ready"], 1)
                differences(0)
                for j in range(LEVELS):
                    keys_queries(j)
                    pick(j)
                    if j + 1 < LEVELS:
                        differences(j + 1)
                pick(LEVELS)
            for h in range(HH):
                dve.wait_ge(S["hstd"], h + 1)
                if h:
                    dve.wait_ge(S["on_ready"], h)
                link(dve.reciprocal(hrs[:, :], hres[:, :]))
                dve.scalar_tensor_tensor(out=hq[:, h, :], in0=hq[:, h, :], scalar=c_("hng", 0), in1=hrs[:, :], op0=ALU.mult,
                                         op1=ALU.mult).then_inc(S["on_ready"], 1)
            dve.wait_ge(S["on_ready"], 8)
            for j in range(8):
                dve.wait_ge(S["hg_act"], j + 1)
                if j >= 2:
                    dve.wait_ge(S["hol_ready"], j - 1)
                dve.tensor_tensor(hon[:, j % 2, :], hq[:, j, :], hsg[:, j % 2, :], ALU.mult).then_inc(S["hon_ready"], 1)
            start_residual(2 * l)
            for m in range(KD):
                dve.wait_ge(S["sub_done"], sb((l, "out"), m + 1))
                residual(l, m, bank(m % 4), 16)

        def split_waits(eng, s0, shift):
            eng.wait_ge(raw_in[(s0 // 2) % RAW], 16 * (s0 // 8 + 1) + shift * 16)
            if not (isinstance(shift, int) and s0 - 3 + 8 * shift <= 0):
                eng.wait_ge(S["sub_done"], s0 - 3 + shift * 8)

        def raw_sub(s0):
            k = chunk_rows[s0 // 2]
            w = raw[:, (s0 // 2) % RAW, :].rearrange("p (k n) -> p k n", k=k)
            return w[:, (s0 % 2) * 8:(s0 % 2) * 8 + 8, :] if k == 16 else w[:, :, (s0 % 2) * (SUB // k):(s0 % 2 + 1) * (SUB // k)]

        def split_sub(w, s0):
            return w[:, s0 % SPL, :].rearrange("p (k n) -> p k n", k=min(chunk_rows[s0 // 2], KD))

        LN_LAST = 2 * DEPTH - 1

        @block.scalar
        def _(act):
            chain = Chain(act, S["act_step"])
            fed = [0, sb((0, "moe")) + 2]

            def high(s0, shift=0):
                split_waits(act, s0, shift)
                act.activation(split_sub(whi, s0), raw_sub(s0), ACT.Copy).then_inc(S["hi_ready"], 1)

            def feed(upto):
                while fed[0] <= min(upto, NSUB - 1, fed[1]):
                    high(fed[0])
                    fed[0] += 1

            def layer_norm(q, last=False):
                for j in range(4):
                    act.wait_ge(S["diff_ready"], 4 * q + j + 1)
                    act.activation(sq[:, 2 * j:2 * j + 2, :], y[:, 2 * j:2 * j + 2, :], ACT.Square).then_inc(S["sq_ready"], 1)
                act.wait_ge(S["var_done"], q + 1)
                act.activation(std[:, :], bank(5), ACT.Sqrt, bias=eps[:, 0:1]).then_inc(S["std_ready"], 1)
                l, w = q // 2, q % 2
                for k in range(KD):
                    act.wait_ge(S["norm_ready"], 8 * q + k + 1)
                    act.activation(x[:, k, :], y[:, k, :], ACT.Identity, scale=c_("lng", (2 * l + w) * 8 + k),
                                   bias=c_("lnb", (2 * l + w) * 8 + k)).then_inc(S["x_ready"], 1)
                    if not last:
                        act.wait_ge(S["h32_ready"], 8 * (q + 1) + k + 1)
                        act.activation(hh[:, k, :], h32[:, k, :], ACT.Copy).then_inc(S["hh_ready"], 1)

            def gmlp(l):
                u = l // 3
                for c in range(8):
                    s = sb((l, "v"), 2 * c)
                    feed(s + 3)
                    act.wait_ge(S["sub_done"], s + 2)
                    for t in range(NT):
                        ins = act.activation(gv[:, t, c * 256:(c + 1) * 256], ps[:, 3 * (c % 2) + t, 0:256], ACT.Gelu)
                    ins.then_inc(S["v_evac"], 1)
                for t in range(NT):
                    act.wait_ge(S["gstat_done"], 3 * u + t + 1)
                    act.activation(grs[:, t, 0:1], gmv[:, t, 1:2], ACT.Sqrt, bias=eps[:, 0:1]).then_inc(S["gstd_done"], 1)

                def product_high(j):
                    act.wait_ge(S["s32_ready"], 16 * u + j + 1)
                    act.activation(gsh[:, j, :], gs32[:, j % 2, :], ACT.Copy).then_inc(S["sh_ready"], 1)

                for j in range(16):
                    s = sb((l, "u"), j)
                    feed(s + 3)
                    act.wait_ge(S["sub_done"], s + 1)
                    if j >= 4:
                        act.wait_ge(S["s32_ready"], 16 * u + j - 3)
                    act.activation(gu[:, j % 4, :], bank(j % 4), ACT.Gelu).then_inc(S["u_evac"], 1)
                    if j >= 3:
                        product_high(j - 3)
                for j in range(13, 16):
                    feed(sb((l, "out")) + 3)
                    product_high(j)
                for m in range(8):
                    feed(sb((l, "out"), 2 * m + 2) + 3)

            def experts(l):
                more = l + 1 < DEPTH
                nm = MOE_MODS // MOE_ITERS if more else 0
                order = moe_order(nm)
                nb = 2 * len(order)
                s_moe = sb((l, "moe"))
                feed(s_moe + 2)
                act.wait_ge(S["router_done"], l + 1)
                act.activation(rt[:, 0, :, :].rearrange("p t e -> p (t e)"), ps[:, 4, 0:NT * NE],
                               ACT.Sigmoid).then_inc(S["route_ready"], 1)
                for t in range(NT):
                    for b in range(4):
                        act.wait_ge(S["cwb_done"], 12 * l + 4 * t + b + 1)
                        act.activation(cwb[:, 4 * b:4 * b + 4, t * P:(t + 1) * P],
                                       ps[:, b, :].rearrange("p (e n) -> p e n", e=4), ACT.Copy).then_inc(S["cwb_read"], 1)

                def step(i, static):
                    e0 = 16 * l + i * EG
                    for p, (what, e) in enumerate(order):
                        for j in range(2):
                            s0 = s_moe + 2 * p + j
                            if static:
                                feed(s0 + nb * i + 3)
                            else:
                                high(s0 + 3, i * (nb // 8))
                            if what == "G":
                                act.wait_ge(S["sub_done"], s0 + 1 + i * nb)
                                act.activation(sg[:, e % 2, j, :], bank(j), ACT.Silu).then_inc(S["gate_read"], 1)
                            if (what == "G" and e >= 1 and j == 1) or (what == "D" and e == 2 and j == 1):
                                f = e - 1 if what == "G" else 3
                                act.wait_ge(S["e32_ready"], e0 + f + 1)
                                act.activation(eh[:, f % 2, :, :], e32[:, f % 2, :, :], ACT.Copy).then_inc(S["eh_ready"], 1)
                with act.Fori(0, MOE_ITERS - 1) as i:
                    step(i, False)
                fed[:] = s_moe + nb * (MOE_ITERS - 1) + 3, sb((l + 1, "moe")) + 2 if more else NSUB - 1
                step(MOE_ITERS - 1, True)

            act.wait_ge(S["cols_in"], 16)
            chain.link(act.activation(condf[:, :, :].rearrange("p k c -> p (k c)"), c_("cond", 0, 16), ACT.Silu))
            act.activation(cond[:, :, 0:2], condf[:, :, :], ACT.Copy).then_inc(S["cond_ready"], 1)
            feed(sb("mod0", 2 * MODC) + 2)
            for k in range(KD):
                act.wait_ge(S["h32_ready"], k + 1)
                act.activation(hh[:, k, :], h32[:, k, :], ACT.Copy).then_inc(S["hh_ready"], 1)
            act.wait_ge(S["router_in"], 16)
            act.activation(wrh[:, :, :], wrt[:, :, :], ACT.Copy).then_inc(S["router_split"], 1)
            for l in range(DEPTH):
                if l % 3 == 0:
                    gmlp(l)
                elif l % 3 == 1:
                    act_ssd(act, l, feed)
                else:
                    act_hgrn(act, l, feed)
                feed(sb((l, "ln1")) + 3)
                layer_norm(2 * l)
                experts(l)
                feed(sb((l, "ln2")) + 3)
                layer_norm(2 * l + 1, last=(2 * l + 1 == LN_LAST))
    
        @block.gpsimd
        def _(pool):
            chain = Chain(pool, S["pool_step"])
            fed = [0, sb((0, "moe")) + 2]

            def low(s0, shift=0):
                pool.wait_ge(S["hi_ready"], s0 + 1 + shift * 8)
                pool.tensor_tensor(split_sub(wlo, s0), raw_sub(s0), split_sub(whi, s0).bitcast(F32),
                                   ALU.subtract).then_inc(S["lo_ready"], 1)

            def feed(upto):
                while fed[0] <= min(upto, NSUB - 1, fed[1]):
                    low(fed[0])
                    fed[0] += 1

            def hidden_low(n):
                for k in range(KD):
                    pool.wait_ge(S["hh_ready"], 8 * n + k + 1)
                    pool.tensor_tensor(hl[:, k, :], h32[:, k, :], hh[:, k, :].bitcast(F32),
                                       ALU.subtract).then_inc(S["hl_ready"], 1)

            def gmlp(l):
                u = l // 3
                for j in range(16):
                    feed(min(sb((l, "u"), j) + 6, sb((l, "out")) + 3))
                    pool.wait_ge(S["sh_ready"], 16 * u + j + 1)
                    pool.tensor_tensor(gsl[:, j, :], gs32[:, j % 2, :], gsh[:, j, :].bitcast(F32),
                                       ALU.subtract).then_inc(S["sl_ready"], 1)

            def experts(l):
                more = l + 1 < DEPTH
                nm = MOE_MODS // MOE_ITERS if more else 0
                order = moe_order(nm)
                nb = 2 * len(order)
                s_moe = sb((l, "moe"))
                feed(s_moe + 2)

                def step(i, static):
                    e0 = 16 * l + i * EG
                    for p, (what, e) in enumerate(order):
                        for j in range(2):
                            s0 = s_moe + 2 * p + j
                            if static:
                                feed(s0 + nb * i + 3)
                            else:
                                low(s0 + 3, i * (nb // 8))
                            if (what == "G" and e >= 1 and j == 1) or (what == "D" and e == 2 and j == 1):
                                f = e - 1 if what == "G" else 3
                                pool.wait_ge(S["eh_ready"], e0 + f + 1)
                                pool.tensor_tensor(el[:, f % 2, :, :], e32[:, f % 2, :, :],
                                                   eh[:, f % 2, :, :].bitcast(F32), ALU.subtract).then_inc(S["el_ready"], 1)
                with pool.Fori(0, MOE_ITERS - 1) as i:
                    step(i, False)
                fed[:] = s_moe + nb * (MOE_ITERS - 1) + 3, sb((l + 1, "moe")) + 2 if more else NSUB - 1
                step(MOE_ITERS - 1, True)

            pool.memset(ones[:, :], 1.0)
            pool.memset(mean_d[:, :], 1.0 / D)
            pool.memset(eps[:, :], EPS).then_inc(S["consts_set"], 1)
            feed(sb("mod0", 2 * MODC) + 2)
            hidden_low(0)
            pool.wait_ge(S["router_split"], 1)
            pool.tensor_tensor(wrl[:, :, :], wrt[:, :, :], wrh[:, :, :].bitcast(F32), ALU.subtract).then_inc(S["router_split"], 1)
            for l in range(DEPTH):
                if l % 3 == 0:
                    gmlp(l)
                elif l % 3 == 1:
                    pool_ssd(pool, l, feed)
                else:
                    pool_hgrn(pool, l, feed)
                feed(sb((l, "ln1")) + 3)
                hidden_low(2 * l + 1)
                experts(l)
                feed(sb((l, "ln2")) + 3)
                if 2 * l + 1 < LN_LAST:
                    hidden_low(2 * l + 2)
    
        @block.tensor
        def _(pe):
            release = {}

            def claim(b, name, value):
                if b in release:
                    pe.wait_ge(*release[b])
                release[b] = (S[name], value)

            def product(out, lhi, llo, rhi, rlo, first, last):
                pe.matmul(out, lhi, rhi, start=first, stop=False)
                pe.matmul(out, lhi, rlo, start=False, stop=False)
                return pe.matmul(out, llo, rhi, start=False, stop=last)

            def full(s0, out, rhi, rlo, k0=0, first=True, last=True, count=1):
                for k in range(KD):
                    w = slice(k * P, (k + 1) * P)
                    ins = product(out, whi[:, s0 % SPL, w], wlo[:, s0 % SPL, w], rhi[:, k0 + k, :], rlo[:, k0 + k, :],
                                  first and k == 0, last and k == KD - 1)
                ins.then_inc(S["sub_done"], count)

            def by_token(s0, outs):
                pair = lambda w, k: w[:, s0 % SPL:s0 % SPL + 2, k * P:(k + 1) * P]
                outs = [o.rearrange("p (a n) -> p a n", a=2) for o in outs]
                for t in range(NT):
                    for k in range(KD):
                        tk = slice(t * P, (t + 1) * P)
                        pe.matmul(outs[t], hh[:, k, tk], pair(whi, k), start=(k == 0), stop=False)
                        pe.matmul(outs[t], hl[:, k, tk], pair(whi, k), start=False, stop=False)
                        ins = pe.matmul(outs[t], hh[:, k, tk], pair(wlo, k), start=False, stop=(k == KD - 1))
                ins.then_inc(S["sub_done"], 2)

            def modulation(s0, n, batch, shift_s=0, shift_b=0):
                if not isinstance(shift_b, int) or batch:
                    pe.wait_ge(S["mod_read"], batch + shift_b)
                for j in range(2 * n):
                    pe.wait_ge(S["lo_ready"], s0 + j + 1 + shift_s)
                    c = 4 * j
                    for k in range(KD):
                        w = slice(k * P, (k + 1) * P)
                        both = [(4, whi), (2, wlo)]
                        for m, part in both[::-1] if k == KD - 1 else both:
                            ins = pe.matmul(ps[:, 7, c:c + m], part[:, (s0 + j) % SPL, w], cond[:, k, 0:m],
                                            start=(k == 0 and m == 4), stop=(k == KD - 1 and m == 4), skip_group_check=True)
                    ins.then_inc(S["sub_done"], 1)

            def mean_step(q, k):
                pe.wait_ge(S["y_ready"], 8 * q + k + 1)
                if k == 0:
                    claim(6, "diff_ready", 4 * q + 4)
                ins = pe.matmul(bank(6), mean_d[:, :], y[:, k, :], start=(k == 0), stop=(k == KD - 1))
                if k == KD - 1:
                    ins.then_inc(S["mean_done"], 1)

            def variance(q):
                claim(5, "std_ready", q + 1)
                for k in range(KD):
                    pe.wait_ge(S["sq_ready"], 4 * q + k // 2 + 1)
                    ins = pe.matmul(bank(5), mean_d[:, :], sq[:, k, :], start=(k == 0), stop=(k == KD - 1))
                ins.then_inc(S["var_done"], 1)

            def out_tiles(l, rhi, rlo, halves):
                q = 2 * l
                for m in range(KD):
                    claim(m % 4, "y_ready", 8 * q + m + 1)
                    for h in range(halves):
                        s = sb((l, "out"), halves * m + h)
                        pe.wait_ge(S["lo_ready"], s + 1)
                        full(s, bank(m % 4), rhi, rlo, 8 * h, h == 0, h == halves - 1)
                    if m:
                        mean_step(q, m - 1)
                mean_step(q, KD - 1)

            def gmlp(l):
                u = l // 3
                for k in range(KD):
                    pe.wait_ge(S["hl_ready"], 8 * (2 * l) + k + 1)
                for c in range(8):
                    s = sb((l, "v"), 2 * c)
                    pe.wait_ge(S["lo_ready"], s + 2)
                    for t in range(NT):
                        claim(3 * (c % 2) + t, "v_evac", 8 * u + c + 1)
                    by_token(s, [ps[:, 3 * (c % 2) + t, 0:256] for t in range(NT)])

                def mix(j):
                    pe.wait_ge(S["v_norm"], 3 * u + 3)
                    claim(4 + j % 2, "a_ready", 16 * u + j + 1)
                    for t in range(NT):
                        ins = pe.matmul(ps[:, 4 + j % 2, t * P:(t + 1) * P], gv[:, t, j * P:(j + 1) * P], gws[:, j // 2, :],
                                        start=True, stop=True)
                    ins.then_inc(S["mix_done"], 1)

                for j in range(16):
                    s = sb((l, "u"), j)
                    pe.wait_ge(S["lo_ready"], s + 1)
                    claim(j % 4, "u_evac", 16 * u + j + 1)
                    full(s, bank(j % 4), hh, hl)
                    if j == 0:
                        pe.wait_ge(S["gmlp_in"], 32 * (u + 1))
                        for h in range(2):
                            claim(6 + h, "rows_read", 2 * u + h + 1)
                            if h:
                                pe.wait_ge(S["mod_read"], mods_before(l))
                            pe.matmul(ps[:, 6 + h, :], ones[:, :], gws[:, 4 * h:4 * h + 4, :],
                                      start=True, stop=True).then_inc(S["rows_done"], 1)
                    if j % 2 and j >= 3:
                        mix(j - 3)
                        mix(j - 2)
                mix(14)
                mix(15)
                pe.wait_ge(S["rows_read"], 2 * u + 2)
                pe.wait_ge(S["sl_ready"], 16 * u + 16)
                out_tiles(l, gsh, gsl, 2)

            def experts(l):
                more = l + 1 < DEPTH
                nm = MOE_MODS // MOE_ITERS if more else 0
                order = moe_order(nm)
                nb = 2 * len(order)
                for k in range(KD):
                    pe.wait_ge(S["hl_ready"], 8 * (2 * l + 1) + k + 1)
                pe.wait_ge(S["router_split"], 2)
                claim(4, "route_ready", l + 1)
                for t in range(NT):
                    tk = slice(t * P, (t + 1) * P)
                    for k in range(KD):
                        ins = product(ps[:, 4, t * NE:(t + 1) * NE], hh[:, k, tk], hl[:, k, tk], wrh[:, k, :], wrl[:, k, :],
                                      k == 0, k == KD - 1)
                ins.then_inc(S["router_done"], 1)
                if more:
                    modulation(sb((l, "router")), ROUTER_MODS, mods_before(l) + 1)
                for t in range(NT):
                    pe.wait_ge(S["cw_ready"], 3 * l + t + 1)
                    for b in range(4):
                        claim(b, "cwb_read", 12 * l + 4 * t + b + 1)
                        pe.matmul(ps[:, b, :], ones[:, :], diag[:, 4 * b:4 * b + 4, :], start=True,
                                  stop=True).then_inc(S["cwb_done"], 1)
                for b in range(4):
                    pe.wait_ge(*release[b])
                for b in (4, 5, 6):
                    if b in release:
                        pe.wait_ge(*release[b])
                s_moe = sb((l, "moe"))
                with pe.Fori(0, MOE_ITERS) as i:
                    for p, (what, e) in enumerate(order):
                        s0 = s_moe + 2 * p
                        if what == "M":
                            if e == 0:
                                modulation(s0, nm, mods_before(l) + 2, i * nb, i)
                            continue
                        if what == "G":
                            pe.wait_ge(S["gate_read"], (16 * l + e) * 2 + i * 8)
                        if what == "U":
                            pe.wait_ge(S["up_read"], 16 * l + e + i * EG)
                        if what == "D":
                            pe.wait_ge(S["el_ready"], 16 * l + e + 1 + i * EG)
                        for j in range(2):
                            pe.wait_ge(S["lo_ready"], s0 + j + 1 + i * nb)
                            if what in "GU":
                                full(s0 + j, bank((what == "U") * 2 + j), hh, hl)
                                continue
                            for m in range(4):
                                d = 4 * j + m
                                pe.wait_ge(S["down_added"], 128 * l + 8 * e + (d - 2 if d >= 3 else 0) + i * 32)
                                for k in range(2):
                                    w = slice(k * 512 + m * P, k * 512 + (m + 1) * P)
                                    ins = product(bank(4 + d % 3), whi[:, (s0 + j) % SPL, w], wlo[:, (s0 + j) % SPL, w],
                                                  eh[:, e % 2, k, :], el[:, e % 2, k, :], k == 0, k == 1)
                                ins.then_inc(S["down_done" if m < 3 else "sub_done"], 1)
                q = 2 * l + 1
                for b in (0, 1):
                    release[b] = (S["gate_read"], 32 * (l + 1))
                for b in (2, 3):
                    release[b] = (S["up_read"], 16 * (l + 1))
                for b in (4, 5, 6):
                    release[b] = (S["down_added"], 128 * (l + 1))
                for k in range(KD):
                    mean_step(q, k)

            pe.wait_ge(S["cond_ready"], 2)
            for j in range(0, MODC, 4):
                modulation(sb("mod0", 2 * j), 4, j // 4)
            pe.wait_ge(S["consts_set"], 1)
            for l in range(DEPTH):
                if l % 3 == 0:
                    gmlp(l)
                elif l % 3 == 1:
                    pe_ssd(pe, l, claim, release, full, by_token, out_tiles)
                else:
                    pe_hgrn(pe, l, claim, release, full, by_token, out_tiles)
                variance(2 * l)
                if l + 1 < DEPTH:
                    modulation(sb((l, "ln1")), LN1_MODS, mods_before(l))
                experts(l)
                variance(2 * l + 1)
                if l + 1 < DEPTH:
                    modulation(sb((l, "ln2")), LN2_MODS, mods_before(l + 1) - 1)

        @block.vector
        def _(dve):
            chain = Chain(dve, S["dve_step"])
            link = chain.link

            def mod_tiles(l, q, n, s0, shift_s=0, shift_q=0):
                dve.wait_ge(S["sub_done"], s0 + 2 * n + shift_s)
                v = ps[:, 7, 0:8 * n].rearrange("p (j c) -> p j c", c=4)
                if isinstance(shift_q, int):
                    b = c_("bmod", 48 * l + 2 * q, 2 * n)
                    dst = mods[:, l % 2, 2 * q:2 * q + 2 * n, :]
                else:
                    b = cols[:, bass.ds(COL["bmod"] + 48 * l + 2 * q + shift_q * 2, 2 * n)]
                    dst = mods[:, l % 2, bass.ds(2 * q + shift_q * 2, 2 * n), :]
                link(dve.tensor_tensor(modt[:, 0:2 * n, :], v[:, :, 0:2], b.unsqueeze(2).to_broadcast([P, 2 * n, 2]), ALU.add))
                dve.tensor_tensor(dst, v[:, :, 2:4], modt[:, 0:2 * n, :], ALU.add).then_inc(S["mod_read"], 1)

            def prepare_scale(l, which):
                par, sc, sh = (l % 2, 32, 24) if which == 0 else ((l + 1) % 2, 8, 0)
                dve.wait_ge(S["mod_read"], mods_before(l) if which == 0 else mods_before(l + 1) - LN2_MODS)
                g = c_("lng", (2 * l + which) * 8, 8).unsqueeze(2).to_broadcast([P, KD, 2])
                b = c_("lnb", (2 * l + which) * 8, 8).unsqueeze(2).to_broadcast([P, KD, 2])
                link(dve.tensor_scalar(cmod[:, 0, :, :], mods[:, par, sc:sc + 8, :], 1.0, None, ALU.add))
                link(dve.tensor_tensor(cmod[:, 1, :, :], cmod[:, 0, :, :], b, ALU.mult))
                link(dve.tensor_tensor(cmod[:, 1, :, :], cmod[:, 1, :, :], mods[:, par, sh:sh + 8, :], ALU.add))
                link(dve.tensor_tensor(cmod[:, 0, :, :], cmod[:, 0, :, :], g, ALU.mult))

            def modulate(src, k):
                for c, a, b in SEGS:
                    ins = dve.tensor_scalar(h32[:, k, a:b], src[:, k, a:b], cmod[:, 0, k, c:c + 1], cmod[:, 1, k, c:c + 1],
                                            ALU.mult, ALU.add)
                ins.then_inc(S["h32_ready"], 1)

            def layer_norm(q, fill, last=False):
                l = q // 2
                if not last:
                    prepare_scale(l, q % 2)
                dve.wait_ge(S["mean_done"], q + 1)
                for j in range(4):
                    dve.tensor_tensor(y[:, 2 * j:2 * j + 2, :], y[:, 2 * j:2 * j + 2, :],
                                      bank(6).unsqueeze(1).to_broadcast([P, 2, T]), ALU.subtract).then_inc(S["diff_ready"], 1)
                dve.wait_ge(S["std_ready"], q + 1)
                link(dve.reciprocal(rstd[:, :], std[:, :]))
                for k in range(KD):
                    dve.tensor_tensor(y[:, k, :], y[:, k, :], rstd[:, :], ALU.mult).then_inc(S["norm_ready"], 1)
                    if not last:
                        dve.wait_ge(S["norm_ready"], 8 * q + k + 1)
                        modulate(y, k)
                if fill:
                    mod_tiles(*fill)

            def start_residual(q):
                dve.wait_ge(S["x_ready"], 8 * (q + 1))
                dve.wait_ge(S["mod_read"], mods_before(q // 2))
                link(dve.tensor_scalar(y[:, :, :], x[:, :, :], ALPHA, None, ALU.mult))

            def residual(l, m, src, g_tile):
                for c, a, b in SEGS:
                    ins = dve.scalar_tensor_tensor(out=y[:, m, a:b], in0=src[:, a:b], scalar=mods[:, l % 2, g_tile + m, c:c + 1],
                                                   in1=y[:, m, a:b], op0=ALU.mult, op1=ALU.add)
                ins.then_inc(S["y_ready"], 1)

            def gmlp(l):
                u = l // 3
                for t in range(NT):
                    dve.wait_ge(S["v_evac"], 8 * u + 8)
                    for c in range(4):
                        ins = dve.bn_stats(gst[:, t, c, :], gv[:, t, c * 512:(c + 1) * 512])
                    link(ins)
                    dve.bn_aggr(gmv[:, t, :], gst[:, t, :, :]).then_inc(S["gstat_done"], 1)
                for t in range(NT):
                    dve.wait_ge(S["gstd_done"], 3 * u + t + 1)
                    link(dve.reciprocal(grs[:, t, 1:2], grs[:, t, 0:1]))
                    dve.tensor_scalar(gv[:, t, :], gv[:, t, :], gmv[:, t, 0:1], grs[:, t, 1:2], ALU.subtract,
                                      ALU.mult).then_inc(S["v_norm"], 1)
                for h in range(2):
                    dve.wait_ge(S["rows_done"], 2 * u + h + 1)
                    dve.tensor_copy(grow[:, 4 * h:4 * h + 4, :].rearrange("p a b -> p (a b)"), ps[:, 6 + h, :]).then_inc(S["rows_read"], 1)
                dve.wait_ge(S["gmlp_in"], 32 * (u + 1))
                dve.wait_ge(S["rows_read"], 2 * u + 2)
                for j in range(16):
                    h = j // 2
                    link(dve.scalar_tensor_tensor(out=gct[:, j % 2, :], in0=grow[:, h, :], scalar=c_("glnb", 16 * u + j),
                                                  in1=gbs[:, h, :], op0=ALU.mult, op1=ALU.add))
                    dve.wait_ge(S["mix_done"], 16 * u + j + 1)
                    dve.scalar_tensor_tensor(out=gat[:, :].rearrange("p (t n) -> p t n", t=NT),
                                             in0=bank(4 + j % 2).rearrange("p (t n) -> p t n", t=NT),
                                             scalar=c_("glng", 16 * u + j),
                                             in1=gct[:, j % 2, :].unsqueeze(1).to_broadcast([P, NT, P]),
                                             op0=ALU.mult, op1=ALU.add).then_inc(S["a_ready"], 1)
                    dve.wait_ge(S["a_ready"], 16 * u + j + 1)
                    dve.wait_ge(S["u_evac"], 16 * u + j + 1)
                    if j >= 2:
                        dve.wait_ge(S["sl_ready"], 16 * u + j - 1)
                    dve.tensor_tensor(gs32[:, j % 2, :], gat[:, :], gu[:, j % 4, :], ALU.mult).then_inc(S["s32_ready"], 1)
                dve.wait_ge(S["sl_ready"], 16 * u + 16)
                start_residual(2 * l)
                for m in range(KD):
                    dve.wait_ge(S["sub_done"], sb((l, "out"), 2 * m + 2))
                    residual(l, m, bank(m % 4), 16)

            def route(l):
                v = lambda n: rt[:, n, :, :]
                g4 = lambda n: rt[:, n, :, 0:NG]
                one = lambda n: rt[:, n, :, 0]
                flat = lambda n: rt[:, n, :, :].rearrange("p t (g e) -> p (t g) e", e=EG)
                pairs = rt[:, 2:4, :, :].rearrange("p a t e -> p (a t e)")[:, 0:72].rearrange("p (g e) -> p g e", e=6)
                dve.wait_ge(S["route_ready"], l + 1)
                link(dve.tensor_tensor(v(1), v(0), c_("brout", 0, 16).unsqueeze(1).to_broadcast([P, NT, NE]), ALU.add))
                dve.tensor_tensor(pairs[:, :, 0:3], flat(1)[:, :, 0:3], flat(1)[:, :, 1:4], ALU.add)
                dve.tensor_tensor(pairs[:, :, 3:5], flat(1)[:, :, 0:2], flat(1)[:, :, 2:4], ALU.add)
                link(dve.tensor_tensor(pairs[:, :, 5:6], flat(1)[:, :, 0:1], flat(1)[:, :, 3:4], ALU.add))
                link(dve.tensor_reduce(rt[:, 4, :, 0:NG], pairs.rearrange("p (t g) e -> p t g e", g=NG), AX.X, ALU.max))

                def first_max(src, tmp, key, n, out):
                    wide = lambda a: a.unsqueeze(2).to_broadcast([P, NT, n])
                    link(dve.tensor_reduce(one(tmp), src, AX.X, ALU.max))
                    link(dve.tensor_tensor(out, src, wide(one(tmp)), ALU.is_equal))
                    link(dve.tensor_tensor(out, out, c_(key, 0, n).unsqueeze(1).to_broadcast([P, NT, n]), ALU.mult))
                    link(dve.tensor_reduce(one(tmp), out, AX.X, ALU.max))
                    link(dve.tensor_tensor(out, out, wide(one(tmp)), ALU.is_equal))

                first_max(g4(4), 5, "gkey", NG, g4(6))
                ing = g4(6).unsqueeze(3).to_broadcast([P, NT, NG, EG])
                e4 = lambda n: rt[:, n, :, :].rearrange("p t (g e) -> p t g e", e=EG)
                link(dve.tensor_tensor(e4(7), e4(1), ing, ALU.mult))
                link(dve.tensor_scalar(g4(8), g4(6), -1.0, BIG, ALU.add, ALU.mult))
                link(dve.tensor_tensor(e4(7), e4(7), g4(8).unsqueeze(3).to_broadcast([P, NT, NG, EG]), ALU.add))
                first_max(v(7), 5, "ekey", NE, v(9))
                link(dve.scalar_tensor_tensor(out=v(7), in0=v(9), scalar=-3 * BIG, in1=v(7), op0=ALU.mult, op1=ALU.add))
                first_max(v(7), 5, "ekey", NE, v(10))
                link(dve.tensor_tensor(v(9), v(9), v(10), ALU.add))
                link(dve.tensor_tensor(v(9), v(9), v(0), ALU.mult))
                link(dve.tensor_reduce(one(5), v(9), AX.X, ALU.add))
                link(dve.reciprocal(one(11), one(5)))
                link(dve.tensor_tensor(v(12), v(9), one(11).unsqueeze(2).to_broadcast([P, NT, NE]), ALU.mult))
                for t in range(NT):
                    if t:
                        dve.wait_ge(S["cwb_done"], 12 * l + 4 * t)
                    dve.tensor_tensor(diag[:, :, :], ident[:, :].unsqueeze(1).to_broadcast([P, NE, P]),
                                      rt[:, 12, t, :].unsqueeze(2).to_broadcast([P, NE, P]), ALU.mult).then_inc(S["cw_ready"], 1)

            def experts(l):
                more = l + 1 < DEPTH
                nm = MOE_MODS // MOE_ITERS if more else 0
                order = moe_order(nm)
                nb = 2 * len(order)
                s_moe = sb((l, "moe"))
                link(dve.memset(acc[:, :, :], 0.0))
                route(l)
                start_residual(2 * l + 1)
                if more:
                    mod_tiles(l + 1, LN1_MODS, ROUTER_MODS, sb((l, "router")))
                per = 1 if more else 0
                dve.wait_ge(S["cwb_read"], 12 * (l + 1))
                with chain.loop(0, MOE_ITERS, per) as i:
                    for p, (what, e) in enumerate(order):
                        s0 = s_moe + 2 * p
                        if what == "M":
                            if e == 0:
                                mod_tiles(l + 1, LN1_MODS + ROUTER_MODS, nm, s0, i * nb, i * nm)
                        elif what == "U":
                            dve.wait_ge(S["gate_read"], (16 * l + e + 1) * 2 + i * 8)
                            dve.wait_ge(S["sub_done"], s0 + 2 + i * nb)
                            dve.wait_ge(S["e32_ready"], 16 * l + e + i * EG)
                            dve.tensor_tensor(et[:, :, :], ps[:, 2:4, 0:T], sg[:, e % 2, :, :], ALU.mult).then_inc(S["up_read"], 1)
                            dve.wait_ge(S["up_read"], 16 * l + e + 1 + i * EG)
                            dve.tensor_tensor(e32[:, e % 2, :, :], et[:, :, :],
                                              cwb[:, bass.ds(e + i * EG, 1), :].to_broadcast([P, 2, T]),
                                              ALU.mult).then_inc(S["e32_ready"], 1)
                        elif what == "D":
                            for d in range(8):
                                if d % 4 < 3:
                                    dve.wait_ge(S["down_done"], 96 * l + 6 * e + 3 * (d // 4) + d % 4 + 1 + i * 24)
                                else:
                                    dve.wait_ge(S["sub_done"], s0 + d // 4 + 1 + i * nb)
                                dve.tensor_tensor(acc[:, d, :], bank(4 + d % 3), acc[:, d, :], ALU.add).then_inc(S["down_added"], 1)
                dve.wait_ge(S["down_added"], 128 * (l + 1))
                for m in range(KD):
                    residual(l, m, acc[:, m, :], 40)

            dve.wait_ge(S["cond_ready"], 1)
            dve.tensor_tensor(cond[:, :, 2:4], condf[:, :, :], cond[:, :, 0:2].bitcast(F32), ALU.subtract).then_inc(S["cond_ready"], 1)
            for j in range(0, MODC, 4):
                mod_tiles(0, j, 4, sb("mod0", 2 * j))
            dve.wait_ge(S["mod_read"], mods_before(0))
            dve.wait_ge(S["x_in"], 48)
            dve.tensor_tensor(x[:, :, LC:T], x[:, :, LC:T], h32[:, :, 0:LS], ALU.add).then_inc(S["x_ready"], 8)
            dve.wait_ge(S["x_ready"], 8)
            link(dve.tensor_scalar(cmod[:, 0, :, :], mods[:, 0, 8:16, :], 1.0, None, ALU.add))
            link(dve.tensor_copy(cmod[:, 1, :, :], mods[:, 0, 0:8, :]))
            for k in range(KD):
                modulate(x, k)
            for l in range(DEPTH):
                if l % 3 == 0:
                    gmlp(l)
                elif l % 3 == 1:
                    dve_ssd(dve, l, link, start_residual, residual)
                else:
                    dve_hgrn(dve, l, link, start_residual, residual)
                more = l + 1 < DEPTH
                layer_norm(2 * l, (l + 1, 0, LN1_MODS, sb((l, "ln1"))) if more else None)
                experts(l)
                layer_norm(2 * l + 1, (l + 1, MODC - LN2_MODS, LN2_MODS, sb((l, "ln2"))) if more else None,
                           2 * l + 1 == LN_LAST)




def masks():
    i = np.arange(P)
    le = (i[:, None] <= i[None, :]).astype(np.float32)
    ge = (i[:, None] >= i[None, :]).astype(np.float32)
    lim = lambda m: np.where(m > 0, 0.0, -BIG).astype(np.float32)
    levels = np.zeros((P, LEVELS, P), np.uint32)
    for j in range(LEVELS):
        h = 1 << j
        same = (i[:, None] // (2 * h)) == (i[None, :] // (2 * h))
        other = (i[:, None] // h) != (i[None, :] // h)
        levels[:, j, :] = same & other
    return np.concatenate([np.eye(P, dtype=np.float32), le, ge, lim(le), lim(ge)], 1), levels


def positions():
    grid_w, quarter = 64, D // 4
    rows = LS // grid_w
    freq = np.exp(-math.log(10000.0) / quarter * np.arange(quarter, dtype=np.float32)).astype(np.float32)
    r = np.repeat(np.arange(rows, dtype=np.float32), grid_w)
    col = np.tile(np.arange(grid_w, dtype=np.float32), rows)
    ar, ac = r[:, None] * freq[None, :], col[:, None] * freq[None, :]
    pos = np.concatenate([np.sin(ar), np.cos(ar), np.sin(ac), np.cos(ac)], -1).astype(np.float32)
    return np.ascontiguousarray(pos.T.reshape(KD, P, LS).transpose(1, 0, 2))


def kernel(**inputs):
    import concourse.bacc as _bacc
    from concourse.bass_utils import run_bass_kernel_spmd as _run

    f = {k: np.asarray(v) for k, v in inputs.items()}
    tiles = lambda a: a.reshape(-1, P).T
    wide = lambda a: np.broadcast_to(a.reshape(1, -1), (P, a.size))
    gkey = np.arange(NG, 0, -1, dtype=np.float32)
    ekey = np.arange(NE, 0, -1, dtype=np.float32)
    cond = np.stack([f["c_ctx"].reshape(KD, P), f["c"].reshape(KD, P)], 1)
    columns = [tiles(f["b_mod"]), tiles(f["ln_g"]), tiles(f["ln_b"]), tiles(f["gmlp_ln_g"]), tiles(f["gmlp_ln_b"]),
               tiles(f["ssd_conv_w"]), tiles(f["ssd_conv_b"]), tiles(np.repeat(f["ssd_d_skip"], SP_, 1)),
               tiles(f["ssd_norm_g"]), tiles(f["hgrn_lb_logits"]), tiles(f["hgrn_norm_g"]), tiles(cond),
               wide(f["ssd_dt_bias"]), wide(f["ssd_a_log"]), wide(f["moe_b_router"]), wide(gkey), wide(ekey)]
    tok = np.concatenate([f["x_prompt"][0], f["x_sample"][0]], 0)
    mask, levels = masks()
    arrays = {
        "cols": np.ascontiguousarray(np.concatenate(columns, 1)),
        "x_t": np.ascontiguousarray(tok.T.reshape(KD, P, T).transpose(1, 0, 2)),
        "pos_t": positions(), "masks": mask, "levels": levels,
        "w_mod": f["w_mod"], "w_router": f["moe_w_router"], "moe_w_gu": f["moe_w_gu"], "moe_w_down": f["moe_w_down"],
        "gmlp_w_in": f["gmlp_w_in"], "gmlp_w_out": f["gmlp_w_out"],
        "gmlp_ws": np.ascontiguousarray(f["gmlp_w_s"].transpose(0, 3, 1, 2)),
        "gmlp_bs": f["gmlp_b_s"].reshape(-1, 8 * P),
        "ssd_w_in": f["ssd_w_in"], "ssd_w_out": f["ssd_w_out"],
        "s_ssd": np.ascontiguousarray(f["state_ssd"][0, 0].transpose(0, 3, 1, 2).reshape(2, SN, SI)),
        "hgrn_w_in": f["hgrn_w_in"], "hgrn_w_out": f["hgrn_w_out"],
        "s_hgrn": np.ascontiguousarray(f["state_hgrn"][0, 0].transpose(2, 0, 1, 3)),
    }
    assert arrays["cols"].shape[1] == NCOL
    nc = _bacc.Bacc("TRN2", target_bir_lowering=False, num_devices=1)
    A = {k: nc.dram_tensor(k, a.shape, mybir.dt.from_np(a.dtype), kind="ExternalInput").ap() for k, a in arrays.items()}
    outs = {"y_t": (P, KD, T), "n_ssd": (2, SN, SI), "n_hgrn": (P, 2, HH, P)}
    O = {k: nc.dram_tensor("o_" + k, s, F32, kind="ExternalOutput").ap() for k, s in outs.items()}
    trunk(nc, A, O)
    r = _run(nc, [arrays], core_ids=[0]).results[0]
    out = np.asarray(r["o_y_t"]).transpose(1, 0, 2).reshape(D, T).T
    ssd = np.asarray(r["o_n_ssd"]).reshape(2, SN, SH, SP_).transpose(0, 2, 3, 1)
    hgrn = np.asarray(r["o_n_hgrn"]).transpose(1, 2, 0, 3)
    return (np.ascontiguousarray(out[None, :LC]), np.ascontiguousarray(out[None, LC:]),
            np.ascontiguousarray(ssd[None, None]), np.ascontiguousarray(hgrn[None, None]))
```

```python
import math
from contextlib import ExitStack, contextmanager

import concourse.bass as bass
import numpy as np
from concourse import mybir

F32 = mybir.dt.float32
F32R = mybir.dt.float32r
U32 = mybir.dt.uint32
ALU = mybir.AluOpType
ACT = mybir.ActivationFunctionType
AX = mybir.AxisListType

P = 128
D = 1024
KD = D // P
LC, LS = 128, 256
T = LC + LS
NT = T // P
DEPTH = 4
ALPHA = (2.0 * DEPTH) ** 0.25
EPS = 1e-5
SEGS = ((0, 0, LC), (1, LC, T))

GW = 2 * D
NE, NG, EG = 16, 4, 4
DE = 256
SH, SP_, SG_, SN = 32, 64, 4, 128
SI = SH * SP_
SSD_IN = 2 * SI + 2 * SG_ * SN + 2 * SH
HH = 8
LEVELS = 7
BIG = 1e30

SUB = 1024
RAW = 4
SPL = 4
MODC = 6 * D // 256
MOD_GROUP = MODC // 6
START_MODS = 2 * MOD_GROUP
V_MODS = (2,) * 6 + (0,) * 2
EARLY = 3
MOE_ITERS = 4

COLS = [("bmod", DEPTH * 48), ("lng", DEPTH * 16), ("lnb", DEPTH * 16), ("glng", 32), ("glnb", 32),
        ("convw", 72), ("convb", 24), ("dskip", 16), ("sng", 16), ("lbl", 64), ("hng", 1), ("cond", 16),
        ("dtb", 64), ("alog", 64), ("brout", 16), ("gkey", NG), ("ekey", NE)]
COL, _at = {}, 0
for _n, _w in COLS:
    COL[_n] = _at
    _at += _w
NCOL = _at

def moe_order(mods):
    order = []
    for e in range(EG):
        order += [("G", e)] + ([("M", e)] if mods else []) + [("U", e)] + ([("D", e - 1)] if e else [])
    return order + [("D", EG - 1)]


LOOP_SPLIT = 2 * len(moe_order(False))


def stream_plan():
    places, rows = {}, []

    def part(name, n, k=KD):
        for _ in range(n):
            places.setdefault(name, []).append(len(rows))
            rows.append(k)

    part(("mod", 0), START_MODS, 0)
    for l in range(DEPTH):
        kind = ("gmlp", "ssd", "hgrn")[l % 3]
        outs, k = 8, 16
        if kind == "gmlp":
            for c in range(8):
                part(("mod", 0), 0 if l else V_MODS[c], 0)
                part((l, "v"), 1)
            part((l, "u"), 8)
        elif kind == "ssd":
            part((l, "dt"), 1); part((l, "xs"), 12); part((l, "z"), 8)
        else:
            part((l, "q"), 4)
            for c in range(8):
                part(("mod", l), 1 if c < MOD_GROUP else 0, 0)
                part((l, "f"), 1)
            part((l, "i"), 4); part((l, "g"), 4)
            outs, k = 4, KD
        for c in range(outs):
            for owner, _ in out_mods(l, c, outs):
                part(("mod", owner), 1, 0)
            part((l, "out"), 1, k)
        for _ in range(MOE_ITERS):
            for what, _ in moe_order(l + 1 < DEPTH):
                part(("mod", l + 1) if what == "M" else (l, "moe"), 1, {"D": 2, "M": 0}.get(what, KD))
    return places, rows


def out_mods(l, c, outs):
    todo = ([(l, MODC - MOD_GROUP + j) for j in range(MOD_GROUP)] if l % 3 < 2 else []) + \
           ([(l + 1, j) for j in range(MOD_GROUP)] if l + 1 < DEPTH else [])
    return todo[c * len(todo) // outs:(c + 1) * len(todo) // outs]


class Chain:
    def __init__(self, eng, sem):
        self.eng, self.sem, self.n, self.shift = eng, sem, 0, 0

    def link(self, ins):
        self.n += 1
        ins.then_inc(self.sem, 1)
        self.eng.wait_ge(self.sem, self.shift + self.n)

    @contextmanager
    def loop(self, start, end, per):
        with self.eng.Fori(start, end) as i:
            first = self.n
            self.shift = (i - start) * per if start else i * per
            yield i
            assert self.n - first == per, (self.n - first, per)
        self.shift = 0
        self.n = first + per * (end - start)


def trunk(nc, A, O):
    places, chunk_rows = stream_plan()
    NCHUNK = len(chunk_rows)
    NSUB = 2 * NCHUNK
    order_of = [s for s in range(NSUB) if chunk_rows[s // 2]]
    nth = [0]
    for s in range(NSUB):
        nth.append(nth[-1] + (chunk_rows[s // 2] > 0))
    mod_at = [c for c in range(NCHUNK) if chunk_rows[c] == 0]
    ctx = ExitStack()
    with ctx:
        def sem(name):
            return ctx.enter_context(nc.semaphore(name))

        place = [0]
        limit = 53200 * 4
        ctx.enter_context(nc.sbuf_tensor("whole", [P, limit // 4], F32))
        org = nc.sbuf_base - limit

        def at(name, shape, dt, offset):
            size = 4 * int(np.prod(shape[1:]))
            assert offset + size <= limit, (name, offset + size, limit)
            return nc.alloc_sbuf_tensor_at(name, shape, dt, offset=org + offset)

        def fixed(name, shape, dt=F32):
            t = at(name, shape, dt, place[0])
            place[0] += -(-4 * int(np.prod(shape[1:])) // 32) * 32
            return t

        raw = fixed("raw", [P, RAW, 2 * SUB])
        whi = fixed("whi", [P, SPL, SUB], F32R)
        wlo = fixed("wlo", [P, SPL, SUB], F32R)
        x = fixed("x_t", [P, KD, T])
        hh = fixed("hh", [P, KD, T], F32R)
        hl = fixed("hl", [P, KD, T], F32R)
        yoff = place[0]
        y = fixed("y_t", [P, KD, T])
        cols = fixed("cols", [P, NCOL])
        ident = fixed("ident", [P, P])
        ones = fixed("ones", [P, P])
        mean_d = fixed("mean_d", [P, P])
        mods = fixed("mods", [P, 2, 48, 2])
        cond = fixed("cond_s", [P, KD, 2])
        cmod = fixed("cmod", [P, 2, KD, 2])
        eps = fixed("eps", [P, 1])
        KB = 1024

        def ar(name, shape, dt=F32, kb=0.0):
            return at(name, shape, dt, AR + int(kb * KB))

        def yr(name, shape, dt=F32, kb=0.0):
            assert kb * KB + 4 * int(np.prod(shape[1:])) <= 12 * KB, name
            return at(name, shape, dt, yoff + int(kb * KB))

        wrt = fixed("wrt", [P, KD, NE])
        wrh = fixed("wrh", [P, KD, NE], F32R)
        wrl = fixed("wrl", [P, KD, NE], F32R)
        AR = place[0]
        sq = ar("ln_sq", [P, KD, T], F32, 0)
        h32 = ar("h32", [P, KD, T], F32, 12)
        std = ar("ln_std", [P, T], F32, 84)
        rstd = ar("ln_rstd", [P, T], F32, 86)
        macc = ar("macc", [P, 2, D], F32, 76)
        gv = ar("gv", [P, NT, GW], F32, 0)
        gsh = ar("gsh", [P, 16, T], F32R, 24)
        gsl = ar("gsl", [P, 16, T], F32R, 48)
        gws = ar("gws", [P, 8, P], F32, 72)
        gu = ar("gu", [P, 4, T], F32, 76)
        gat = ar("gat", [P, T], F32, 82)
        gct = ar("gct", [P, 2, P], F32, 83.5)
        gst = ar("gst", [P, NT, 4, 6], F32, 85)
        gmv = ar("gmv", [P, NT, 2], F32, 86)
        grs = ar("grs", [P, NT, 2], F32, 86.5)
        gbs = yr("gbs", [P, 8, P], F32, 0)
        grow = yr("grow", [P, 8, P], F32, 4)
        gs32 = yr("gs32", [P, 2, T], F32, 8)
        cwb = ar("cwb", [P, NE, T], F32, 0)
        acc = ar("acc", [P, KD, T], F32, 24)
        diag = ar("diag", [P, NE, P], F32, 36)
        sg = ar("sg", [P, 2, 2, T], F32, 44)
        e32 = ar("e32", [P, 2, 2, T], F32, 50)
        eh = ar("eh", [P, 2, 2, T], F32R, 56)
        el = ar("el", [P, 2, 2, T], F32R, 62)
        et = ar("et", [P, 2, T], F32, 68)
        rt = ar("rt", [P, 16, NT, NE], F32, 71)
        xs = ar("xs", [P, 16, T], F32, 0)
        syh = ar("syh", [P, 16, T], F32R, 24)
        syl = ar("syl", [P, 16, T], F32R, 48)
        bc = ar("bc", [P, 8, T], F32, 24)
        xt = ar("xt", [P, NT, SI], F32, 36)
        bt = ar("bt", [P, NT, 4 * SN], F32, 60)
        cb = ar("cb", [P, NT, P], F32, 66)
        tri = ar("tri", [P, 2, P], F32, 72)
        lim = ar("lim", [P, 2, P], F32, 73)
        dt = ar("dt", [P, NT, 64], F32, 74)
        dta = ar("dta", [P, NT, 64], F32, 74.75)
        acs = ar("acs", [P, NT, 64], F32, 75.5)
        dend = ar("dend", [P, NT, 64], F32, 76.25)
        edec = ar("edec", [P, NT, 64], F32, 77)
        ea = ar("ea", [P, 64], F32, 77.75)
        se = [ar("se0", [P, 2, 4, P], F32, 78), ar("se1", [P, 2, 4, P], F32, 67.5)]
        sce = [ar("sce0", [P, 2, 4, P], F32, 82), yr("sce1", [P, 2, 4, P], F32, 8)]
        swt = ar("swt", [P, 4, P], F32, 86)
        stg = ar("stg", [P, 2, T + 4], F32, 78)
        ctm = ar("ctm", [P, 2, T + 4], F32, 82)
        szt = ar("szt", [P, 2, T], F32, 78)
        sgy = ar("sgy", [P, 2, T], F32, 81)
        ssq = ar("ssq", [P, 2, T], F32, 84)
        srr = ar("srr", [P, T], F32, 87)
        sout = ar("sout", [P, 2, T], F32, 0)
        s0 = yr("s0", [P, 2, 512], F32, 0)
        s1 = yr("s1", [P, 2, 512], F32, 4)
        xdd = yr("xdd", [P, 2, 512], F32, 8)
        dtw = ar("dtw", [P, 6, NT * 64], F32, 82)
        hq = ar("hq", [P, HH, T], F32, 0)
        hk = ar("hk", [P, 2, HH, T], F32, 12)
        hoh = ar("hoh", [P, HH, T], F32R, 12)
        hol = ar("hol", [P, HH, T], F32R, 24)
        hf = ar("hf", [P, 2, HH, T], F32, 36)
        hv = ar("hv", [P, NT, D], F32, 60)
        lvl = ar("lvl", [P, LEVELS, P], U32, 72)
        hrs = ar("hrs", [P, T], F32, 72)
        uws = [ar("uw0", [P, 2, T], F32, 76), ar("uw1", [P, 2, T], F32, 79), ar("uw2", [P, 2, T], F32, 85.75)]
        att = yr("att", [P, T], F32, 10)
        hs0 = yr("hs0", [P, 2, HH, P], F32, 0)
        hqe = yr("hqe", [P, 2, LS], F32, 8)
        hkh = ar("hkh", [P, 2, P], F32, 82)
        hkt = ar("hkt", [P, 2, P], F32, 83)
        hs1 = ar("hs1", [P, 2, P], F32, 84)
        hsto = [ar("hsto0", [P, P], F32, 75.5), yr("hsto1", [P, P], F32, 11.5)]
        hmask = ar("hmask", [P, T], F32, 86)
        lbt2 = ar("lbt", [P, 96], F32, 75.5)
        hed = ar("hed", [P, 2], F32, 85)
        hres = ar("hres", [P, T], F32, 74)
        hsg = ar("hsg", [P, 2, T], F32, 76)
        hon = ar("hon", [P, 2, T], F32, 80)
        hsq = ar("hsq", [P, 2, T], F32, 84)

        ps = ctx.enter_context(nc.psum_tensor("ps", [P, 8, 512], F32))
        def bank(b):
            return ps[:, b, 0:T]

        raw_in = [sem(f"raw_in{i}") for i in range(RAW)]
        hst_out = [sem(f"hst_out{d}") for d in range(2)]
        names = """cols_in x_in consts_set hi_ready lo_ready sub_done w_sub wq_ready mac_step mod_summed mod_read cond_ready
            h32_ready hh_ready hl_ready y_ready mean_done diff_ready sq_ready var_done std_ready norm_ready x_ready
            v_evac v_norm u_evac rows_done rows_read mix_done a_ready s32_ready sh_ready sl_ready gmlp_in
            router_in router_split router_done route_ready cw_ready cwb_done cwb_read
            gate_read up_read e32_ready eh_ready el_ready down_added down_done
            dve_step act_step pool_step out_done ssd_in gstat_done gstd_done dt_act dt_vec acs_done
            stage_ready conv_ready xbc_ready xpose_done xpose_read cb_done cb_read s0_in
            xdd_ready st_done s1_ready stout_read seg_done seg_ready exp_ready ce_exp ce_ready w_ready ydone y_read
            z_act gz_ready gy_ready gsq_ready syh_ready syl_ready rms_done rms_std
            hgrn_in q_evac f_act k_ready f_ln scan_ready vi_evac u_sub u_exp uw_ready lv_done lv_read
            kh_exp kh_ready khT_done khT_read hst_done hs1_ready qe_exp qe_ready o_done o_read
            ho_sq hms_done hstd on_ready hg_act hon_ready hoh_ready hol_ready hmask_set conv_pad st_out edec_ready lb_act lb_vec""".split()
        S = {n: sem(n) for n in names}

        block = ctx.enter_context(nc.Block())

        def c_(name, i, n=1):
            return cols[:, COL[name] + i:COL[name] + i + n]

        @block.sync
        def _(sp):
            def load(c, src):
                if c >= RAW:
                    if chunk_rows[c - RAW]:
                        sp.wait_ge(S["sub_done"], nth[2 * (c - RAW)] + 2)
                    else:
                        sp.wait_ge(S["mac_step"], 4 * (mod_at.index(c - RAW) + 1))
                fill(c, src)

            def fill(c, src):
                dst = raw[:, c % RAW, :].rearrange("p (k n) -> p k n", k=src.shape[1])
                sp.dma_start(dst, src).then_inc(raw_in[c % RAW], 16)

            def run(name, start, end, view, lo=0):
                for j in range(start, end):
                    load(places[name][j], view[lo + j])

            def load_mod(l, q):
                load(places["mod", l][q], mview[l][q // MOD_GROUP][q % MOD_GROUP])

            def run_out(l, view):
                outs = len(places[l, "out"])
                for c in range(outs):
                    for owner, q in out_mods(l, c, outs):
                        load_mod(owner, q)
                    load(places[l, "out"][c], view[c])

            v8 = lambda w: w.rearrange("(k p) (c n) -> c p k n", p=P, n=2 * P)
            v16 = lambda w: w.rearrange("(k p) (c n) -> c p k n", p=P, n=P)
            sp.dma_start(cols[:, :], A["cols"]).then_inc(S["cols_in"], 16)
            mview = [A["w_mod"][l].rearrange("(q k p) (g n) -> g q p k n", p=P, k=2, n=D) for l in range(DEPTH)]
            for j in range(START_MODS):
                load_mod(0, j)
                if j == 3:
                    sp.dma_start(x[:, :, :], A["x_t"]).then_inc(S["x_in"], 16)
                    sp.dma_start(h32[:, :, 0:LS], A["pos_t"]).then_inc(S["x_in"], 16)
                    sp.dma_start(ident[:, :], A["masks"][:, 0:P]).then_inc(S["x_in"], 16)
                    sp.dma_start(wrt[:, :, :], A["w_router"].rearrange("(k p) e -> p k e", p=P)).then_inc(S["router_in"], 16)
            for l in range(DEPTH):
                kind = ("gmlp", "ssd", "hgrn")[l % 3]
                if kind == "gmlp":
                    g = l // 3
                    win = v8(A["gmlp_w_in"][g])
                    if l:
                        for c in range(EARLY):
                            load(places[l, "v"][c], win[8 + c])
                        sp.wait_ge(S["hl_ready"], 8 * (2 * l + 1))
                    sp.dma_start(gws[:, :, :], A["gmlp_ws"][g]).then_inc(S["gmlp_in"], 16)
                    sp.dma_start(gbs[:, :, :], A["gmlp_bs"][g:g + 1, :].partition_broadcast(P)).then_inc(S["gmlp_in"], 16)
                    for c in range(EARLY if l else 0, 8):
                        for j in range(0 if l else V_MODS[c]):
                            load_mod(0, START_MODS + sum(V_MODS[:c]) + j)
                        load(places[l, "v"][c], win[8 + c])
                    run((l, "u"), 0, 8, win)
                    run_out(l, v16(A["gmlp_w_out"][g]))
                elif kind == "ssd":
                    w = A["ssd_w_in"][0]
                    run((l, "dt"), 0, 1, v8(w[:, SSD_IN - 256:SSD_IN]))
                    wx = v8(w[:, SI:2 * SI + 2 * SG_ * SN])
                    run((l, "xs"), 0, EARLY - 1, wx)
                    sp.wait_ge(S["hl_ready"], 8 * (2 * l + 1))
                    sp.dma_start(tri[:, :, :], A["masks"][:, P:3 * P]).then_inc(S["ssd_in"], 16)
                    sp.dma_start(lim[:, :, :], A["masks"][:, 3 * P:5 * P]).then_inc(S["ssd_in"], 16)
                    run((l, "xs"), EARLY - 1, 12, wx)
                    z = v8(w[:, 0:SI])
                    run((l, "z"), 0, 4, z)
                    for g in range(SG_):
                        if g:
                            sp.wait_ge(S["y_read"], 6 * g)
                        else:
                            sp.wait_ge(S["acs_done"], 2)
                        sp.dma_start(s0[:, :, :], A["s_ssd"][:, :, g * 512:(g + 1) * 512].rearrange("d n c -> n d c")).then_inc(S["s0_in"], 16)
                        if g in (1, 2):
                            run((l, "z"), 2 * g + 2, 2 * g + 4, z)
                    run_out(l, v16(A["ssd_w_out"][0]))
                else:
                    w = v8(A["hgrn_w_in"][0])
                    run((l, "q"), 0, EARLY, w)
                    sp.wait_ge(S["hl_ready"], 8 * (2 * l + 1))
                    sp.dma_start(lvl[:, :, :], A["levels"]).then_inc(S["hgrn_in"], 16)
                    sp.dma_start(hs0[:, :, :, :], A["s_hgrn"]).then_inc(S["hgrn_in"], 16)
                    run((l, "q"), EARLY, 4, w)
                    for c in range(8):
                        if c < MOD_GROUP:
                            load_mod(l, MODC - MOD_GROUP + c)
                        load(places[l, "f"][c], w[4 + c])
                    run((l, "i"), 0, 4, w, 12)
                    run((l, "g"), 0, 4, w, 16)
                    run_out(l, v8(A["hgrn_w_out"][0]))
                more = l + 1 < DEPTH
                gu_ = A["moe_w_gu"][l].rearrange("e (k p) (c n) -> e c p k n", p=P, n=2 * P)
                dn = A["moe_w_down"][l].rearrange("e (k p) n -> e p k n", p=P)
                order = moe_order(more)
                c0 = places[l, "moe"][0]
                m0 = 4 * len([c for c in mod_at if c < c0])
                with sp.Fori(0, MOE_ITERS) as i:
                    for p, (what, j) in enumerate(order):
                        c = c0 + p
                        if p < RAW:
                            after = [w for w, _ in order[len(order) + p - RAW + 1:] if w != "M"]
                            used = nth[2 * c0] - 2 * len(after)
                            if chunk_rows[c - RAW]:
                                used = max(used, nth[2 * (c - RAW)] + 2)
                            sp.wait_ge(S["sub_done"], used + i * LOOP_SPLIT)
                            if p == 0:
                                sp.wait_ge(S["mac_step"], m0 + i * 4 * MOD_GROUP if more else m0)
                        elif order[p - RAW][0] == "M":
                            sp.wait_ge(S["mac_step"], m0 + 4 * (order[p - RAW][1] + 1) + i * 4 * MOD_GROUP)
                        else:
                            sp.wait_ge(S["sub_done"], nth[2 * (c - RAW)] + 2 + i * LOOP_SPLIT)
                        if what == "M":
                            fill(c, mview[l + 1][bass.ds(1 + i, 1)][0][j])
                        elif what == "D":
                            fill(c, dn[bass.ds(j + i * EG, 1)][0])
                        else:
                            fill(c, gu_[bass.ds(j + i * EG, 1)][0][int(what == "U")])
            sp.wait_ge(S["x_ready"], 8 * (2 * DEPTH + 1))
            sp.dma_start(O["y_t"], x[:, :, :]).then_inc(S["out_done"], 16)
            sp.wait_ge(S["out_done"], 16)
            sp.wait_ge(S["st_out"], 16 * 2 * SG_)
            for d in range(2):
                sp.wait_ge(hst_out[d], 16 * HH)
        def sb(name, j=0):
            part = places[name]
            return 2 * part[j // 2] + j % 2 if j < 2 * len(part) else 2 * part[-1] + 2 + j - 2 * len(part)

        def end_of_experts(l):
            return 2 * places[l, "moe"][-1] + 2

        STATES = ((0, 0), (0, 1), (1, 0), (2, 1))
        SCAN_Z = 4 * (SG_ - 1)

        def z_of(u):
            return 4 * (u // 6 - 1) + {0: 0, 1: 1, 3: 2, 4: 3}[u % 6] if u >= 6 and u % 6 in (0, 1, 3, 4) else None

        def z_pair(u):
            return 4 * (u // 6 - 1) + {2: 0, 5: 2}[u % 6] if u >= 6 and u % 6 in (2, 5) else None

        def toks(t):
            return slice(t * P, (t + 1) * P)

        def act_ssd(act, l, feed):
            for j in range(24):
                s = sb((l, "xs"), j)
                if j == 0:
                    feed(sb((l, "dt")) + 3)
                    act.wait_ge(S["dt_vec"], 1)
                    act.activation(dtw[:, 2, :], dtw[:, 1, :], ACT.Exp).then_inc(S["dt_act"], 1)
                    act.activation(ea[:, :], c_("alog", 0, 64), ACT.Exp).then_inc(S["dt_act"], 1)
                    act.wait_ge(S["dt_vec"], 2)
                    act.activation(dtw[:, 4, :], dtw[:, 3, :], ACT.Ln).then_inc(S["dt_act"], 1)
                    act.wait_ge(S["dt_vec"], 4)
                    act.activation(dend[:, :, :], dend[:, :, :], ACT.Exp).then_inc(S["dt_act"], 1)
                    act.activation(edec[:, :, :], ps[:, 5, 0:NT * 64].rearrange("p (t h) -> p t h", t=NT),
                                   ACT.Exp).then_inc(S["dt_act"], 1)
                    act.wait_ge(S["conv_pad"], 1)
                feed(s + 3)
                act.wait_ge(S["sub_done"], nth[s] + 1)
                if j >= 2:
                    act.wait_ge(S["conv_ready"], j - 1)
                act.activation(stg[:, j % 2, 1:LC + 1], ps[:, j % 4, 0:LC], ACT.Copy)
                act.activation(stg[:, j % 2, LC + 3:T + 3], ps[:, j % 4, LC:T], ACT.Copy).then_inc(S["stage_ready"], 1)
                for i in ([j - 1] if j else []) + ([23] if j == 23 else []):
                    act.wait_ge(S["conv_ready"], i + 1)
                    dst = xs[:, i, :] if i < 16 else bc[:, i - 16, :]
                    act.activation(dst[:, 0:LC], ctm[:, i % 2, 0:LC], ACT.Silu)
                    act.activation(dst[:, LC:T], ctm[:, i % 2, LC + 2:T + 2], ACT.Silu).then_inc(S["xbc_ready"], 1)
            feed(sb((l, "z")) + 3)
            for n in range(15):
                act.wait_ge(S["xpose_done"], n + 1)
                t, g = divmod(n, 5)
                dst = xt[:, t, g * 512:(g + 1) * 512] if g < 4 else bt[:, t, :]
                act.activation(dst, ps[:, 4 + n % 4, :], ACT.Copy).then_inc(S["xpose_read"], 1)
            for g in range(SG_):
                act.wait_ge(S["cb_done"], g + 1)
                act.activation(cb[:, :, :].rearrange("p t n -> p (t n)"), bank(6 + g % 2), ACT.Copy).then_inc(S["cb_read"], 1)
                for d in range(2):
                    act.wait_ge(S["st_done"], 4 * g + d + 1)
                    act.activation(sce[0][:, d, :, :].rearrange("p a b -> p (a b)"), ps[:, 4 + d, :], ACT.Copy).then_inc(S["stout_read"], 1)
                    act.wait_ge(S["stout_read"], 2 * g + d + 1)
                    act.dma_start(O["n_ssd"][d][:, g * 512:(g + 1) * 512],
                                  sce[0][:, d, :, :].rearrange("p a b -> p (a b)")).then_inc(S["st_out"], 16)
                for u in range(6 * g, 6 * g + 6):
                    t = (u % 6) // 2
                    act.wait_ge(S["seg_ready"], u + 1)
                    act.activation(se[u % 2][:, :, :, :], se[u % 2][:, :, :, :], ACT.Exp).then_inc(S["exp_ready"], 1)
                    if t:
                        if u % 6 == 2:
                            act.wait_ge(S["st_out"], 32 * (g + 1))
                        elif u % 6 == 3:
                            act.wait_ge(S["st_done"], 4 * g + 4)
                        else:
                            act.wait_ge(S["ydone"], u - 1)
                        act.activation(sce[u % 2][:, :, :, :].rearrange("p d r n -> p d (r n)"),
                                       ps[:, 2 * (u % 2):2 * (u % 2) + 2, :], ACT.Exp).then_inc(S["ce_exp"], 1)
                    if z_of(u) is not None:
                        feed(sb((l, "z"), z_of(u)) + 3)
                    if z_pair(u) is not None:
                        act.wait_ge(S["sub_done"], nth[sb((l, "z"), z_pair(u) + 1)] + 1)
                        act.activation(ps[:, 4:6, 0:T], ps[:, 4:6, 0:T], ACT.Silu).then_inc(S["z_act"], 2)
            for j in range(17):
                if j % 2 == 0 and j < 8:
                    feed(sb((l, "z"), SCAN_Z + j // 2) + 3)
                if j % 2 == 0 and 2 <= j < 10:
                    f = SCAN_Z + j // 2 - 1
                    act.wait_ge(S["sub_done"], nth[sb((l, "z"), f)] + 1)
                    if f >= SCAN_Z + 2:
                        act.wait_ge(S["gz_ready"], f - 1)
                    act.activation(szt[:, f % 2, :], bank(f % 4), ACT.Silu).then_inc(S["z_act"], 1)
                if j:
                    act.wait_ge(S["gz_ready"], j)
                    if j >= 3:
                        act.wait_ge(S["rms_done"], j - 2)
                    act.activation(ssq[:, (j - 1) % 2, :], xs[:, j - 1, :], ACT.Square).then_inc(S["gsq_ready"], 1)
                    act.wait_ge(S["gy_ready"], j)
                    act.activation(syh[:, j - 1, :], sgy[:, (j - 1) % 2, :], ACT.Copy).then_inc(S["syh_ready"], 1)
            feed(sb((l, "out")) + 3)
            act.wait_ge(S["rms_done"], 16)
            act.activation(srr[:, :], bank(6), ACT.Sqrt, bias=eps[:, 0:1], scale=0.5).then_inc(S["rms_std"], 1)
            for m in range(8):
                feed(sb((l, "out"), 2 * m + 2) + 3)

        def pool_ssd(pool, l, feed):
            pool.memset(stg[:, :, :], 0.0).then_inc(S["conv_pad"], 1)
            feed(sb((l, "z")) + 3)
            for u in range(24):
                if (u % 6) // 2:
                    t, g = (u % 6) // 2, u // 6
                    n = sum(1 for v in range(u) if (v % 6) // 2)
                    pool.wait_ge(S["ce_exp"], n + 1)
                    e = sce[u % 2][:, :, :, :].rearrange("p d r n -> p (d r) n")
                    pool.tensor_tensor(e, e,
                                       bc[:, 4 + g, toks(t)].unsqueeze(1).to_broadcast([P, 8, P]), ALU.mult).then_inc(S["ce_ready"], 1)
                if z_of(u) is not None:
                    feed(sb((l, "z"), z_of(u)) + 3)
            for j in range(16):
                feed(sb((l, "z"), min(SCAN_Z + j // 2, 15)) + 3)
                pool.wait_ge(S["syh_ready"], j + 1)
                pool.tensor_tensor(syl[:, j, :], sgy[:, j % 2, :], syh[:, j, :].bitcast(F32), ALU.subtract).then_inc(S["syl_ready"], 1)

        def pe_ssd(pe, l, claim, release, full, by_token, out_tiles):
            s = sb((l, "dt"))
            pe.wait_ge(S["lo_ready"], nth[s] + 2)
            claim(4, "dt_vec", 1)
            for t in range(NT):
                for k in range(KD):
                    w = slice(k * P + 64, (k + 1) * P)
                    o = ps[:, 4, t * 64:(t + 1) * 64]
                    if t == 0:
                        pe.wait_ge(S["hl_ready"], 8 * (2 * l) + k + 1)
                    pe.matmul(o, hh[:, k, toks(t)], whi[:, (nth[s] + 1) % SPL, w], start=(k == 0), stop=False)
                    pe.matmul(o, hl[:, k, toks(t)], whi[:, (nth[s] + 1) % SPL, w], start=False, stop=False)
                    ins = pe.matmul(o, hh[:, k, toks(t)], wlo[:, (nth[s] + 1) % SPL, w], start=False, stop=(k == KD - 1))
            ins.then_inc(S["sub_done"], 2)
            for j in range(24):
                s = sb((l, "xs"), j)
                pe.wait_ge(S["lo_ready"], nth[s] + 1)
                if j == 0:
                    for b in range(4):
                        claim(b, "stage_ready", b + 1)
                else:
                    claim(j % 4, "stage_ready", j + 1) if j >= 4 else None
                full(s, bank(j % 4), hh, hl)
                if j == 1:
                    pe.wait_ge(S["dt_vec"], 3)
                    pe.wait_ge(S["ssd_in"], 32)
                    claim(5, "dt_act", 5)
                    claim(4, "dt_vec", 4)
                    for t in range(NT):
                        for d in range(2):
                            c = t * 64 + d * 32
                            ins = pe.matmul(ps[:, 4, c:c + 32], tri[:, d, :], dta[:, t, d * 32:(d + 1) * 32], start=True, stop=True)
                    ins.then_inc(S["acs_done"], 1)
                    pe.matmul(ps[:, 5, 0:NT * 64], ones[:, :], dta[:, :, :].rearrange("p t h -> p (t h)"), start=True,
                              stop=True).then_inc(S["acs_done"], 1)
            pe.wait_ge(S["dt_act"], 5)
            for n in range(15):
                t, g = divmod(n, 5)
                pe.wait_ge(S["xbc_ready"], 4 * g + 4)
                claim(4 + n % 4, "xpose_read", n + 1)
                for i in range(4):
                    src = xs[:, 4 * g + i, toks(t)] if g < 4 else bc[:, i, toks(t)]
                    ins = pe.transpose(ps[:, 4 + n % 4, i * P:(i + 1) * P], src, ident[:, :])
                ins.then_inc(S["xpose_done"], 1)
            pe.wait_ge(S["xbc_ready"], 24)

            def seg(u):
                t, h0 = (u % 6) // 2, (u // 6) * 8 + (u % 2) * 4
                if u < 2:
                    claim(2 * u, "w_ready", 0); claim(2 * u + 1, "w_ready", 0)
                for d in range(2):
                    for r in range(4):
                        ins = pe.matmul(ps[:, 2 * (u % 2) + d, r * P:(r + 1) * P],
                                        dta[:, t, d * 32 + h0 + r:d * 32 + h0 + r + 1].to_broadcast([P, P]), tri[:, d, :],
                                        start=True, stop=True)
                ins.then_inc(S["seg_done"], 1)

            for g in range(SG_):
                claim(6 + g % 2, "cb_read", g + 1)
                if g:
                    pe.wait_ge(S["w_ready"], 6 * g)
                for t in range(NT):
                    ins = pe.matmul(ps[:, 6 + g % 2, toks(t)], bc[:, g, toks(t)], bc[:, 4 + g, toks(t)], start=True, stop=True)
                ins.then_inc(S["cb_done"], 1)
                for j, (t, d) in enumerate(STATES):
                    pe.wait_ge(S["xdd_ready"], 4 * g + j + 1)
                    if j < 2:
                        claim(4 + j, "stout_read", 2 * g + j + 1)
                    else:
                        claim(2 + j, "s1_ready", 2 * g + j - 1)
                    pe.matmul(ps[:, 4 + j % 2, :], bt[:, t, g * SN:(g + 1) * SN], xdd[:, j % 2, :], start=True,
                              stop=True).then_inc(S["st_done"], 1)
                if g == 0:
                    seg(0)
                    seg(1)
                for u in range(6 * g, 6 * g + 6):
                    t, q = (u % 6) // 2, u % 2
                    pe.wait_ge(S["cb_read"], g + 1)
                    pe.wait_ge(S["w_ready"], u + 1)
                    if t:
                        n = sum(1 for v in range(u) if (v % 6) // 2)
                        pe.wait_ge(S["ce_ready"], n + 1)
                        pe.wait_ge(S["s1_ready"], 2 * g + 2)
                    if u + 2 < 24:
                        seg(u + 2)
                    claim(6 + u % 2, "y_read", u + 1)
                    for r in range(4):
                        o = ps[64 * (r % 2):64 * (r % 2) + 64, 6 + u % 2, (r // 2) * P:(r // 2 + 1) * P]
                        hc = slice((4 * q + r) * SP_, (4 * q + r + 1) * SP_)
                        ins = pe.matmul(o, xt[:, t, g * 512 + hc.start:g * 512 + hc.stop], swt[:, r, :], start=True, stop=(t == 0))
                        if t:
                            pe.matmul(o, (s0 if t == 1 else s1)[:, 0, hc], sce[u % 2][:, 0, r, :], start=False, stop=False)
                            ins = pe.matmul(o, (s1 if t == 1 else s0)[:, 1, hc], sce[u % 2][:, 1, r, :], start=False, stop=True)
                    ins.then_inc(S["ydone"], 1)
                    if z_of(u) is not None:
                        f = z_of(u)
                        s = sb((l, "z"), f)
                        pe.wait_ge(S["lo_ready"], nth[s] + 1)
                        claim(4 + f % 2, "gz_ready", f - f % 2 + 2)
                        full(s, bank(4 + f % 2), hh, hl)
            for b in range(4):
                release[b] = (S["w_ready"], 24)

            def squares(j):
                pe.wait_ge(S["gsq_ready"], j + 1)
                pe.matmul(bank(6), mean_d[:, :], ssq[:, j % 2, :], start=(j == 0),
                          stop=(j == 15)).then_inc(S["rms_done"], 1)

            claim(6, "rms_std", 1)
            for j in range(16):
                if j % 2 == 0 and j < 8:
                    f = SCAN_Z + j // 2
                    s = sb((l, "z"), f)
                    pe.wait_ge(S["lo_ready"], nth[s] + 1)
                    claim(f % 4, "z_act", f + 1)
                    full(s, bank(f % 4), hh, hl)
                if j >= 2:
                    squares(j - 2)
            squares(14)
            squares(15)
            out_tiles(l, syh, syl, 2, "syl_ready", 0)

        def dve_ssd(dve, l, link, start_residual, residual, out_chunk_mods, mod_take):
            w3 = lambda n: dtw[:, n, :].rearrange("p (t h) -> p t h", t=NT)
            dve.wait_ge(S["sub_done"], nth[sb((l, "dt"))] + 2)
            link(dve.tensor_tensor(w3(0), ps[:, 4, 0:NT * 64].rearrange("p (t h) -> p t h", t=NT),
                                   c_("dtb", 0, 64).unsqueeze(1).to_broadcast([P, NT, 64]), ALU.add))
            link(dve.tensor_scalar(dtw[:, 1, :], dtw[:, 0, :], -1.0, None, ALU.mult))
            dve.tensor_tensor(dtw[:, 1, :], dtw[:, 1, :], dtw[:, 0, :], ALU.min).then_inc(S["dt_vec"], 1)
            dve.wait_ge(S["dt_act"], 1)
            dve.tensor_scalar(dtw[:, 3, :], dtw[:, 2, :], 1.0, None, ALU.add).then_inc(S["dt_vec"], 1)
            dve.wait_ge(S["dt_vec"], 2)
            link(dve.tensor_scalar(dtw[:, 5, :], dtw[:, 3, :], -1.0, None, ALU.add))
            link(dve.tensor_tensor(dtw[:, 5, :], dtw[:, 2, :], dtw[:, 5, :], ALU.subtract))
            link(dve.reciprocal(dtw[:, 1, :], dtw[:, 3, :]))
            link(dve.tensor_tensor(dtw[:, 5, :], dtw[:, 5, :], dtw[:, 1, :], ALU.mult))
            dve.wait_ge(S["dt_act"], 3)
            link(dve.tensor_tensor(dtw[:, 5, :], dtw[:, 5, :], dtw[:, 4, :], ALU.add))
            link(dve.scalar_tensor_tensor(out=dt[:, :, :], in0=w3(0), scalar=0.0, in1=w3(5), op0=ALU.max, op1=ALU.add))
            dve.scalar_tensor_tensor(out=dta[:, :, :], in0=dt[:, :, :], scalar=-1.0,
                                     in1=ea[:, :].unsqueeze(1).to_broadcast([P, NT, 64]), op0=ALU.mult,
                                     op1=ALU.mult).then_inc(S["dt_vec"], 1)
            dve.wait_ge(S["acs_done"], 2)
            link(dve.tensor_copy(acs[:, :, :].rearrange("p t h -> p (t h)"), ps[:, 4, 0:NT * 64]))
            dve.tensor_tensor(dend[:, :, :].rearrange("p t h -> p (t h)"), ps[:, 5, 0:NT * 64],
                              acs[:, :, :].rearrange("p t h -> p (t h)"), ALU.subtract).then_inc(S["dt_vec"], 1)
            dve.wait_ge(S["dt_act"], 4)
            link(dve.tensor_tensor(dend[:, :, :], dend[:, :, :], dt[:, :, :], ALU.mult))
            for j in range(24):
                dve.wait_ge(S["stage_ready"], j + 1)
                if j >= 2:
                    dve.wait_ge(S["xbc_ready"], j - 1)
                a, n = ctm[:, j % 2, 0:T + 2], T + 2
                link(dve.tensor_scalar(a, stg[:, j % 2, 0:n], c_("convw", j), c_("convb", j), ALU.mult, ALU.add))
                link(dve.scalar_tensor_tensor(out=a, in0=stg[:, j % 2, 1:n + 1], scalar=c_("convw", 24 + j), in1=a, op0=ALU.mult, op1=ALU.add))
                dve.scalar_tensor_tensor(out=a, in0=stg[:, j % 2, 2:n + 2], scalar=c_("convw", 48 + j), in1=a, op0=ALU.mult,
                                         op1=ALU.add).then_inc(S["conv_ready"], 1)
            heads = lambda a, t, d, g: a[:, t, d * 32 + 8 * g:d * 32 + 8 * g + 8].unsqueeze(2).to_broadcast([P, 8, SP_])
            by_head = lambda a: a.rearrange("p (h w) -> p h w", w=SP_)

            def segment(u):
                t, h0 = (u % 6) // 2, (u // 6) * 8 + (u % 2) * 4
                dve.wait_ge(S["seg_done"], u + 1)
                if u >= 2:
                    dve.wait_ge(S["w_ready"], u - 1)
                for d in range(2):
                    for r in range(4):
                        ins = dve.scalar_tensor_tensor(out=se[u % 2][:, d, r, :], in0=ps[:, 2 * (u % 2) + d, r * P:(r + 1) * P],
                                                       scalar=acs[:, t, d * 32 + h0 + r:d * 32 + h0 + r + 1], in1=lim[:, d, :],
                                                       op0=ALU.subtract, op1=ALU.min)
                ins.then_inc(S["seg_ready"], 1)

            def y_out(u):
                t, g, q = (u % 6) // 2, u // 6, u % 2
                dve.wait_ge(S["ydone"], u + 1)
                for i in range(2):
                    f = 4 * g + 2 * q + i
                    ins = dve.scalar_tensor_tensor(out=xs[:, f, toks(t)], in0=xs[:, f, toks(t)], scalar=c_("dskip", f),
                                                   in1=ps[:, 6 + u % 2, i * P:(i + 1) * P], op0=ALU.mult, op1=ALU.add)
                ins.then_inc(S["y_read"], 1)

            dve.wait_ge(S["xpose_read"], 15)
            for g in range(SG_):
                if g:
                    y_out(6 * g - 1)
                for j, (t, d) in enumerate(STATES):
                    if 4 * g + j >= 2:
                        dve.wait_ge(S["st_done"], 4 * g + j - 1)
                    dve.tensor_tensor(by_head(xdd[:, j % 2, :]), by_head(xt[:, t, g * 512:(g + 1) * 512]), heads(dend, t, d, g),
                                      ALU.mult).then_inc(S["xdd_ready"], 1)
                dve.wait_ge(S["s0_in"], 16 * (g + 1))
                for j in (2, 3):
                    t, d = STATES[j]
                    link(dve.tensor_tensor(by_head(s1[:, d, :]), by_head(s0[:, d, :]), heads(edec, t, d, g), ALU.mult))
                    dve.wait_ge(S["st_done"], 4 * g + j + 1)
                    dve.tensor_tensor(s1[:, d, :], s1[:, d, :], ps[:, 4 + j % 2, :], ALU.add).then_inc(S["s1_ready"], 1)
                if g == 0:
                    segment(0)
                for u in range(6 * g, 6 * g + 6):
                    t, h0 = (u % 6) // 2, g * 8 + (u % 2) * 4
                    if u + 1 < 24:
                        segment(u + 1)
                    dve.wait_ge(S["exp_ready"], u + 1)
                    e = se[u % 2]
                    for r in range(4):
                        ins = dve.tensor_scalar(e[:, 1, r, :], e[:, 1, r, :], dt[:, t, 32 + h0 + r:33 + h0 + r], None, ALU.mult)
                    link(ins)
                    for r in range(4):
                        ins = dve.scalar_tensor_tensor(out=e[:, 0, r, :], in0=e[:, 0, r, :], scalar=dt[:, t, h0 + r:h0 + r + 1],
                                                       in1=e[:, 1, r, :], op0=ALU.mult, op1=ALU.add)
                    link(ins)
                    dve.wait_ge(S["cb_read"], g + 1)
                    if u:
                        dve.wait_ge(S["ydone"], u)
                    dve.tensor_tensor(swt[:, :, :], e[:, 0, :, :], cb[:, t, :].unsqueeze(1).to_broadcast([P, 4, P]),
                                      ALU.mult).then_inc(S["w_ready"], 1)
                    if u % 6:
                        y_out(u - 1)
                    if z_pair(u) is not None:
                        f = z_pair(u)
                        dve.wait_ge(S["z_act"], f + 2)
                        dve.wait_ge(S["y_read"], 6 * g)
                        dve.tensor_tensor(xs[:, f:f + 2, :], xs[:, f:f + 2, :], ps[:, 4:6, 0:T], ALU.mult).then_inc(S["gz_ready"], 2)
            y_out(23)
            dve.wait_ge(S["y_read"], 24)
            for j in range(16):
                if j % 2 and 3 <= j < 11:
                    f = SCAN_Z + (j - 3) // 2
                    dve.wait_ge(S["z_act"], f + 1)
                    dve.tensor_tensor(xs[:, f, :], xs[:, f, :], szt[:, f % 2, :], ALU.mult).then_inc(S["gz_ready"], 1)
                dve.wait_ge(S["gz_ready"], j + 1)
                if j >= 2:
                    dve.wait_ge(S["syl_ready"], j - 1)
                dve.tensor_scalar(sgy[:, j % 2, :], xs[:, j, :], c_("sng", j), None, ALU.mult).then_inc(S["gy_ready"], 1)
            start_residual(2 * l)
            dve.wait_ge(S["syl_ready"], 16)
            dve.wait_ge(S["rms_std"], 1)
            link(dve.reciprocal(srr[:, :], srr[:, :]))
            for m in range(KD):
                out_chunk_mods(l, m, 1)
                dve.wait_ge(S["sub_done"], nth[sb((l, "out"), 2 * m + 1)] + 1)
                link(dve.tensor_tensor(sout[:, m % 2, :], bank(m % 4), srr[:, :], ALU.mult))
                residual(l, m, sout[:, m % 2, :], 16)
                for group in sums_after(l, m):
                    mod_take(group)

        def act_hgrn(act, l, feed):
            feed(sb((l, "q")) + 3)
            act.wait_ge(S["lb_vec"], 1)
            act.activation(lbt2[:, 0:64], lbt2[:, 0:64], ACT.Exp).then_inc(S["lb_act"], 1)
            for j in range(8):
                s = sb((l, "q"), j)
                feed(s + 3)
                act.wait_ge(S["sub_done"], nth[s] + 1)
                act.activation(hq[:, j, :], bank(j % 4), ACT.Copy).then_inc(S["q_evac"], 1)
            for j in range(16):
                s = sb((l, "f"), j)
                feed(s + 3)
                act.wait_ge(S["sub_done"], nth[s] + 1)
                act.activation(hk[:, j // 8, j % 8, :], bank(j % 4), ACT.Sigmoid).then_inc(S["f_act"], 1)
            for c in range(4):
                s = sb((l, "i"), 2 * c)
                feed(s + 3)
                act.wait_ge(S["sub_done"], nth[s] + 2)
                for t in range(NT):
                    ins = act.activation(hv[:, t, c * 256:(c + 1) * 256], ps[:, 3 * (c % 2) + t, 0:256], ACT.Copy)
                ins.then_inc(S["vi_evac"], 1)
                if c < 2:
                    act.wait_ge(S["k_ready"], 8 * (c + 1))
                    act.activation(hf[:, c, :, :], hf[:, c, :, :], ACT.Ln).then_inc(S["f_ln"], 1)
            feed(sb((l, "g")) + 3)
            for h in range(HH):
                for j, (t, d) in enumerate(STATES):
                    n = 4 * h + j
                    act.wait_ge(S["scan_ready"], 8 + h + 1)
                    if n >= 2:
                        act.wait_ge(S["khT_done"], n - 1)
                    last = t * P + (P - 1 if d == 0 else 0)
                    act.activation(hkh[:, n % 2, :], hf[:, d, h, toks(t)], ACT.Exp, scale=-1.0,
                                   bias=hf[:, d, h, last:last + 1]).then_inc(S["kh_exp"], 1)
                if h:
                    act.wait_ge(S["o_done"], h)
                    act.activation(hq[:, h - 1, :], bank(2 + (h - 1) % 2), ACT.Copy).then_inc(S["o_read"], 1)
                act.activation(hqe[:, :, :], hf[:, :, h, LC:T], ACT.Exp).then_inc(S["qe_exp"], 1)
                for j in (2, 3):
                    t, d = STATES[j]
                    last = t * P + (P - 1 if d == 0 else 0)
                    if h:
                        act.wait_ge(S["hs1_ready"], 2 * h)
                    act.activation(hed[:, d:d + 1], hf[:, d, h, last:last + 1], ACT.Exp).then_inc(S["edec_ready"], 1)
                for j in range(2):
                    act.wait_ge(S["hst_done"], 4 * h + j + 1)
                    if h:
                        act.wait_ge(hst_out[j], 16 * h)
                    act.activation(hsto[j][:, :], ps[:, 6 + j, 0:P], ACT.Copy).then_inc(S["stout_read"], 1)
                    act.wait_ge(S["stout_read"], 2 * SG_ + 2 * h + j + 1)
                    act.dma_start(O["n_hgrn"][:, j, h, :], hsto[j][:, :]).then_inc(hst_out[j], 16)
                for j in range(LEVELS):
                    n = LEVELS * h + j
                    act.wait_ge(S["u_sub"], n + 1)
                    act.wait_ge(S["w_sub"], n + 1)
                    act.activation(uw_at(h, j + 1)[:, :, :], uw_at(h, j + 1)[:, :, :], ACT.Exp).then_inc(S["u_exp"], 1)
            act.wait_ge(S["o_done"], HH)
            act.activation(hq[:, HH - 1, :], bank(2 + (HH - 1) % 2), ACT.Copy).then_inc(S["o_read"], 1)
            for d in range(2):
                act.wait_ge(hst_out[d], 16 * HH)
            for h in range(HH):
                if h >= 2:
                    act.wait_ge(S["hms_done"], h - 1)
                act.wait_ge(S["o_read"], h + 1)
                act.activation(hsq[:, h % 2, :], hq[:, h, :], ACT.Square).then_inc(S["ho_sq"], 1)
                if h >= 1:
                    act.wait_ge(S["hms_done"], h)
                    if h >= 2:
                        act.wait_ge(S["on_ready"], h - 1)
                    act.activation(hres[:, :], bank(4 + (h - 1) % 2), ACT.Sqrt, bias=eps[:, 0:1], scale=8.0).then_inc(S["hstd"], 1)
                if h < 6:
                    feed(sb((l, "g"), h) + 3)
            act.wait_ge(S["hms_done"], HH)
            act.wait_ge(S["on_ready"], HH - 1)
            act.activation(hres[:, :], bank(4 + (HH - 1) % 2), ACT.Sqrt, bias=eps[:, 0:1], scale=8.0).then_inc(S["hstd"], 1)
            for j in range(9):
                if j < 8:
                    s = sb((l, "g"), j)
                    feed(s + 3)
                    act.wait_ge(S["sub_done"], nth[s] + 1)
                    if j >= 2:
                        act.wait_ge(S["hon_ready"], j - 1)
                    act.activation(hsg[:, j % 2, :], bank(G_BANKS[j]), ACT.Silu).then_inc(S["hg_act"], 1)
                if j:
                    act.wait_ge(S["hon_ready"], j)
                    act.activation(hoh[:, j - 1, :], hon[:, (j - 1) % 2, :], ACT.Copy).then_inc(S["hoh_ready"], 1)
            feed(sb((l, "out")) + 3)
            for m in range(8):
                feed(sb((l, "out"), m + 1) + 3)

        G_BANKS = (0, 1, 2, 3, 6, 7, 0, 1)

        def halves(a, j):
            return a.rearrange("p (b two n) -> p b two n", two=2, n=1 << j)

        def uw_at(h, j):
            return uws[((LEVELS + 1) * h + j) % 3]

        def borders(h, j):
            hw, nb = 1 << j, T // (2 << j)
            F, G = halves(hf[:, 0, h, :], j), halves(hf[:, 1, h, :], j)
            return F, G, F[:, :, 0, hw - 1:hw].to_broadcast([P, nb, hw]), G[:, :, 1, 0:1].to_broadcast([P, nb, hw])

        def pool_hgrn(pool, l, feed):
            pool.memset(hmask[:, :], 1.0).then_inc(S["hmask_set"], 1)
            pool.wait_ge(S["hmask_set"], 1)
            pool.memset(hmask[:, :].rearrange("p (t n) -> p t n", t=NT)[:, :, 0:1], 0.0).then_inc(S["hmask_set"], 1)
            feed(sb((l, "g")) + 3)
            pool.wait_ge(S["scan_ready"], 16)
            pool.wait_ge(S["q_evac"], 8)
            for h in range(HH):
                pool.wait_ge(S["qe_exp"], h + 1)
                pool.tensor_tensor(hqe[:, :, :], hqe[:, :, :], hq[:, h, LC:T].unsqueeze(1).to_broadcast([P, 2, LS]),
                                   ALU.mult).then_inc(S["qe_ready"], 1)
                for j in range(LEVELS + 1):
                    if j < LEVELS:
                        F, G, rf, rg = borders(h, j)
                        W = halves(uw_at(h, j + 1)[:, 1, :], j)
                        if (LEVELS + 1) * h + j >= 2:
                            pool.wait_ge(S["lv_done"], (LEVELS + 1) * h + j - 1)
                        pool.tensor_tensor(W[:, :, 1, :], F[:, :, 1, :], rf, ALU.subtract)
                        pool.tensor_tensor(W[:, :, 0, :], G[:, :, 0, :], rg, ALU.subtract).then_inc(S["w_sub"], 1)
                    if j:
                        pool.wait_ge(S["u_exp"], LEVELS * h + j)
                        W = uw_at(h, j)[:, 1, :]
                        pool.tensor_tensor(W, W, hq[:, h, :], ALU.mult).then_inc(S["wq_ready"], 1)
            feed(sb((l, "g"), 4) + 3)
            for j in range(8):
                pool.wait_ge(S["hoh_ready"], j + 1)
                pool.tensor_tensor(hol[:, j, :], hon[:, j % 2, :], hoh[:, j, :].bitcast(F32), ALU.subtract).then_inc(S["hol_ready"], 1)

        def pe_hgrn(pe, l, claim, release, full, by_token, out_tiles, mod_sum):
            for part, n, name in (("q", 8, "q_evac"), ("f", 16, "f_act")):
                for j in range(n):
                    s = sb((l, part), j)
                    pe.wait_ge(S["lo_ready"], nth[s] + 1)
                    claim(j % 4, name, j + 1)
                    full(s, bank(j % 4), hh, hl, arrives=("hl_ready", 16 * l) if part == "q" and j == 0 else None)
                    if part == "f" and j == 2 * MOD_GROUP:
                        mod_sum(6 * l + 5)
            for c in range(4):
                s = sb((l, "i"), 2 * c)
                pe.wait_ge(S["lo_ready"], nth[s] + 2)
                for t in range(NT):
                    claim(3 * (c % 2) + t, "vi_evac", c + 1)
                by_token(s, [ps[:, 3 * (c % 2) + t, 0:256] for t in range(NT)])
            for b in range(6):
                pe.wait_ge(*release[b])
            for b in (6, 7):
                if b in release:
                    pe.wait_ge(*release[b])
            pe.wait_ge(S["mod_read"], 6 * l + 6)
            pe.wait_ge(S["hgrn_in"], 32)
            for h in range(HH):
                hc = slice(h * P, (h + 1) * P)

                def state(j):
                    n, (t, d) = 4 * h + j, STATES[j]
                    pe.wait_ge(S["khT_read"], n + 1)
                    if j >= 2:
                        pe.wait_ge(S["stout_read"], 2 * SG_ + 2 * h + j - 1)
                    elif h:
                        pe.wait_ge(S["hs1_ready"], 2 * h - 1 + j)
                    pe.matmul(ps[:, 6 + n % 2, 0:P], hkt[:, n % 2, :], hv[:, t, hc], start=True, stop=True).then_inc(S["hst_done"], 1)

                for j in range(4):
                    n = 4 * h + j
                    pe.wait_ge(S["kh_ready"], n + 1)
                    if n >= 2:
                        pe.wait_ge(S["khT_read"], n - 1)
                    pe.transpose(ps[:, 4 + n % 2, 0:P], hkh[:, n % 2, :], ident[:, :]).then_inc(S["khT_done"], 1)
                    if j:
                        state(j - 1)
                state(3)
                for j in range(LEVELS + 1):
                    n = (LEVELS + 1) * h + j
                    pe.wait_ge(S["uw_ready"], n + 1)
                    if j:
                        pe.wait_ge(S["wq_ready"], LEVELS * h + j)
                    if n >= 2:
                        pe.wait_ge(S["lv_read"], n - 1)
                    for t in range(NT):
                        rhs = uw_at(h, j)[:, 1, toks(t)] if j else hq[:, h, toks(t)]
                        ins = pe.matmul(ps[:, n % 2, toks(t)], uw_at(h, j)[:, 0, toks(t)], rhs, start=True, stop=True)
                    ins.then_inc(S["lv_done"], 1)
                pe.wait_ge(S["lv_read"], (LEVELS + 1) * (h + 1))
                pe.wait_ge(S["qe_ready"], h + 1)
                pe.wait_ge(S["hs1_ready"], 2 * h + 2)
                if h >= 2:
                    pe.wait_ge(S["o_read"], h - 1)
                for t in range(NT):
                    o = ps[:, 2 + h % 2, toks(t)]
                    ins = pe.matmul(o, hv[:, t, hc], att[:, toks(t)], start=True, stop=(t == 0))
                    if t:
                        pe.matmul(o, hs0[:, 0, h, :] if t == 1 else hs1[:, 0, :], hqe[:, 0, toks(t - 1)], start=False, stop=False)
                        ins = pe.matmul(o, hs1[:, 1, :] if t == 1 else hs0[:, 1, h, :], hqe[:, 1, toks(t - 1)], start=False, stop=True)
                ins.then_inc(S["o_done"], 1)
            pe.wait_ge(S["khT_read"], 32)
            for b, v in ((0, ("lv_read", 64)), (1, ("lv_read", 64)), (2, ("o_read", 8)), (3, ("o_read", 8)),
                         (6, ("hs1_ready", 16)), (7, ("hs1_ready", 16))):
                release[b] = (S[v[0]], v[1])

            def g_tile(j):
                s = sb((l, "g"), j)
                pe.wait_ge(S["lo_ready"], nth[s] + 1)
                claim(G_BANKS[j], "hg_act", j + 1)
                full(s, bank(G_BANKS[j]), hh, hl)

            for h in range(HH):
                pe.wait_ge(S["ho_sq"], h + 1)
                if h >= 2:
                    pe.wait_ge(S["hstd"], h - 1)
                pe.matmul(bank(4 + h % 2), mean_d[:, :], hsq[:, h % 2, :], start=True, stop=True).then_inc(S["hms_done"], 1)
                if h < 6:
                    g_tile(h)
            release[4] = release[5] = (S["hstd"], 8)
            g_tile(6)
            g_tile(7)
            pe.wait_ge(*release[7])
            out_tiles(l, hoh, hol, 1, "hol_ready", 0)

        def dve_hgrn(dve, l, link, start_residual, residual, out_chunk_mods, mod_take, mod_chunk):
            lg = lambda i: c_("lbl", 16 * i, 16)
            e = lambda i: lbt2[:, 16 * i:16 * i + 16]
            link(dve.tensor_tensor(e(4), lg(0), lg(1), ALU.max))
            link(dve.tensor_tensor(e(4), e(4), lg(2), ALU.max))
            link(dve.tensor_tensor(e(4), e(4), lg(3), ALU.max))
            link(dve.tensor_tensor(lbt2[:, 0:64].rearrange("p (i c) -> p i c", i=DEPTH), c_("lbl", 0, 64).rearrange("p (i c) -> p i c", i=DEPTH),
                                   e(4).unsqueeze(1).to_broadcast([P, DEPTH, 16]), ALU.subtract))
            dve.tensor_copy(e(5), e(4)).then_inc(S["lb_vec"], 1)
            dve.wait_ge(S["lb_act"], 1)
            link(dve.tensor_tensor(e(4), e(0), e(1), ALU.add))
            link(dve.tensor_tensor(e(4), e(4), e(2), ALU.add))
            link(dve.tensor_tensor(e(5), e(4), e(3), ALU.add))
            link(dve.reciprocal(e(5), e(5)))
            link(dve.tensor_tensor(e(0), e(0), e(5), ALU.mult))
            link(dve.tensor_tensor(e(4), e(4), e(5), ALU.mult))
            link(dve.tensor_tensor(e(4), e(4), e(0), ALU.subtract))
            link(dve.tensor_scalar(e(5), e(4), -1.0, 1.0, ALU.mult, ALU.add))
            for j in range(16):
                if j % 2 == 0 and j < 2 * MOD_GROUP:
                    mod_chunk(MODC * l + MODC - MOD_GROUP + j // 2)
                if j == 2 * MOD_GROUP + 1:
                    mod_take(6 * l + 5)
                dve.wait_ge(S["f_act"], j + 1)
                f, k = hf[:, j // 8, j % 8, :], hk[:, j // 8, j % 8, :]
                link(dve.tensor_scalar(f, k, e(5)[:, j:j + 1], e(4)[:, j:j + 1], ALU.mult, ALU.add))
                dve.tensor_scalar(k, f, -1.0, 1.0, ALU.mult, ALU.add).then_inc(S["k_ready"], 1)
            dve.wait_ge(S["hmask_set"], 2)
            for j in range(16):
                dve.wait_ge(S["f_ln"], j // 8 + 1)
                f = hf[:, j // 8, j % 8, :]
                f = f[:, ::-1] if j >= 8 else f
                dve.tensor_tensor_scan(f, hmask[:, :], f, 0.0, ALU.mult, ALU.add).then_inc(S["scan_ready"], 1)
            dve.wait_ge(S["scan_ready"], 16)
            dve.wait_ge(S["hgrn_in"], 32)
            dve.wait_ge(S["q_evac"], 8)
            for h in range(HH):
                for j in range(4):
                    n, (t, d) = 4 * h + j, STATES[j]
                    dve.wait_ge(S["kh_exp"], n + 1)
                    dve.tensor_tensor(hkh[:, n % 2, :], hkh[:, n % 2, :], hk[:, d, h, toks(t)], ALU.mult).then_inc(S["kh_ready"], 1)
                    dve.wait_ge(S["khT_done"], n + 1)
                    if n >= 2:
                        dve.wait_ge(S["hst_done"], n - 1)
                    dve.tensor_copy(hkt[:, n % 2, :], ps[:, 4 + n % 2, 0:P]).then_inc(S["khT_read"], 1)
                if h:
                    dve.wait_ge(S["o_done"], h)
                for j in (2, 3):
                    t, d = STATES[j]
                    last = t * P + (P - 1 if d == 0 else 0)
                    dve.wait_ge(S["edec_ready"], 2 * h + j - 1)
                    dve.wait_ge(S["hst_done"], 4 * h + j + 1)
                    dve.scalar_tensor_tensor(out=hs1[:, d, :], in0=hs0[:, d, h, :], scalar=hed[:, d:d + 1], in1=ps[:, 6 + j % 2, 0:P],
                                             op0=ALU.mult, op1=ALU.add).then_inc(S["hs1_ready"], 1)
                kf, kb = hk[:, 0, h, :], hk[:, 1, h, :]

                def differences(j):
                    F, G, rf, rg = borders(h, j)
                    U = halves(uw_at(h, j + 1)[:, 0, :], j)
                    if (LEVELS + 1) * h + j >= 2:
                        dve.wait_ge(S["lv_done"], (LEVELS + 1) * h + j - 1)
                    dve.tensor_tensor(U[:, :, 0, :], rf, F[:, :, 0, :], ALU.subtract)
                    dve.tensor_tensor(U[:, :, 1, :], rg, G[:, :, 1, :], ALU.subtract).then_inc(S["u_sub"], 1)

                def keys(j):
                    n = LEVELS * h + j
                    U = uw_at(h, j + 1)[:, 0, :]
                    dve.wait_ge(S["u_exp"], n + 1)
                    dve.tensor_tensor(halves(U, j)[:, :, 0, :], halves(U, j)[:, :, 0, :], halves(kf, j)[:, :, 0, :], ALU.mult)
                    dve.tensor_tensor(halves(U, j)[:, :, 1, :], halves(U, j)[:, :, 1, :], halves(kb, j)[:, :, 1, :],
                                      ALU.mult).then_inc(S["uw_ready"], 1)

                a3 = att[:, :].rearrange("p (t n) -> p t n", t=NT)

                def pick(j):
                    n = (LEVELS + 1) * h + j
                    dve.wait_ge(S["lv_done"], n + 1)
                    dve.wait_ge(S["lv_read"], n)
                    src = bank(n % 2).rearrange("p (t n) -> p t n", t=NT)
                    if j == 0:
                        ins = dve.tensor_tensor(a3, src, ident[:, :].unsqueeze(1).to_broadcast([P, NT, P]), ALU.mult)
                    else:
                        ins = dve.copy_predicated(a3, lvl[:, j - 1, :].unsqueeze(1).to_broadcast([P, NT, P]), src)
                    ins.then_inc(S["lv_read"], 1)

                if h:
                    dve.wait_ge(S["lv_done"], (LEVELS + 1) * h)
                dve.tensor_tensor(uw_at(h, 0)[:, 0, :], kf, kb, ALU.add).then_inc(S["uw_ready"], 1)
                differences(0)
                for j in range(LEVELS):
                    if j + 1 < LEVELS:
                        differences(j + 1)
                    keys(j)
                    pick(j)
                pick(LEVELS)
            for h in range(HH):
                dve.wait_ge(S["hstd"], h + 1)
                if h:
                    dve.wait_ge(S["on_ready"], h)
                link(dve.reciprocal(hrs[:, :], hres[:, :]))
                dve.scalar_tensor_tensor(out=hq[:, h, :], in0=hq[:, h, :], scalar=c_("hng", 0), in1=hrs[:, :], op0=ALU.mult,
                                         op1=ALU.mult).then_inc(S["on_ready"], 1)
            dve.wait_ge(S["on_ready"], 8)
            for j in range(8):
                dve.wait_ge(S["hg_act"], j + 1)
                if j >= 2:
                    dve.wait_ge(S["hol_ready"], j - 1)
                dve.tensor_tensor(hon[:, j % 2, :], hq[:, j, :], hsg[:, j % 2, :], ALU.mult).then_inc(S["hon_ready"], 1)
            start_residual(2 * l)
            dve.wait_ge(S["hol_ready"], 8)
            for m in range(KD):
                out_chunk_mods(l, m, 2)
                dve.wait_ge(S["sub_done"], nth[sb((l, "out"), m)] + 1)
                residual(l, m, bank(m % 4), 16)
                for group in sums_after(l, m):
                    mod_take(group)

        def split_waits(eng, n, i):
            c, looped = order_of[n] // 2, not isinstance(i, int)
            rounds = i * (loop_chunks(c) // RAW) if looped else 0
            eng.wait_ge(raw_in[c % RAW], 16 * (c // RAW + 1) + rounds * 16)
            if looped:
                eng.wait_ge(S["sub_done"], n - SPL + 1 + i * LOOP_SPLIT)
            elif n >= SPL:
                eng.wait_ge(S["sub_done"], n - SPL + 1)

        def raw_sub(s0):
            k = chunk_rows[s0 // 2] or KD
            w = raw[:, (s0 // 2) % RAW, :].rearrange("p (k n) -> p k n", k=k)
            return w[:, (s0 % 2) * 8:(s0 % 2) * 8 + 8, :] if k == 16 else w[:, :, (s0 % 2) * (SUB // k):(s0 % 2 + 1) * (SUB // k)]

        def split_sub(w, s0):
            return w[:, nth[s0] % SPL, :].rearrange("p (k n) -> p k n", k=min(chunk_rows[s0 // 2], KD))

        LN_LAST = 2 * DEPTH - 1

        def sums_after(l, m):
            if l % 3 == 2:
                done = {7: 6 * l + 6}
            else:
                done = {3: 6 * l + 5, 7: 6 * l + 6} if l + 1 < DEPTH else {7: 6 * l + 5}
            return [done[m]] if m in done else []

        def loop_chunks(c):
            l = max(k for k in range(DEPTH) if places[k, "moe"][0] <= c)
            return len(moe_order(l + 1 < DEPTH))

        @block.scalar
        def _(act):
            chain = Chain(act, S["act_step"])
            fed = [0, nth[sb((0, "moe"))] + 2]

            def high(n, i=0):
                s0 = order_of[n]
                split_waits(act, n, i)
                act.activation(split_sub(whi, s0), raw_sub(s0), ACT.Copy).then_inc(S["hi_ready"], 1)

            def feed(upto):
                first = min(upto - SPL + 1, NSUB)
                while fed[0] <= min(nth[first] + SPL - 1, nth[NSUB] - 1, fed[1]) and order_of[fed[0]] // 2 < first // 2 + RAW:
                    high(fed[0])
                    fed[0] += 1

            def layer_norm(q, last=False):
                for j in range(4):
                    act.wait_ge(S["diff_ready"], 4 * q + j + 1)
                    act.activation(sq[:, 2 * j:2 * j + 2, :], y[:, 2 * j:2 * j + 2, :], ACT.Square).then_inc(S["sq_ready"], 1)
                act.wait_ge(S["var_done"], q + 1)
                act.activation(std[:, :], bank(5), ACT.Sqrt, bias=eps[:, 0:1]).then_inc(S["std_ready"], 1)
                l, w = q // 2, q % 2
                for k in range(KD):
                    act.wait_ge(S["norm_ready"], 8 * q + k + 1)
                    act.activation(x[:, k, :], y[:, k, :], ACT.Identity, scale=c_("lng", (2 * l + w) * 8 + k),
                                   bias=c_("lnb", (2 * l + w) * 8 + k)).then_inc(S["x_ready"], 1)
                    if not last:
                        act.wait_ge(S["h32_ready"], 8 * (q + 1) + k + 1)
                        act.activation(hh[:, k, :], h32[:, k, :], ACT.Copy).then_inc(S["hh_ready"], 1)

            def gmlp(l):
                u = l // 3
                for c in range(8):
                    s = sb((l, "v"), 2 * c)
                    feed(s + 3)
                    act.wait_ge(S["sub_done"], nth[s] + 2)
                    for t in range(NT):
                        ins = act.activation(gv[:, t, c * 256:(c + 1) * 256], ps[:, 3 * (c % 2) + t, 0:256], ACT.Gelu)
                    ins.then_inc(S["v_evac"], 1)
                for t in range(NT):
                    act.wait_ge(S["gstat_done"], 3 * u + t + 1)
                    act.activation(grs[:, t, 0:1], gmv[:, t, 1:2], ACT.Sqrt, bias=eps[:, 0:1]).then_inc(S["gstd_done"], 1)

                def product_high(j):
                    act.wait_ge(S["s32_ready"], 16 * u + j + 1)
                    act.activation(gsh[:, j, :], gs32[:, j % 2, :], ACT.Copy).then_inc(S["sh_ready"], 1)

                for j in range(16):
                    s = sb((l, "u"), j)
                    feed(s + 3)
                    act.wait_ge(S["sub_done"], nth[s] + 1)
                    if j >= 4:
                        act.wait_ge(S["s32_ready"], 16 * u + j - 3)
                    act.activation(gu[:, j % 4, :], bank(j % 4), ACT.Gelu).then_inc(S["u_evac"], 1)
                    if j >= 3:
                        product_high(j - 3)
                for j in range(13, 16):
                    feed(sb((l, "out")) + 3)
                    product_high(j)
                for m in range(8):
                    feed(sb((l, "out"), 2 * m + 2) + 3)

            def experts(l):
                more = l + 1 < DEPTH
                order = moe_order(more)
                nb = 2 * len(order)
                s_moe = sb((l, "moe"))
                feed(s_moe + 2)
                act.wait_ge(S["router_done"], l + 1)
                act.activation(rt[:, 0, :, :], ps[:, 4:4 + NT, 0:NE], ACT.Sigmoid).then_inc(S["route_ready"], 1)

                def combine_weights():
                    for n in range(4 * NT):
                        t, b = divmod(n, 4)
                        act.wait_ge(S["cwb_done"], 12 * l + n + 1)
                        act.activation(cwb[:, 4 * b:4 * b + 4, t * P:(t + 1) * P],
                                       ps[:, 4 + n % 3, :].rearrange("p (e n) -> p e n", e=4), ACT.Copy).then_inc(S["cwb_read"], 1)

                def step(i, static):
                    e0 = 16 * l + i * EG
                    for p, (what, e) in enumerate(order):
                        for j in range(0 if what == "M" else 2):
                            s0 = s_moe + 2 * p + j
                            if static:
                                feed(s0 + nb * i + 3)
                            else:
                                high(nth[s0] + 3, i)
                            if what == "G":
                                act.wait_ge(S["sub_done"], nth[s0] + 1 + i * LOOP_SPLIT)
                                act.activation(sg[:, e % 2, j, :], bank(j), ACT.Silu).then_inc(S["gate_read"], 1)
                            if (what == "G" and e >= 1 and j == 1) or (what == "D" and e == 2 and j == 1):
                                f = e - 1 if what == "G" else 3
                                act.wait_ge(S["e32_ready"], e0 + f + 1)
                                act.activation(eh[:, f % 2, :, :], e32[:, f % 2, :, :], ACT.Copy).then_inc(S["eh_ready"], 1)
                        if static and i == 0 and (what, e) == ("U", 0):
                            combine_weights()
                fed[1] = nth[s_moe] + LOOP_SPLIT + 2
                step(0, True)
                with act.Fori(1, MOE_ITERS - 1) as i:
                    step(i, False)
                fed[:] = nth[s_moe] + LOOP_SPLIT * (MOE_ITERS - 1) + 3, nth[sb((l + 1, "moe"))] + 2 if more else NSUB
                step(MOE_ITERS - 1, True)

            act.wait_ge(S["cols_in"], 16)
            act.activation(cond[:, :, :].rearrange("p k c -> p (k c)"), c_("cond", 0, 16), ACT.Silu).then_inc(S["cond_ready"], 1)
            for k in range(KD):
                act.wait_ge(S["h32_ready"], k + 1)
                act.activation(hh[:, k, :], h32[:, k, :], ACT.Copy).then_inc(S["hh_ready"], 1)
            feed(sb((0, "v")) + 3)
            act.wait_ge(S["router_in"], 16)
            act.activation(wrh[:, :, :], wrt[:, :, :], ACT.Copy).then_inc(S["router_split"], 1)
            for l in range(DEPTH):
                if l % 3 == 0:
                    gmlp(l)
                elif l % 3 == 1:
                    act_ssd(act, l, feed)
                else:
                    act_hgrn(act, l, feed)
                feed(sb((l, "moe")) + 3)
                layer_norm(2 * l)
                experts(l)
                feed(end_of_experts(l) + 3)
                layer_norm(2 * l + 1, last=(2 * l + 1 == LN_LAST))
    
        @block.gpsimd
        def _(pool):
            chain = Chain(pool, S["pool_step"])
            fed = [0, nth[sb((0, "moe"))] + 2]

            def low(n, i=0):
                s0 = order_of[n]
                pool.wait_ge(S["hi_ready"], n + 1 + i * LOOP_SPLIT)
                pool.tensor_tensor(split_sub(wlo, s0), raw_sub(s0), split_sub(whi, s0).bitcast(F32),
                                   ALU.subtract).then_inc(S["lo_ready"], 1)

            def feed(upto):
                first = min(upto - SPL + 1, NSUB)
                while fed[0] <= min(nth[first] + SPL - 1, nth[NSUB] - 1, fed[1]) and order_of[fed[0]] // 2 < first // 2 + RAW:
                    low(fed[0])
                    fed[0] += 1

            def hidden_low(n):
                for k in range(KD):
                    pool.wait_ge(S["hh_ready"], 8 * n + k + 1)
                    pool.tensor_tensor(hl[:, k, :], h32[:, k, :], hh[:, k, :].bitcast(F32),
                                       ALU.subtract).then_inc(S["hl_ready"], 1)

            def gmlp(l):
                u = l // 3
                for j in range(16):
                    feed(min(sb((l, "u"), j) + 6, sb((l, "u"), 15) + 3))
                    pool.wait_ge(S["sh_ready"], 16 * u + j + 1)
                    pool.tensor_tensor(gsl[:, j, :], gs32[:, j % 2, :], gsh[:, j, :].bitcast(F32),
                                       ALU.subtract).then_inc(S["sl_ready"], 1)

            def experts(l):
                more = l + 1 < DEPTH
                order = moe_order(more)
                nb = 2 * len(order)
                s_moe = sb((l, "moe"))
                feed(s_moe + 2)

                def step(i, static):
                    e0 = 16 * l + i * EG
                    for p, (what, e) in enumerate(order):
                        for j in range(0 if what == "M" else 2):
                            s0 = s_moe + 2 * p + j
                            if static:
                                feed(s0 + nb * i + 3)
                            else:
                                low(nth[s0] + 3, i)
                            if (what == "G" and e >= 1 and j == 1) or (what == "D" and e == 2 and j == 1):
                                f = e - 1 if what == "G" else 3
                                pool.wait_ge(S["eh_ready"], e0 + f + 1)
                                pool.tensor_tensor(el[:, f % 2, :, :], e32[:, f % 2, :, :],
                                                   eh[:, f % 2, :, :].bitcast(F32), ALU.subtract).then_inc(S["el_ready"], 1)
                fed[1] = nth[s_moe] + LOOP_SPLIT + 2
                step(0, True)
                with pool.Fori(1, MOE_ITERS - 1) as i:
                    step(i, False)
                fed[:] = nth[s_moe] + LOOP_SPLIT * (MOE_ITERS - 1) + 3, nth[sb((l + 1, "moe"))] + 2 if more else NSUB
                step(MOE_ITERS - 1, True)

            pool.memset(ones[:, :], 1.0)
            pool.memset(mean_d[:, :], 1.0 / D)
            pool.memset(eps[:, :], EPS).then_inc(S["consts_set"], 1)
            hidden_low(0)
            feed(sb((0, "v")) + 3)
            pool.wait_ge(S["router_split"], 1)
            pool.tensor_tensor(wrl[:, :, :], wrt[:, :, :], wrh[:, :, :].bitcast(F32), ALU.subtract).then_inc(S["router_split"], 1)
            for l in range(DEPTH):
                if l % 3 == 0:
                    gmlp(l)
                elif l % 3 == 1:
                    pool_ssd(pool, l, feed)
                else:
                    pool_hgrn(pool, l, feed)
                feed(sb((l, "moe")) + 3)
                hidden_low(2 * l + 1)
                experts(l)
                feed(end_of_experts(l) + 3)
                if 2 * l + 1 < LN_LAST:
                    hidden_low(2 * l + 2)
    
        @block.tensor
        def _(pe):
            release = {}

            def claim(b, name, value):
                if b in release:
                    pe.wait_ge(*release[b])
                release[b] = (S[name], value)

            def product(out, lhi, llo, rhi, rlo, first, last):
                pe.matmul(out, lhi, rhi, start=first, stop=False)
                pe.matmul(out, lhi, rlo, start=False, stop=False)
                return pe.matmul(out, llo, rhi, start=False, stop=last)

            def full(s0, out, rhi, rlo, k0=0, first=True, last=True, arrives=None):
                for k in range(KD):
                    w = slice(k * P, (k + 1) * P)
                    if arrives:
                        pe.wait_ge(S[arrives[0]], arrives[1] + k + 1)
                    ins = product(out, whi[:, nth[s0] % SPL, w], wlo[:, nth[s0] % SPL, w], rhi[:, k0 + k, :], rlo[:, k0 + k, :],
                                  first and k == 0, last and k == KD - 1)
                ins.then_inc(S["sub_done"], 1)

            def by_token(s0, outs, arrives=None):
                pair = lambda w, k: w[:, nth[s0] % SPL:nth[s0] % SPL + 2, k * P:(k + 1) * P]
                outs = [o.rearrange("p (a n) -> p a n", a=2) for o in outs]
                for k in range(KD):
                    if arrives is not None:
                        pe.wait_ge(S["hl_ready"], 8 * arrives + k + 1)
                    for t in range(NT):
                        tk = slice(t * P, (t + 1) * P)
                        pe.matmul(outs[t], hh[:, k, tk], pair(whi, k), start=(k == 0), stop=False)
                        pe.matmul(outs[t], hl[:, k, tk], pair(whi, k), start=False, stop=False)
                        ins = pe.matmul(outs[t], hh[:, k, tk], pair(wlo, k), start=False, stop=(k == KD - 1))
                ins.then_inc(S["sub_done"], 2)

            def mod_sum(group, i=0):
                pe.wait_ge(S["mac_step"], 16 * (group + 1) + i * 16)
                if isinstance(i, int):
                    claim(7, "mod_read", group + 1)
                else:
                    pe.wait_ge(S["mod_read"], group + i)
                for j in range(KD):
                    for v in range(2):
                        ins = pe.matmul(ps[:, 7, 2 * j + v:2 * j + v + 1], macc[:, v, j * P:(j + 1) * P], ones[:, 0:1],
                                        start=True, stop=True)
                ins.then_inc(S["mod_summed"], 1)

            def mean_step(q, k):
                pe.wait_ge(S["y_ready"], 8 * q + k + 1)
                if k == 0:
                    claim(6, "diff_ready", 4 * q + 4)
                ins = pe.matmul(bank(6), mean_d[:, :], y[:, k, :], start=(k == 0), stop=(k == KD - 1))
                if k == KD - 1:
                    ins.then_inc(S["mean_done"], 1)

            def variance(q):
                claim(5, "std_ready", q + 1)
                for k in range(KD):
                    pe.wait_ge(S["sq_ready"], 4 * q + k // 2 + 1)
                    ins = pe.matmul(bank(5), mean_d[:, :], sq[:, k, :], start=(k == 0), stop=(k == KD - 1))
                ins.then_inc(S["var_done"], 1)

            def out_tiles(l, rhi, rlo, halves, ready, count):
                q = 2 * l
                for m in range(KD):
                    claim(m % 4, "y_ready", 8 * q + m + 1)
                    for h in range(halves):
                        s = sb((l, "out"), halves * m + h)
                        pe.wait_ge(S["lo_ready"], nth[s] + 1)
                        full(s, bank(m % 4), rhi, rlo, 8 * h, h == 0, h == halves - 1, None if m else (ready, count + 8 * h))
                    for group in sums_after(l, m):
                        mod_sum(group)
                    if m:
                        mean_step(q, m - 1)
                mean_step(q, KD - 1)

            def gmlp(l):
                u = l // 3
                for c in range(8):
                    s = sb((l, "v"), 2 * c)
                    pe.wait_ge(S["lo_ready"], nth[s] + 2)
                    for t in range(NT):
                        claim(3 * (c % 2) + t, "v_evac", 8 * u + c + 1)
                    by_token(s, [ps[:, 3 * (c % 2) + t, 0:256] for t in range(NT)], None if c else 2 * l)
                    if l == 0 and c in (1, 3, 5):
                        mod_sum(2 + c // 2)

                def mix(j):
                    pe.wait_ge(S["v_norm"], 3 * u + 3)
                    claim(4 + j % 2, "a_ready", 16 * u + j + 1)
                    for t in range(NT):
                        ins = pe.matmul(ps[:, 4 + j % 2, t * P:(t + 1) * P], gv[:, t, j * P:(j + 1) * P], gws[:, j // 2, :],
                                        start=True, stop=True)
                    ins.then_inc(S["mix_done"], 1)

                for j in range(16):
                    s = sb((l, "u"), j)
                    pe.wait_ge(S["lo_ready"], nth[s] + 1)
                    claim(j % 4, "u_evac", 16 * u + j + 1)
                    full(s, bank(j % 4), hh, hl)
                    if j == 0:
                        pe.wait_ge(S["gmlp_in"], 32 * (u + 1))
                        for h in range(2):
                            claim(6 + h, "rows_read", 2 * u + h + 1)
                            if h:
                                pe.wait_ge(S["mod_read"], 6 * l + 5)
                            pe.matmul(ps[:, 6 + h, :], ones[:, :], gws[:, 4 * h:4 * h + 4, :],
                                      start=True, stop=True).then_inc(S["rows_done"], 1)
                    if j % 2 and j >= 3:
                        mix(j - 3)
                        mix(j - 2)
                mix(14)
                mix(15)
                pe.wait_ge(S["rows_read"], 2 * u + 2)
                out_tiles(l, gsh, gsl, 2, "sl_ready", 16 * u)

            def experts(l):
                more = l + 1 < DEPTH
                order = moe_order(more)
                pe.wait_ge(S["router_split"], 2)
                for t in range(NT):
                    claim(4 + t, "route_ready", l + 1)
                for k in range(KD):
                    pe.wait_ge(S["hl_ready"], 8 * (2 * l + 1) + k + 1)
                    for t in range(NT):
                        tk = slice(t * P, (t + 1) * P)
                        ins = product(ps[:, 4 + t, 0:NE], hh[:, k, tk], hl[:, k, tk], wrh[:, k, :], wrl[:, k, :],
                                      k == 0, k == KD - 1)
                ins.then_inc(S["router_done"], 1)
                for b in range(4):
                    if b in release:
                        pe.wait_ge(*release[b])
                s_moe = sb((l, "moe"))

                def combine_weights():
                    for n in range(4 * NT):
                        pe.wait_ge(S["cw_ready"], 12 * l + n + 1)
                        claim(4 + n % 3, "cwb_read", 12 * l + n + 1)
                        pe.matmul(ps[:, 4 + n % 3, :], ones[:, :], diag[:, 4 * (n % 4):4 * (n % 4) + 4, :], start=True,
                                  stop=True).then_inc(S["cwb_done"], 1)
                    for b in (4, 5, 6):
                        pe.wait_ge(*release[b])

                def after(name, value, i, per):
                    if not isinstance(i, int) or value + i * per:
                        pe.wait_ge(S[name], value + i * per)

                def step(i):
                    for p, (what, e) in enumerate(order):
                        s0 = s_moe + 2 * p
                        if what == "M":
                            continue
                        if what == "G":
                            after("gate_read", (16 * l + e) * 2, i, 8)
                        if what == "U":
                            after("up_read", 16 * l + e, i, EG)
                        if what == "D" and e == EG - 1 and more:
                            mod_sum(6 * (l + 1) + 1, i)
                        if what == "D":
                            pe.wait_ge(S["el_ready"], 16 * l + e + 1 + i * EG)
                        for j in range(2):
                            pe.wait_ge(S["lo_ready"], nth[s0 + j] + 1 + i * LOOP_SPLIT)
                            if what in "GU":
                                full(s0 + j, bank((what == "U") * 2 + j), hh, hl)
                                continue
                            for m in range(4):
                                d = 4 * j + m
                                after("down_added", 128 * l + 8 * e + (d - 2 if d >= 3 else 0), i, 32)
                                for k in range(2):
                                    w = slice(k * 512 + m * P, k * 512 + (m + 1) * P)
                                    ins = product(bank(4 + d % 3), whi[:, nth[s0 + j] % SPL, w], wlo[:, nth[s0 + j] % SPL, w],
                                                  eh[:, e % 2, k, :], el[:, e % 2, k, :], k == 0, k == 1)
                                ins.then_inc(S["down_done" if m < 3 else "sub_done"], 1)
                        if isinstance(i, int) and (what, e) == ("U", 0):
                            combine_weights()
                step(0)
                with pe.Fori(1, MOE_ITERS) as i:
                    step(i)
                q = 2 * l + 1
                for b in (0, 1):
                    release[b] = (S["gate_read"], 32 * (l + 1))
                for b in (2, 3):
                    release[b] = (S["up_read"], 16 * (l + 1))
                for b in (4, 5, 6):
                    release[b] = (S["down_added"], 128 * (l + 1))
                if more:
                    release[7] = (S["mod_read"], 6 * (l + 1) + 5)
                for k in range(KD):
                    mean_step(q, k)

            pe.wait_ge(S["consts_set"], 1)
            mod_sum(0)
            mod_sum(1)
            for l in range(DEPTH):
                if l % 3 == 0:
                    gmlp(l)
                elif l % 3 == 1:
                    pe_ssd(pe, l, claim, release, full, by_token, out_tiles)
                else:
                    pe_hgrn(pe, l, claim, release, full, by_token, out_tiles, mod_sum)
                variance(2 * l)
                experts(l)
                variance(2 * l + 1)

        @block.vector
        def _(dve):
            chain = Chain(dve, S["dve_step"])
            link = chain.link

            def mod_chunk(m, i=0):
                c, q, looped = mod_at[m], m % MOD_GROUP, not isinstance(i, int)
                rounds = i * (len(moe_order(True)) // RAW) if looped else 0
                dve.wait_ge(raw_in[c % RAW], 16 * (c // RAW + 1) + rounds * 16)
                w = raw[:, c % RAW, :].rearrange("p (k n) -> p k n", k=2)
                if m == 0:
                    dve.wait_ge(S["cond_ready"], 1)
                elif q == 0:
                    dve.wait_ge(S["mod_summed"], m // MOD_GROUP + i)
                for k in range(2):
                    for v in range(2):
                        by = cond[:, 2 * q + k, v:v + 1]
                        if q == 0 and k == 0:
                            ins = dve.tensor_scalar(macc[:, v, :], w[:, k, :], by, None, ALU.mult)
                        else:
                            dve.wait_ge(S["mac_step"], 4 * m + 2 * k + v - 1 + i * 4 * MOD_GROUP)
                            ins = dve.scalar_tensor_tensor(out=macc[:, v, :], in0=w[:, k, :], scalar=by, in1=macc[:, v, :],
                                                           op0=ALU.mult, op1=ALU.add)
                        ins.then_inc(S["mac_step"], 1)

            def mod_take(group, i=0):
                l, g = divmod(group, 6)
                dve.wait_ge(S["mod_summed"], group + 1 + i)
                at = 48 * l + 8 * g
                if isinstance(i, int):
                    b, dst = c_("bmod", at, 8), mods[:, l % 2, 8 * g:8 * g + 8, :]
                else:
                    b = cols[:, bass.ds(COL["bmod"] + at + i * 8, 8)]
                    dst = mods[:, l % 2, bass.ds(8 * g + i * 8, 8), :]
                dve.tensor_tensor(dst, ps[:, 7, 0:16].rearrange("p (j c) -> p j c", c=2), b.unsqueeze(2).to_broadcast([P, 8, 2]),
                                  ALU.add).then_inc(S["mod_read"], 1)

            def out_chunk_mods(l, m, tiles):
                if m % tiles == 0:
                    for owner, q in out_mods(l, m // tiles, KD // tiles):
                        mod_chunk(MODC * owner + q)

            def prepare_scale(l, which):
                par, sc, sh = (l % 2, 32, 24) if which == 0 else ((l + 1) % 2, 8, 0)
                dve.wait_ge(S["mod_read"], 6 * l + 5 + (6 if which else 0))
                g = c_("lng", (2 * l + which) * 8, 8).unsqueeze(2).to_broadcast([P, KD, 2])
                b = c_("lnb", (2 * l + which) * 8, 8).unsqueeze(2).to_broadcast([P, KD, 2])
                link(dve.tensor_scalar(cmod[:, 0, :, :], mods[:, par, sc:sc + 8, :], 1.0, None, ALU.add))
                link(dve.tensor_tensor(cmod[:, 1, :, :], cmod[:, 0, :, :], b, ALU.mult))
                link(dve.tensor_tensor(cmod[:, 1, :, :], cmod[:, 1, :, :], mods[:, par, sh:sh + 8, :], ALU.add))
                link(dve.tensor_tensor(cmod[:, 0, :, :], cmod[:, 0, :, :], g, ALU.mult))

            def modulate(src, k):
                for c, a, b in SEGS:
                    ins = dve.tensor_scalar(h32[:, k, a:b], src[:, k, a:b], cmod[:, 0, k, c:c + 1], cmod[:, 1, k, c:c + 1],
                                            ALU.mult, ALU.add)
                ins.then_inc(S["h32_ready"], 1)

            def layer_norm(q, last=False):
                l = q // 2
                if not last:
                    prepare_scale(l, q % 2)
                dve.wait_ge(S["mean_done"], q + 1)
                for j in range(4):
                    dve.tensor_tensor(y[:, 2 * j:2 * j + 2, :], y[:, 2 * j:2 * j + 2, :],
                                      bank(6).unsqueeze(1).to_broadcast([P, 2, T]), ALU.subtract).then_inc(S["diff_ready"], 1)
                dve.wait_ge(S["std_ready"], q + 1)
                link(dve.reciprocal(rstd[:, :], std[:, :]))
                for k in range(KD):
                    dve.tensor_tensor(y[:, k, :], y[:, k, :], rstd[:, :], ALU.mult).then_inc(S["norm_ready"], 1)
                    if not last:
                        dve.wait_ge(S["norm_ready"], 8 * q + k + 1)
                        modulate(y, k)

            def start_residual(q):
                dve.wait_ge(S["x_ready"], 8 * (q + 1))
                dve.wait_ge(S["mod_read"], 6 * (q // 2) + 5)
                link(dve.tensor_scalar(y[:, :, :], x[:, :, :], ALPHA, None, ALU.mult))

            def residual(l, m, src, g_tile):
                for c, a, b in SEGS:
                    ins = dve.scalar_tensor_tensor(out=y[:, m, a:b], in0=src[:, a:b], scalar=mods[:, l % 2, g_tile + m, c:c + 1],
                                                   in1=y[:, m, a:b], op0=ALU.mult, op1=ALU.add)
                ins.then_inc(S["y_ready"], 1)

            def gmlp(l):
                u = l // 3
                if l == 0:
                    for m in range(START_MODS, START_MODS + sum(V_MODS)):
                        mod_chunk(m)
                        if m % MOD_GROUP == MOD_GROUP - 1:
                            mod_take(m // MOD_GROUP)
                for t in range(NT):
                    dve.wait_ge(S["v_evac"], 8 * u + 8)
                    for c in range(4):
                        ins = dve.bn_stats(gst[:, t, c, :], gv[:, t, c * 512:(c + 1) * 512])
                    link(ins)
                    dve.bn_aggr(gmv[:, t, :], gst[:, t, :, :]).then_inc(S["gstat_done"], 1)
                for t in range(NT):
                    dve.wait_ge(S["gstd_done"], 3 * u + t + 1)
                    link(dve.reciprocal(grs[:, t, 1:2], grs[:, t, 0:1]))
                    dve.tensor_scalar(gv[:, t, :], gv[:, t, :], gmv[:, t, 0:1], grs[:, t, 1:2], ALU.subtract,
                                      ALU.mult).then_inc(S["v_norm"], 1)
                for h in range(2):
                    dve.wait_ge(S["rows_done"], 2 * u + h + 1)
                    dve.tensor_copy(grow[:, 4 * h:4 * h + 4, :].rearrange("p a b -> p (a b)"), ps[:, 6 + h, :]).then_inc(S["rows_read"], 1)
                dve.wait_ge(S["gmlp_in"], 32 * (u + 1))
                dve.wait_ge(S["rows_read"], 2 * u + 2)
                for j in range(16):
                    h = j // 2
                    link(dve.scalar_tensor_tensor(out=gct[:, j % 2, :], in0=grow[:, h, :], scalar=c_("glnb", 16 * u + j),
                                                  in1=gbs[:, h, :], op0=ALU.mult, op1=ALU.add))
                    dve.wait_ge(S["mix_done"], 16 * u + j + 1)
                    dve.scalar_tensor_tensor(out=gat[:, :].rearrange("p (t n) -> p t n", t=NT),
                                             in0=bank(4 + j % 2).rearrange("p (t n) -> p t n", t=NT),
                                             scalar=c_("glng", 16 * u + j),
                                             in1=gct[:, j % 2, :].unsqueeze(1).to_broadcast([P, NT, P]),
                                             op0=ALU.mult, op1=ALU.add).then_inc(S["a_ready"], 1)
                    dve.wait_ge(S["a_ready"], 16 * u + j + 1)
                    dve.wait_ge(S["u_evac"], 16 * u + j + 1)
                    if j >= 2:
                        dve.wait_ge(S["sl_ready"], 16 * u + j - 1)
                    dve.tensor_tensor(gs32[:, j % 2, :], gat[:, :], gu[:, j % 4, :], ALU.mult).then_inc(S["s32_ready"], 1)
                dve.wait_ge(S["sl_ready"], 16 * u + 16)
                start_residual(2 * l)
                for m in range(KD):
                    out_chunk_mods(l, m, 1)
                    dve.wait_ge(S["sub_done"], nth[sb((l, "out"), 2 * m + 1)] + 1)
                    residual(l, m, bank(m % 4), 16)
                    for group in sums_after(l, m):
                        mod_take(group)

            def route(l):
                v = lambda n: rt[:, n, :, :]
                g4 = lambda n: rt[:, n, :, 0:NG]
                one = lambda n: rt[:, n, :, 0]
                flat = lambda n: rt[:, n, :, :].rearrange("p t (g e) -> p (t g) e", e=EG)
                pairs = rt[:, 2:4, :, :].rearrange("p a t e -> p (a t e)")[:, 0:72].rearrange("p (g e) -> p g e", e=6)
                dve.wait_ge(S["route_ready"], l + 1)
                link(dve.tensor_tensor(v(1), v(0), c_("brout", 0, 16).unsqueeze(1).to_broadcast([P, NT, NE]), ALU.add))
                dve.tensor_tensor(pairs[:, :, 0:3], flat(1)[:, :, 0:3], flat(1)[:, :, 1:4], ALU.add)
                dve.tensor_tensor(pairs[:, :, 3:5], flat(1)[:, :, 0:2], flat(1)[:, :, 2:4], ALU.add)
                link(dve.tensor_tensor(pairs[:, :, 5:6], flat(1)[:, :, 0:1], flat(1)[:, :, 3:4], ALU.add))
                link(dve.tensor_reduce(rt[:, 4, :, 0:NG], pairs.rearrange("p (t g) e -> p t g e", g=NG), AX.X, ALU.max))

                def first_max(src, tmp, key, n, out):
                    wide = lambda a: a.unsqueeze(2).to_broadcast([P, NT, n])
                    link(dve.tensor_reduce(one(tmp), src, AX.X, ALU.max))
                    link(dve.tensor_tensor(out, src, wide(one(tmp)), ALU.is_equal))
                    link(dve.tensor_tensor(out, out, c_(key, 0, n).unsqueeze(1).to_broadcast([P, NT, n]), ALU.mult))
                    link(dve.tensor_reduce(one(tmp), out, AX.X, ALU.max))
                    link(dve.tensor_tensor(out, out, wide(one(tmp)), ALU.is_equal))

                first_max(g4(4), 5, "gkey", NG, g4(6))
                ing = g4(6).unsqueeze(3).to_broadcast([P, NT, NG, EG])
                e4 = lambda n: rt[:, n, :, :].rearrange("p t (g e) -> p t g e", e=EG)
                link(dve.tensor_tensor(e4(7), e4(1), ing, ALU.mult))
                link(dve.tensor_scalar(g4(8), g4(6), -1.0, BIG, ALU.add, ALU.mult))
                link(dve.tensor_tensor(e4(7), e4(7), g4(8).unsqueeze(3).to_broadcast([P, NT, NG, EG]), ALU.add))
                first_max(v(7), 5, "ekey", NE, v(9))
                link(dve.scalar_tensor_tensor(out=v(7), in0=v(9), scalar=-3 * BIG, in1=v(7), op0=ALU.mult, op1=ALU.add))
                first_max(v(7), 5, "ekey", NE, v(10))
                link(dve.tensor_tensor(v(9), v(9), v(10), ALU.add))
                link(dve.tensor_tensor(v(9), v(9), v(0), ALU.mult))
                link(dve.tensor_reduce(one(5), v(9), AX.X, ALU.add))
                link(dve.reciprocal(one(11), one(5)))
                link(dve.tensor_tensor(v(12), v(9), one(11).unsqueeze(2).to_broadcast([P, NT, NE]), ALU.mult))
                for n in range(4 * NT):
                    t, b = divmod(n, 4)
                    if t:
                        dve.wait_ge(S["cwb_done"], 12 * l + n - 3)
                    dve.tensor_tensor(diag[:, 4 * b:4 * b + 4, :], ident[:, :].unsqueeze(1).to_broadcast([P, 4, P]),
                                      rt[:, 12, t, 4 * b:4 * b + 4].unsqueeze(2).to_broadcast([P, 4, P]),
                                      ALU.mult).then_inc(S["cw_ready"], 1)

            def experts(l):
                more = l + 1 < DEPTH
                order = moe_order(more)
                nb = 2 * len(order)
                s_moe = sb((l, "moe"))
                link(dve.memset(acc[:, :, :], 0.0))
                if more:
                    mod_chunk(MODC * (l + 1) + MOD_GROUP)
                route(l)

                def step(i):
                    for p, (what, e) in enumerate(order):
                        s0 = s_moe + 2 * p
                        if what == "M":
                            if not isinstance(i, int) or e:
                                mod_chunk(MODC * (l + 1) + MOD_GROUP + e, i)
                        elif what == "U":
                            dve.wait_ge(S["gate_read"], (16 * l + e + 1) * 2 + i * 8)
                            dve.wait_ge(S["sub_done"], nth[s0] + 2 + i * LOOP_SPLIT)
                            if not isinstance(i, int) or l or e:
                                dve.wait_ge(S["e32_ready"], 16 * l + e + i * EG)
                            dve.tensor_tensor(et[:, :, :], ps[:, 2:4, 0:T], sg[:, e % 2, :, :], ALU.mult).then_inc(S["up_read"], 1)
                            dve.wait_ge(S["up_read"], 16 * l + e + 1 + i * EG)
                            if isinstance(i, int) and e == 0:
                                dve.wait_ge(S["cwb_read"], 12 * (l + 1))
                            w = cwb[:, e:e + 1, :] if isinstance(i, int) else cwb[:, bass.ds(e + i * EG, 1), :]
                            dve.tensor_tensor(e32[:, e % 2, :, :], et[:, :, :], w.to_broadcast([P, 2, T]),
                                              ALU.mult).then_inc(S["e32_ready"], 1)
                        elif what == "D":
                            for d in range(8):
                                if d % 4 < 3:
                                    dve.wait_ge(S["down_done"], 96 * l + 6 * e + 3 * (d // 4) + d % 4 + 1 + i * 24)
                                else:
                                    dve.wait_ge(S["sub_done"], nth[s0] + d // 4 + 1 + i * LOOP_SPLIT)
                                dve.tensor_tensor(acc[:, d, :], bank(4 + d % 3), acc[:, d, :], ALU.add).then_inc(S["down_added"], 1)
                    if more:
                        mod_take(6 * (l + 1) + 1, i)
                step(0)
                start_residual(2 * l + 1)
                with dve.Fori(1, MOE_ITERS) as i:
                    step(i)
                dve.wait_ge(S["down_added"], 128 * (l + 1))
                for m in range(KD):
                    residual(l, m, acc[:, m, :], 40)

            for m in range(START_MODS):
                mod_chunk(m)
                if m % MOD_GROUP == MOD_GROUP - 1:
                    mod_take(m // MOD_GROUP)
            dve.wait_ge(S["mod_read"], 2)
            dve.wait_ge(S["x_in"], 48)
            dve.tensor_tensor(x[:, :, LC:T], x[:, :, LC:T], h32[:, :, 0:LS], ALU.add).then_inc(S["x_ready"], 8)
            dve.wait_ge(S["x_ready"], 8)
            link(dve.tensor_scalar(cmod[:, 0, :, :], mods[:, 0, 8:16, :], 1.0, None, ALU.add))
            link(dve.tensor_copy(cmod[:, 1, :, :], mods[:, 0, 0:8, :]))
            for k in range(KD):
                modulate(x, k)
            for l in range(DEPTH):
                if l % 3 == 0:
                    gmlp(l)
                elif l % 3 == 1:
                    dve_ssd(dve, l, link, start_residual, residual, out_chunk_mods, mod_take)
                else:
                    dve_hgrn(dve, l, link, start_residual, residual, out_chunk_mods, mod_take, mod_chunk)
                more = l + 1 < DEPTH
                layer_norm(2 * l)
                experts(l)
                layer_norm(2 * l + 1, 2 * l + 1 == LN_LAST)




def masks():
    i = np.arange(P)
    le = (i[:, None] <= i[None, :]).astype(np.float32)
    ge = (i[:, None] >= i[None, :]).astype(np.float32)
    lim = lambda m: np.where(m > 0, 0.0, -BIG).astype(np.float32)
    levels = np.zeros((P, LEVELS, P), np.uint32)
    for j in range(LEVELS):
        h = 1 << j
        same = (i[:, None] // (2 * h)) == (i[None, :] // (2 * h))
        other = (i[:, None] // h) != (i[None, :] // h)
        levels[:, j, :] = same & other
    return np.concatenate([np.eye(P, dtype=np.float32), le, ge, lim(le), lim(ge)], 1), levels


def positions():
    grid_w, quarter = 64, D // 4
    rows = LS // grid_w
    freq = np.exp(-math.log(10000.0) / quarter * np.arange(quarter, dtype=np.float32)).astype(np.float32)
    r = np.repeat(np.arange(rows, dtype=np.float32), grid_w)
    col = np.tile(np.arange(grid_w, dtype=np.float32), rows)
    ar, ac = r[:, None] * freq[None, :], col[:, None] * freq[None, :]
    pos = np.concatenate([np.sin(ar), np.cos(ar), np.sin(ac), np.cos(ac)], -1).astype(np.float32)
    return np.ascontiguousarray(pos.T.reshape(KD, P, LS).transpose(1, 0, 2))


def kernel(**inputs):
    import concourse.bacc as _bacc
    from concourse.bass_utils import run_bass_kernel_spmd as _run

    f = {k: np.asarray(v) for k, v in inputs.items()}
    tiles = lambda a: a.reshape(-1, P).T
    wide = lambda a: np.broadcast_to(a.reshape(1, -1), (P, a.size))
    gkey = np.arange(NG, 0, -1, dtype=np.float32)
    ekey = np.arange(NE, 0, -1, dtype=np.float32)
    cond = np.stack([f["c_ctx"].reshape(KD, P), f["c"].reshape(KD, P)], 1)
    columns = [tiles(f["b_mod"]), tiles(f["ln_g"]), tiles(f["ln_b"]), tiles(f["gmlp_ln_g"]), tiles(f["gmlp_ln_b"]),
               tiles(f["ssd_conv_w"]), tiles(f["ssd_conv_b"]), tiles(np.repeat(f["ssd_d_skip"], SP_, 1)),
               tiles(f["ssd_norm_g"]), tiles(f["hgrn_lb_logits"]), tiles(f["hgrn_norm_g"]), tiles(cond),
               wide(f["ssd_dt_bias"]), wide(f["ssd_a_log"]), wide(f["moe_b_router"]), wide(gkey), wide(ekey)]
    tok = np.concatenate([f["x_prompt"][0], f["x_sample"][0]], 0)
    mask, levels = masks()
    arrays = {
        "cols": np.ascontiguousarray(np.concatenate(columns, 1)),
        "x_t": np.ascontiguousarray(tok.T.reshape(KD, P, T).transpose(1, 0, 2)),
        "pos_t": positions(), "masks": mask, "levels": levels,
        "w_mod": f["w_mod"], "w_router": f["moe_w_router"], "moe_w_gu": f["moe_w_gu"], "moe_w_down": f["moe_w_down"],
        "gmlp_w_in": f["gmlp_w_in"], "gmlp_w_out": f["gmlp_w_out"],
        "gmlp_ws": np.ascontiguousarray(f["gmlp_w_s"].transpose(0, 3, 1, 2)),
        "gmlp_bs": f["gmlp_b_s"].reshape(-1, 8 * P),
        "ssd_w_in": f["ssd_w_in"], "ssd_w_out": f["ssd_w_out"],
        "s_ssd": np.ascontiguousarray(f["state_ssd"][0, 0].transpose(0, 3, 1, 2).reshape(2, SN, SI)),
        "hgrn_w_in": f["hgrn_w_in"], "hgrn_w_out": f["hgrn_w_out"],
        "s_hgrn": np.ascontiguousarray(f["state_hgrn"][0, 0].transpose(2, 0, 1, 3)),
    }
    assert arrays["cols"].shape[1] == NCOL
    nc = _bacc.Bacc("TRN2", target_bir_lowering=False, num_devices=1)
    A = {k: nc.dram_tensor(k, a.shape, mybir.dt.from_np(a.dtype), kind="ExternalInput").ap() for k, a in arrays.items()}
    outs = {"y_t": (P, KD, T), "n_ssd": (2, SN, SI), "n_hgrn": (P, 2, HH, P)}
    O = {k: nc.dram_tensor("o_" + k, s, F32, kind="ExternalOutput").ap() for k, s in outs.items()}
    trunk(nc, A, O)
    r = _run(nc, [arrays], core_ids=[0]).results[0]
    out = np.asarray(r["o_y_t"]).transpose(1, 0, 2).reshape(D, T).T
    ssd = np.asarray(r["o_n_ssd"]).reshape(2, SN, SH, SP_).transpose(0, 2, 3, 1)
    hgrn = np.asarray(r["o_n_hgrn"]).transpose(1, 2, 0, 3)
    return (np.ascontiguousarray(out[None, :LC]), np.ascontiguousarray(out[None, LC:]),
            np.ascontiguousarray(ssd[None, None]), np.ascontiguousarray(hgrn[None, None]))
```
